# Optimizing a Trainium2 kernel written in Bass

```python
import jax
import jax.numpy as jnp
from jax import lax
import numpy as np

D_MODEL = 1024
BATCH = 1
SEQ = 512
DEPTH = 2

N_BRANCHES = 4
BRANCH_WIDTH = D_MODEL // 4
HEAD_DIM = 64
N_HEADS = BRANCH_WIDTH // HEAD_DIM
HGRN_CHUNK = 64
IDX_HEADS = 8
IDX_DIM = 32
TOPK_MAX = 256
Q_BLOCK = 128
ROPE_THETA = 10000.0
RWKV_W_LORA = 32
RWKV_A_LORA = 32
RWKV_V_LORA = 32
RWKV_G_LORA = 64
RWKV_COLS = 3 * BRANCH_WIDTH + RWKV_W_LORA + RWKV_A_LORA + RWKV_G_LORA
D_FF = 4 * D_MODEL
NORM_EPS = 1e-6
RWKV_GN_EPS = 64e-5
MASK_VALUE = -1e30
COL_SIZES = (
    BRANCH_WIDTH, BRANCH_WIDTH, BRANCH_WIDTH, BRANCH_WIDTH,
    BRANCH_WIDTH, BRANCH_WIDTH, BRANCH_WIDTH,
    IDX_HEADS * IDX_DIM, IDX_DIM, IDX_HEADS,
    RWKV_COLS,
    BRANCH_WIDTH, BRANCH_WIDTH, BRANCH_WIDTH, N_HEADS,
    N_BRANCHES * D_MODEL,
)
IN_COLS = sum(COL_SIZES)

kernel_name = 'hybrid_gated_hgrn2_dsa_rwkv7_fox'

F32 = jnp.float32

def rms_norm(t, g, eps=NORM_EPS):
    tf = t.astype(F32)
    y = tf * lax.rsqrt(jnp.mean(tf * tf, axis=-1, keepdims=True) + eps)
    return (y * g.astype(F32)).astype(t.dtype)

def split_cols(t, sizes):
    out, off = [], 0
    for s in sizes:
        out.append(t[..., off:off + s])
        off += s
    return out

def rope_tables(seq_len, dim):
    inv = 1.0 / (ROPE_THETA ** (jnp.arange(0, dim, 2, dtype=F32) / dim))
    ang = jnp.arange(seq_len, dtype=F32)[:, None] * inv[None, :]
    return jnp.cos(ang), jnp.sin(ang)

def apply_rope(t, cos, sin):
    half = t.shape[-1] // 2
    tf = t.astype(F32)
    t1, t2 = tf[..., :half], tf[..., half:]
    c, s = cos[None, :, None, :], sin[None, :, None, :]
    return jnp.concatenate([t1 * c - t2 * s, t2 * c + t1 * s], axis=-1).astype(t.dtype)

def hgrn2_mixer(q, f_logit, i_in, g_out, lb, norm_w):
    dt = q.dtype
    B_, T, _ = q.shape
    H, d, C = N_HEADS, HEAD_DIM, HGRN_CHUNK
    nc = T // C
    fl = f_logit.astype(F32)
    f = lb + (1.0 - lb) * jax.nn.sigmoid(fl)
    logf = jnp.log(f)
    k = (1.0 - lb) * jax.nn.sigmoid(-fl)

    def to_chunks(t):
        return t.astype(F32).reshape(B_, nc, C, H, d).transpose(1, 0, 3, 2, 4)

    qc = to_chunks(q) * (d ** -0.5)
    kc, vc, gc = to_chunks(k), to_chunks(i_in), to_chunks(logf)
    causal = jnp.tril(jnp.ones((C, C), dtype=bool))[:, :, None]

    def step(S, inp):
        qb, kb, vb, gb = inp
        b = jnp.cumsum(gb, axis=2)
        diff = b[:, :, :, None, :] - b[:, :, None, :, :]
        decay = jnp.where(causal, jnp.exp(jnp.where(causal, diff, 0.0)), 0.0)
        attn = jnp.einsum('bhtd,bhtsd,bhsd->bhts', qb, decay, kb)
        o = jnp.einsum('bhts,bhsv->bhtv', attn, vb) + jnp.einsum('bhtd,bhdv->bhtv', qb * jnp.exp(b), S)
        b_last = b[:, :, -1:, :]
        S = S * jnp.exp(b_last[:, :, 0, :, None]) + jnp.einsum('bhsd,bhsv->bhdv', kb * jnp.exp(b_last - b), vb)
        return S, o

    S0 = jnp.zeros((B_, H, d, d), F32)
    _, o = lax.scan(step, S0, (qc, kc, vc, gc))
    o = o.transpose(1, 0, 3, 2, 4).reshape(B_, T, H, d)
    o = o * lax.rsqrt(jnp.mean(o * o, axis=-1, keepdims=True) + NORM_EPS) * norm_w.astype(F32)
    gate = jax.nn.silu(g_out.astype(F32)).reshape(B_, T, H, d)
    return (o * gate).reshape(B_, T, H * d).astype(dt)

def dsa_mixer(q, k, v, q_idx, k_idx, w_idx, cos_h, sin_h, cos_i, sin_i):
    dt = q.dtype
    B_, T, _ = q.shape
    H, d = N_HEADS, HEAD_DIM
    qh = apply_rope(q.reshape(B_, T, H, d), cos_h, sin_h)
    kh = apply_rope(k.reshape(B_, T, H, d), cos_h, sin_h)
    vh = v.reshape(B_, T, H, d)
    qi = apply_rope(q_idx.reshape(B_, T, IDX_HEADS, IDX_DIM), cos_i, sin_i).astype(F32) * (IDX_DIM ** -0.5)
    ki = apply_rope(k_idx[:, :, None, :], cos_i, sin_i)[:, :, 0, :].astype(F32)
    wi = w_idx.astype(F32) * (IDX_HEADS ** -0.5)
    topk = min(TOPK_MAX, T // 4)
    key_pos = jnp.arange(T)

    def block(bi):
        start = bi * Q_BLOCK
        q_pos = start + jnp.arange(Q_BLOCK)
        qib = lax.dynamic_slice_in_dim(qi, start, Q_BLOCK, axis=1)
        wib = lax.dynamic_slice_in_dim(wi, start, Q_BLOCK, axis=1)
        qb = lax.dynamic_slice_in_dim(qh, start, Q_BLOCK, axis=1)
        score = jnp.einsum('bqhd,bsd->bqhs', qib, ki)
        score = jnp.einsum('bqhs,bqh->bqs', jax.nn.relu(score), wib)
        score = jnp.where((key_pos[None, :] <= q_pos[:, None])[None], score, MASK_VALUE)
        _, idx = lax.top_k(score, topk)
        valid = idx <= q_pos[None, :, None]
        k_sel = jax.vmap(lambda kk_, ii: kk_[ii])(kh, idx)
        v_sel = jax.vmap(lambda vv_, ii: vv_[ii])(vh, idx)
        logits = jnp.einsum('bqhd,bqkhd->bqhk', qb, k_sel).astype(F32) * (d ** -0.5)
        logits = jnp.where(valid[:, :, None, :], logits, MASK_VALUE)
        p = jax.nn.softmax(logits, axis=-1)
        return jnp.einsum('bqhk,bqkhd->bqhd', p.astype(v_sel.dtype), v_sel)

    out = lax.map(block, jnp.arange(T // Q_BLOCK))
    return out.transpose(1, 0, 2, 3, 4).reshape(B_, T, H * d).astype(dt)

def rwkv7_mixer(pc, mu, w0, w2, a0, a2, g2, k_k, k_a, r_k, ln_w, ln_b, v_first, v_gate):
    dt = pc.dtype
    B_, T, _ = pc.shape
    H, N = N_HEADS, HEAD_DIM
    p = pc.astype(F32)
    prev = jnp.pad(p, ((0, 0), (1, 0), (0, 0)))[:, :T]
    xm = p + (prev - p) * mu.astype(F32)
    r, k, v, w_in, a_in, g_in = split_cols(
        xm, (BRANCH_WIDTH, BRANCH_WIDTH, BRANCH_WIDTH, RWKV_W_LORA, RWKV_A_LORA, RWKV_G_LORA))
    w_log = -jax.nn.softplus(-(w0 + jnp.tanh(w_in) @ w2.astype(F32))) - 0.5
    decay = jnp.exp(-jnp.exp(w_log))
    a = jax.nn.sigmoid(a0 + a_in @ a2.astype(F32))
    g = jax.nn.sigmoid(g_in) @ g2.astype(F32)
    if v_gate is not None:
        v0, v1, v2 = v_gate
        v = v + (v_first - v) * jax.nn.sigmoid(v0 + (v @ v1.astype(F32)) @ v2.astype(F32))

    def heads(t):
        return t.reshape(B_, T, H, N)

    kk = heads(k * k_k)
    kk = kk * lax.rsqrt(jnp.maximum(jnp.sum(kk * kk, axis=-1, keepdims=True), 1e-24))
    k = k * (1.0 + (a - 1.0) * k_a)
    rh, wh, kh, vh, ah = heads(r), heads(decay), heads(k), heads(v), heads(a)
    xs = tuple(t.transpose(1, 0, 2, 3) for t in (rh, wh, kh, vh, kk, ah))

    def step(S, inp):
        rt, wt, kt, vt, kkt, at = inp
        sa = jnp.einsum('bhvi,bhi->bhv', S, -kkt)
        S = S * wt[:, :, None, :] + sa[..., None] * (kkt * at)[:, :, None, :] + vt[..., None] * kt[:, :, None, :]
        return S, jnp.einsum('bhvj,bhj->bhv', S, rt)

    S0 = jnp.zeros((B_, H, N, N), F32)
    _, y = lax.scan(step, S0, xs)
    y = y.transpose(1, 0, 2, 3)
    mean = jnp.mean(y, axis=-1, keepdims=True)
    var = jnp.mean(jnp.square(y - mean), axis=-1, keepdims=True)
    y = (y - mean) * lax.rsqrt(var + RWKV_GN_EPS) * ln_w.reshape(H, N) + ln_b.reshape(H, N)
    y = y + jnp.sum(rh * kh * r_k, axis=-1, keepdims=True) * vh
    return (y.reshape(B_, T, H * N) * g).astype(dt), v

def fox_mixer(q, k, v, f_logit, f_bias):
    dt = q.dtype
    B_, T, _ = q.shape
    H, d = N_HEADS, HEAD_DIM
    qh, kh, vh = q.reshape(B_, T, H, d), k.reshape(B_, T, H, d), v.reshape(B_, T, H, d)
    logf = jax.nn.log_sigmoid(f_logit.astype(F32) + f_bias.astype(F32))
    c = jnp.cumsum(logf, axis=1).transpose(0, 2, 1)
    key_pos = jnp.arange(T)

    def block(bi):
        start = bi * Q_BLOCK
        q_pos = start + jnp.arange(Q_BLOCK)
        qb = lax.dynamic_slice_in_dim(qh, start, Q_BLOCK, axis=1)
        cb = lax.dynamic_slice_in_dim(c, start, Q_BLOCK, axis=2)
        logits = jnp.einsum('bqhd,bshd->bhqs', qb, kh).astype(F32) * (d ** -0.5)
        logits = logits + cb[..., None] - c[:, :, None, :]
        logits = jnp.where(key_pos[None, :] <= q_pos[:, None], logits, MASK_VALUE)
        p = jax.nn.softmax(logits, axis=-1)
        return jnp.einsum('bhqs,bshd->bqhd', p.astype(vh.dtype), vh)

    out = lax.map(block, jnp.arange(T // Q_BLOCK))
    return out.transpose(1, 0, 2, 3, 4).reshape(B_, T, H * d).astype(dt)

def setup_inputs(seed: int = 0) -> dict:
    key = jax.random.key(seed)
    ks = jax.random.split(key, 32)
    W = BRANCH_WIDTH

    def nrm(k, shape, scale):
        return scale * jax.random.normal(k, shape, F32)

    def gain(k, n):
        return 1.0 + nrm(k, (DEPTH, n), 0.02)

    return {
        'x': nrm(ks[0], (BATCH, SEQ, D_MODEL), 1.0),
        'norm_mix_pre': gain(ks[1], D_MODEL),
        'norm_mix_post': gain(ks[2], D_MODEL),
        'norm_mlp_pre': gain(ks[3], D_MODEL),
        'norm_mlp_post': gain(ks[4], D_MODEL),
        'w_in': nrm(ks[5], (DEPTH, D_MODEL, IN_COLS), D_MODEL ** -0.5),
        'w_branch': nrm(ks[6], (DEPTH, N_BRANCHES, W, D_MODEL), W ** -0.5),
        'w_out': nrm(ks[7], (DEPTH, D_MODEL, D_MODEL), D_MODEL ** -0.5),
        'hgrn_lb_logits': nrm(ks[8], (DEPTH, W), 1.0),
        'hgrn_norm_w': gain(ks[9], HEAD_DIM),
        'fox_f_bias': 2.0 + nrm(ks[10], (DEPTH, N_HEADS), 0.5),
        'rwkv_mu': jax.random.uniform(ks[11], (DEPTH, RWKV_COLS), F32),
        'rwkv_w0': -3.0 + nrm(ks[12], (DEPTH, W), 1.0),
        'rwkv_w2': nrm(ks[13], (DEPTH, RWKV_W_LORA, W), 0.5 * RWKV_W_LORA ** -0.5),
        'rwkv_a0': nrm(ks[14], (DEPTH, W), 0.5),
        'rwkv_a2': nrm(ks[15], (DEPTH, RWKV_A_LORA, W), RWKV_A_LORA ** -0.5),
        'rwkv_g2': nrm(ks[16], (DEPTH, RWKV_G_LORA, W), RWKV_G_LORA ** -0.5),
        'rwkv_k_k': 0.85 + nrm(ks[17], (DEPTH, W), 0.05),
        'rwkv_k_a': 1.0 + nrm(ks[18], (DEPTH, W), 0.05),
        'rwkv_r_k': nrm(ks[19], (DEPTH, N_HEADS, HEAD_DIM), 0.1),
        'rwkv_ln_w': gain(ks[20], W),
        'rwkv_ln_b': nrm(ks[21], (DEPTH, W), 0.02),
        'rwkv_v0': nrm(ks[22], (DEPTH - 1, W), 0.5),
        'rwkv_v1': nrm(ks[23], (DEPTH - 1, W, RWKV_V_LORA), W ** -0.5),
        'rwkv_v2': nrm(ks[24], (DEPTH - 1, RWKV_V_LORA, W), RWKV_V_LORA ** -0.5),
        'w_up': nrm(ks[25], (DEPTH, D_MODEL, D_FF), D_MODEL ** -0.5),
        'w_down': nrm(ks[26], (DEPTH, D_FF, D_MODEL), D_FF ** -0.5),
    }

def reference(x, norm_mix_pre, norm_mix_post, norm_mlp_pre, norm_mlp_post, w_in, w_branch, w_out,
              hgrn_lb_logits, hgrn_norm_w, fox_f_bias, rwkv_mu, rwkv_w0, rwkv_w2, rwkv_a0, rwkv_a2,
              rwkv_g2, rwkv_k_k, rwkv_k_a, rwkv_r_k, rwkv_ln_w, rwkv_ln_b, rwkv_v0, rwkv_v1, rwkv_v2,
              w_up, w_down):
    B_, T, _ = x.shape
    cos_h, sin_h = rope_tables(T, HEAD_DIM)
    cos_i, sin_i = rope_tables(T, IDX_DIM)
    lb_soft = jax.nn.softmax(hgrn_lb_logits.astype(F32), axis=0)
    lower_bounds = jnp.cumsum(lb_soft, axis=0) - lb_soft[0:1]
    v_first = None
    for l in range(DEPTH):
        h = rms_norm(x, norm_mix_pre[l])
        proj = h @ w_in[l]
        (a_q, a_f, a_i, a_g, b_q, b_k, b_v, b_iq, b_ik, b_iw, c_all,
         d_q, d_k, d_v, d_f, gate_logits) = split_cols(proj, COL_SIZES)
        y_a = hgrn2_mixer(a_q, a_f, a_i, a_g, lower_bounds[l], hgrn_norm_w[l])
        y_b = dsa_mixer(b_q, b_k, b_v, b_iq, b_ik, b_iw, cos_h, sin_h, cos_i, sin_i)
        v_gate = None if l == 0 else (rwkv_v0[l - 1], rwkv_v1[l - 1], rwkv_v2[l - 1])
        y_c, v_c = rwkv7_mixer(c_all, rwkv_mu[l], rwkv_w0[l], rwkv_w2[l], rwkv_a0[l], rwkv_a2[l], rwkv_g2[l],
                               rwkv_k_k[l], rwkv_k_a[l], rwkv_r_k[l], rwkv_ln_w[l], rwkv_ln_b[l],
                               v_first, v_gate)
        if l == 0:
            v_first = v_c
        y_d = fox_mixer(d_q, d_k, d_v, d_f, fox_f_bias[l])
        gates = jax.nn.sigmoid(gate_logits.astype(F32)).reshape(B_, T, N_BRANCHES, D_MODEL)
        merged = (gates[:, :, 0] * (y_a @ w_branch[l, 0]).astype(F32)
                  + gates[:, :, 1] * (y_b @ w_branch[l, 1]).astype(F32)
                  + gates[:, :, 2] * (y_c @ w_branch[l, 2]).astype(F32)
                  + gates[:, :, 3] * (y_d @ w_branch[l, 3]).astype(F32))
        mix = merged.astype(x.dtype) @ w_out[l]
        x = x + rms_norm(mix, norm_mix_post[l])
        hm = rms_norm(x, norm_mlp_pre[l])
        u = jax.nn.relu(hm @ w_up[l])
        x = x + rms_norm(jnp.square(u) @ w_down[l], norm_mlp_post[l])
    return x


_drawn_inputs = setup_inputs


def setup_inputs(seed=0):
    import zlib

    import numpy as np

    out = dict(_drawn_inputs(seed))
    spreads = {}
    factors = {'norm_mlp_pre': 2.72,
     'norm_mlp_post': 2.907,
     'hgrn_norm_w': 13.517,
     'rwkv_ln_w': 19.107,
     'rwkv_ln_b': 18.539,
     'norm_mix_post': 2.749,
     'fox_f_bias': 5.521,
     'rwkv_r_k': 4.058}
    for name, (base, spread) in spreads.items():
        noise = np.random.default_rng([zlib.crc32(name.encode()), seed]).standard_normal(out[name].shape)
        drawn = base * np.exp(spread * noise) if base else spread * noise
        out[name] = jnp.asarray(drawn.astype(out[name].dtype))
    for name, factor in factors.items():
        out[name] = (out[name] * factor).astype(out[name].dtype)
    return out
```

```python
import numpy as np
import concourse.bass as bass
from concourse import mybir
from contextlib import ExitStack

LAYERS, T, D = 2, 512, 1024
P = 128
KT = D // P
W = D // 4
HD = 64
H = W // HD
NT = T // P
FT = W // P
IH, IDIM, TOPK = 8, 32, min(256, T // 4)
DFF = 4 * D
QUARTERS = 4
EPS, GN_EPS = 1e-6, 64e-5
NEG = -8e30
TAKEN = -3e38
CH = KT * 256
CHM = CH + FT * 256

A_Q, A_F, A_I, A_G = 0, 256, 512, 768
B_Q, B_K, B_V, B_IQ, B_IK, B_IW = 1024, 1280, 1536, 1792, 2048, 2080
C_R, C_K, C_V, C_L = 2088, 2344, 2600, 2856
D_Q, D_K, D_V, D_F, GATE = 2984, 3240, 3496, 3752, 3756
SM_IK, SM_F, SM_IW = 0, 32, 64
PROJ_CHUNKS, MERGE_CHUNKS, REST_CHUNKS = 16, 16, 4 + 8 * QUARTERS
CHUNKS = PROJ_CHUNKS + MERGE_CHUNKS + REST_CHUNKS

DENSE = []
for name, kind, n in (("aq", "fm", 2), ("af", "fm", 2), ("ai", "tm", 2), ("ag", "fm", 2),
                      ("bq", "fm", 2), ("bk", "fm", 2), ("bv", "tm", 2), ("biq", "fm", 2), ("bs", "fm", 1),
                      ("cr", "fm", 2), ("ck", "fm", 2), ("cv", "fm", 2), ("cl", "fm", 1),
                      ("dq", "fm", 2), ("dk", "fm", 2), ("dv", "tm", 2)):
    DENSE += [(name, i, kind, "act") for i in range(n)]
for n in range(4):
    for m in range(KT):
        DENSE += [(f"gate{n}", m, "fm", "act"), (f"branch{n}", m, "fm", "dve")]
DENSE += [("out", m, "fm", "act") for m in range(KT)]
DENSE += [("pad", i, "pad", "none") for i in range(-len(DENSE) % 4)]
MLP0 = len(DENSE)
INDEX = {(n, i): k for k, (n, i, _, _) in enumerate(DENSE)}
TAKEN_BY = {e: [sum(x[3] == e for x in DENSE[:k + 1]) for k in range(MLP0)] for e in ("act", "dve")}
ACT0, DVE0 = TAKEN_BY["act"][-1], TAKEN_BY["dve"][-1]
REAL0 = sum(x[3] != "none" for x in DENSE)


def issued(k):
    return sum(x[3] != "none" for x in DENSE[:k + 1])


PC, _n = {}, 0
for name, n in (("pre", 8), ("post", 8), ("mpre", 8), ("mpost", 8), ("hgw", 1), ("lb0", 2), ("lb1", 2),
                ("foxb", 1), ("mu", 7), ("w0", 2), ("a0", 2), ("kk", 2), ("ka", 2), ("rk", 2), ("lnw", 2),
                ("lnb", 2), ("v0", 2), ("flag", 1)):
    PC[name] = _n
    _n += n
NPAR = _n
PAR = NPAR + 256 + 64 + 256

CC, _n = {}, 0
for name, n in (("ident", P), ("ones", P), ("blk", P), ("roth", P), ("roti", P), ("rep", P), ("reprot", P),
                ("cneg", P), ("slt", P), ("sle", P), ("sgt", P), ("sel", H), ("seg", T)):
    CC[name] = _n
    _n += n
NCON = _n
LEVELS = [2 ** i for i in range(7)]


def constants():
    c = np.zeros((P, NCON), np.float32)
    i, j = np.arange(P)[:, None], np.arange(P)[None, :]
    put = lambda name, v: c.__setitem__((slice(None), slice(CC[name], CC[name] + v.shape[1])), v)
    put("ident", (i == j) * 1.0)
    put("ones", np.ones((P, P)))
    put("blk", (i // HD == j // HD) * 1.0)

    def rot(dim):
        half, r = dim // 2, j % dim
        return np.where((r < half) & (i == j + half), -1.0, 0.0) + np.where((r >= half) & (i == j - half), 1.0, 0.0)
    put("roth", rot(HD))
    put("roti", rot(IDIM))
    put("rep", (i == j % IDIM) * 1.0)
    put("reprot", (rot(IDIM)[:, :IDIM])[:, np.arange(P) % IDIM])
    put("cneg", np.where(j > i, NEG, 0.0))
    put("slt", (i < j) * 1.0)
    put("sle", (i <= j) * 1.0)
    put("sgt", (i > j) * 1.0)
    sel = np.zeros((P, H))
    for h in range(H):
        sel[SM_F + h, h] = 8.0
    put("sel", sel)
    put("seg", np.broadcast_to((np.arange(T) % P != 0) * 1.0, (P, T)))
    m = np.zeros((P, 2, len(LEVELS), P), np.float32)
    for k, n in enumerate(LEVELS):
        same = i // (2 * n) == j // (2 * n)
        m[:, 0, k] = same & (i % (2 * n) < n) & (j % (2 * n) >= n)
        m[:, 1, k] = m[:, 0, k].T
    rope = np.zeros((P, 4, T), np.float32)
    for k, dim in enumerate((HD, IDIM)):
        inv = (1.0 / (np.float32(10000.0) ** (np.arange(0, dim, 2, dtype=np.float32) / np.float32(dim)))).astype(np.float32)
        ang = np.arange(T, dtype=np.float32)[None, :] * inv[:, None]
        rope[:, 2 * k] = np.tile(np.cos(ang), (2 * P // dim, 1))
        rope[:, 2 * k + 1] = np.tile(np.sin(ang), (2 * P // dim, 1))
    return c, m.reshape(P, -1), rope.reshape(P, -1)


class Signal:

    def __init__(self, handle, name, per_layer):
        self.handle, self.name, self.per_layer, self.count = handle, name, per_layer, 0

    def at(self, layer, k):
        return self.handle, layer * self.per_layer + k

    def up(self, times=1):
        self.count += times
        return self.handle, 1


def trunk_kernel(nc, x_in, wproj, wmerge, wrest, par_in, con_in, mask_in, rope_in, out):
    f32, u8 = mybir.dt.float32, mybir.dt.uint8
    ALU, ACT, AX = mybir.AluOpType, mybir.ActivationFunctionType, mybir.AxisListType
    nc.disable_value_cache = True
    MUL, ADD, SUB = ALU.mult, ALU.add, ALU.subtract
    ctx = ExitStack()
    with ctx:
        def sb(name, shape, dt=f32):
            return ctx.enter_context(nc.sbuf_tensor(name, shape, dt))

        signals = []

        def signal(name, per_layer):
            signals.append(Signal(ctx.enter_context(nc.semaphore(name)), name, per_layer))
            return signals[-1]

        x = sb("x", [P, KT, T])
        hn = sb("hn", [P, KT, T])
        acc = sb("acc", [P, KT, T])
        u = sb("u", [P, KT, T])
        y = sb("y", [P, 4, FT, T])
        wsl = sb("wsl", [P, 2, CHM])
        slab = sb("slab", [P, 19, FT * T])
        con = sb("con", [P, NCON])
        msk = sb("msk", [P, 2 * len(LEVELS) * P], u8)
        par = sb("par", [P, PAR])
        tmp = sb("tmp", [P, 4, T])
        rstd = sb("rstd", [P, 2, T])
        small = sb("small", [P, T])
        iw = sb("iw", [P, NT, IH])
        st = sb("st", [P, FT, HD])
        lb = sb("lb", [P, 2, FT])
        col = sb("col", [P, 8, 8])
        v1st = sb("v1st", [P, FT, T])
        ps = [ctx.enter_context(nc.psum_tensor(f"bank{i}", [P, 512], f32)) for i in range(8)]

        def S(i, half=None):
            v = slab[:, i, :].rearrange("p (t n) -> p t n", t=FT)
            return v if half is None else v[:, half, :]

        def C(name, lo=0, hi=P, n=P):
            return con[lo:hi, CC[name]:CC[name] + n]

        def pcol(name, i=0, lo=0, hi=P):
            return par[lo:hi, PC[name] + i:PC[name] + i + 1]

        def heads(ap):
            return ap.rearrange("p (h t) -> p h t", h=H)

        def over_heads(ap):
            return ap[:, None, :].to_broadcast([P, H, P])

        def level(side, k):
            m = (side * len(LEVELS) + k) * P
            return over_heads(msk[:, m:m + P])

        lora = par[:, NPAR:NPAR + 256]
        v1w = par[:, NPAR + 256:NPAR + 320].rearrange("p (t n) -> p t n", t=FT)
        v2w = par[0:32, NPAR + 320:NPAR + 576]

        once = ctx.enter_context(nc.semaphore("tables_loaded"))
        x_loaded = ctx.enter_context(nc.semaphore("x_loaded"))
        masks_ready = ctx.enter_context(nc.semaphore("masks_ready"))
        cleared = ctx.enter_context(nc.semaphore("buffers_cleared"))
        carrier = ctx.enter_context(nc.semaphore("wait_carrier"))
        stored = ctx.enter_context(nc.semaphore("out_stored"))
        rope_in_ = signal("rope_loaded", 16)
        w_arrived = ctx.enter_context(nc.semaphore("weights_arrived"))
        w_free = ctx.enter_context(nc.semaphore("weights_free"))
        par_loaded = signal("params_loaded", 16)
        x_tiles = signal("x_updated", 2 * KT)
        dense_done = signal("dense_done", REAL0 + 16 * QUARTERS)
        act_took = signal("act_took_dense", ACT0 + 8 * QUARTERS)
        dve_took = signal("dve_took_dense", DVE0 + 8 * QUARTERS)
        dve_step = signal("dve_step", 177)
        act_step = signal("act_step", 8)
        squared = signal("squared", 4 * KT)
        sumsq = signal("sum_of_squares", 4 * KT)
        var_ready = signal("variance_ready", 4)
        rstd_done = signal("rstd_by_exp", 4)
        h_ready = signal("h_ready", 2 * KT)
        a_prep = signal("a_gate_logit_ready", 1)
        a_ln = signal("a_log_gate_ready", 1)
        a_diff = signal("a_decay_exponents_ready", 8)
        a_exp = signal("a_decays_ready", 9)
        a_ops = signal("a_level_operands_ready", 9)
        a_sc = signal("a_scores_ready", 8 * NT)
        a_sc_used = signal("a_scores_taken", 8 * NT)
        a_tr = signal("a_keys_transposed", 4)
        a_tr_used = signal("a_keys_taken", 4)
        a_o = signal("a_outputs_ready", NT)
        a_o_used = signal("a_outputs_taken", NT)
        a_su = signal("a_state_update_ready", NT)
        a_st = signal("a_state_ready", NT + 1)
        a_sq = signal("a_squared", 2)
        a_ss = signal("a_sum_ready", 2)
        a_var = signal("a_var_ready", 1)
        a_r = signal("a_rstd_ready", 1)
        y_ready = signal("y_ready", 2)
        lb_in = signal("bound_logits_ready", 1)
        lb_exp = signal("bound_exps_ready", 1)
        b_iwt = signal("b_index_weights_transposed", 1)
        b_rot = signal("b_rotated", 7)
        b_rep = signal("b_index_key_replicated", 1)
        b_rope = signal("b_rope_done", 7)
        b_ix = signal("b_index_scores_ready", IH * 3)
        b_relu = signal("b_relu_done", IH * 3)
        b_acc = signal("b_index_scores_used", IH * 3)
        b_iwc = signal("b_index_weights_copied", 1)
        at_lg = signal("logits_ready", 32)
        at_mx = signal("logits_masked", 32)
        at_ex = signal("exps_ready", 32)
        at_p = signal("probs_ready", 32)
        at_tr = signal("probs_transposed", 32)
        at_pt = signal("probs_taken", 32)
        at_pv = signal("attention_ready", 2 * NT)
        at_o = signal("attention_taken", 2 * NT)
        d_abs = signal("d_forget_logit_ready", 1)
        d_ln = signal("d_softplus_ready", 1)
        d_c = signal("d_cumulated", 1)
        d_bc = signal("d_cumulated_broadcast", H)
        d_bcu = signal("d_broadcast_taken", H)
        c_mix = signal("c_shifted", 1)
        c_act = signal("c_lora_hidden_ready", 1)
        c_lw = signal("c_lora_out_ready", 6)
        c_sg = signal("c_lora_out_taken", 6)
        c_vh = signal("c_value_hidden_ready", 1)
        c_vhc = signal("c_value_hidden_copied", 1)
        c_vg = signal("c_value_gate_ready", 2)
        c_vgs = signal("c_value_gate_taken", 2)
        c_sq = signal("c_squares_ready", 4)
        c_ss = signal("c_sums_ready", 4)
        c_kkv = signal("c_key_norm_ready", 1)
        c_kkr = signal("c_key_rnorm_ready", 1)
        c_ex = signal("c_exponents_ready", 1)
        c_exd = signal("c_exps_ready", 1)
        c_til = signal("c_operands_ready", 1)
        c_tr = signal("c_transposed", 6)
        c_tru = signal("c_transposes_taken", 6)
        c_m = signal("c_pairwise_ready", 6 * NT)
        c_mu = signal("c_pairwise_masked", 6 * NT)
        c_x1 = signal("c_inverse_started", NT)
        c_pp = signal("c_level_product_ready", 6 * NT)
        c_ppu = signal("c_level_product_masked", 6 * NT)
        c_xx = signal("c_level_inverse_ready", 11 * NT)
        c_xxu = signal("c_level_inverse_taken", 11 * NT)
        c_b = signal("c_rhs_ready", NT)
        c_bu = signal("c_rhs_taken", NT)
        c_u = signal("c_solution_ready", NT)
        c_uu = signal("c_solution_taken", NT)
        c_y = signal("c_outputs_ready", NT)
        c_yu = signal("c_outputs_taken", NT)
        c_s = signal("c_state_update_ready", NT)
        c_st = signal("c_state_ready", NT + 1)
        c_mean = signal("c_mean_ready", 2)
        c_cen = signal("c_centred", 1)
        c_csq = signal("c_centred_squared", 2)
        c_var = signal("c_variance_sum_ready", 2)
        c_vv = signal("c_variance_ready", 1)
        c_rr = signal("c_rstd_ready", 1)
        merged = signal("merged_ready", 4 * KT)
        product = dve_took
        acc0 = signal("acc_cleared", 1)
        u_ready = signal("hidden_ready", 4 + 8 * QUARTERS)

        block = ctx.enter_context(nc.Block())
        ONCE = 16 * 2

        @block.sync
        def _(sp):
            sp.dma_start(con[:, :], con_in).then_inc(once, 16)
            NM = 2 * len(LEVELS) * P
            sp.dma_start(slab[:, 0:2, :].rearrange("p a n -> p (a n)")[:, 0:NM], mask_in).then_inc(once, 16)
            sp.dma_start(x[:, :, :].rearrange("p k t -> p (k t)"), x_in).then_inc(x_loaded, 16)
            sp.sem_inc(w_free, 1)
            with sp.Fori(0, LAYERS) as layer:
                for src, first, count, size in ((wproj, 0, PROJ_CHUNKS, CH), (wmerge, PROJ_CHUNKS, MERGE_CHUNKS, CHM),
                                                (wrest, PROJ_CHUNKS + MERGE_CHUNKS, REST_CHUNKS, CH)):
                    with sp.Fori(0, count // 2) as pair:
                        for s in range(2):
                            at = sp.snap(layer * count + 2 * pair + s)
                            need = sp.snap(layer * CHUNKS + 2 * pair + (first + s + 1))
                            sp.wait_ge(w_free, need)
                            sp.dma_start(wsl[:, s, 0:size],
                                         src[bass.ds(at, 1)].rearrange("a p n -> (a p) n")).then_inc(w_arrived, 16)
            sp.wait_ge(x_tiles.handle, LAYERS * 2 * KT + 1)
            sp.dma_start(out, x[:, :, :].rearrange("p k t -> p (k t)")).then_inc(stored, 16)
            sp.wait_ge(stored, 16)

        @block.tensor
        def _(pe):
            pe.wait_ge(once, ONCE)
            pe.wait_ge(cleared, 1)
            mm = pe.matmul
            with pe.Fori(0, LAYERS) as L:
                chunk = [0]
                quarter = [0]
                fresh = [False]

                def next_chunk():
                    c = chunk[0]
                    chunk[0] += 1
                    pe.wait_ge(w_arrived, L * (16 * CHUNKS) + 16 * (c + 1 + 8 * quarter[0]))
                    fresh[0] = True
                    return c % 2

                def first_in_chunk(ins):
                    if fresh[0]:
                        ins.then_inc(w_free, 1)
                        fresh[0] = False

                def bank_free(d):
                    p = d - 4
                    if p >= 0 and DENSE[p][3] == "act":
                        pe.wait_ge(*act_took.at(L, TAKEN_BY["act"][p]))
                    elif p >= 0 and DENSE[p][3] == "dve":
                        pe.wait_ge(*dve_took.at(L, TAKEN_BY["dve"][p]))

                def dense_fm(d, slot, m, rhs=None, kts=KT, base=0):
                    bank_free(d)
                    for k in range(kts):
                        w0 = base + k * 256 + m * P
                        ins = mm(ps[d % 4][:, :], wsl[:, slot, w0:w0 + P], rhs(k), start=k == 0, stop=k == kts - 1)
                        if k == 0:
                            first_in_chunk(ins)
                    ins.then_inc(*dense_done.up())

                def dense_tm(d, slot, pair):
                    bank_free(d)
                    for j in range(2):
                        tt = 2 * pair + j
                        for k in range(KT):
                            ins = mm(ps[d % 4][:, j * 256:(j + 1) * 256], hn[:, k, tt * P:(tt + 1) * P],
                                     wsl[:, slot, k * 256:(k + 1) * 256], start=k == 0, stop=k == KT - 1)
                            if j == 0 and k == 0:
                                first_in_chunk(ins)
                    ins.then_inc(*dense_done.up())

                def hk(k):
                    return hn[:, k, :]

                def project(names):
                    for name in names:
                        slot = next_chunk()
                        for i in range(2):
                            if (name, i) in INDEX:
                                d = INDEX[(name, i)]
                                if DENSE[d][2] == "fm":
                                    dense_fm(d, slot, i, hk)
                                else:
                                    dense_tm(d, slot, i)

                def norm_sum(j, m):
                    pe.wait_ge(*squared.at(L, j * KT + m + 1))
                    mm(ps[4][:, :], C("ones"), tmp[:, m % 2, :], start=m == 0, stop=m == KT - 1).then_inc(*sumsq.up())

                def norm_sums(j):
                    for m in range(KT):
                        norm_sum(j, m)

                def attention(which, q, k, v, o):
                    base = 16 * which

                    def logits(i):
                        b, h = divmod(i, H)
                        lo = (h % 2) * HD
                        n = (b + 1) * P
                        if i >= 2:
                            pe.wait_ge(*at_mx.at(L, base + i - 1))
                        last = which == 0
                        ins = mm(ps[4 + i % 2][:, 0:n], q[lo:lo + HD, h // 2, b * P:(b + 1) * P],
                                 k[lo:lo + HD, h // 2, 0:n], start=True, stop=last)
                        if not last:
                            ins = mm(ps[4 + i % 2][:, b * P:n], C("ident"), C("cneg"), start=False, stop=True)
                        ins.then_inc(*at_lg.up())
                    logits(0)
                    for i in range(16):
                        b, h = divmod(i, H)
                        if i + 1 < 16:
                            logits(i + 1)
                        pe.wait_ge(*at_p.at(L, base + i + 1))
                        if i:
                            pe.wait_ge(*at_pt.at(L, base + i))
                        for j in range(b + 1):
                            ins = pe.transpose(ps[6][:, j * P:(j + 1) * P], S(14 + i % 4 // 2, i % 2)[:, j * P:(j + 1) * P],
                                               C("ident"))
                        ins.then_inc(*at_tr.up())
                        pe.wait_ge(*at_pt.at(L, base + i + 1))
                        if h == 0 and (b or which):
                            pe.wait_ge(*at_o.at(L, which * NT + b))
                        lo = (h % 2) * HD
                        for j in range(b + 1):
                            ins = mm(ps[7][lo:lo + HD, (h // 2) * P:(h // 2 + 1) * P], v[:, j, h * HD:(h + 1) * HD],
                                     S(16 + i % 4 // 2, i % 2)[:, j * P:(j + 1) * P], start=j == 0, stop=j == b)
                        if h == H - 1:
                            ins.then_inc(*at_pv.up())

                norm_sums(0)
                pe.wait_ge(*h_ready.at(L, KT))
                pe.wait_ge(*par_loaded.at(L, 16))

                project(("aq", "af", "ai", "ag"))
                E, k_ = S(5), S(1)
                for lv in range(8):
                    pe.wait_ge(*a_ops.at(L, lv + 1))
                    kk_, qq_ = (k_, S(0)) if lv == 0 else (E, E)
                    for b in range(4):
                        lo = (b % 2) * HD
                        if lv:
                            pe.wait_ge(*a_sc_used.at(L, (lv - 1) * NT + b + 1))
                        for i in range(4):
                            c, t = 2 * (b // 2) + i // 2, i % 2
                            ins = mm(ps[4 + b][:, i * P:(i + 1) * P], kk_[lo:lo + HD, t, c * P:(c + 1) * P],
                                     qq_[lo:lo + HD, t, c * P:(c + 1) * P], start=True, stop=True)
                        ins.then_inc(*a_sc.up())
                pe.wait_ge(*a_ops.at(L, 9))
                for c in range(NT):
                    if c == 0:
                        pe.wait_ge(*a_sc_used.at(L, 8 * NT))
                    else:
                        pe.wait_ge(*a_tr_used.at(L, c))
                    for t in range(FT):
                        ins = pe.transpose(ps[4][:, t * P:(t + 1) * P], S(8)[:, t, c * P:(c + 1) * P], C("ident"))
                    ins.then_inc(*a_tr.up())
                v_tm, khm = S(4), S(9)
                AT = [slab[:, 10 + c // 2, (c % 2) * T:(c % 2 + 1) * T] for c in range(NT)]
                v_ = slab[:, 4, :].rearrange("p (c n) -> p c n", c=NT)
                kh_ = slab[:, 9, :].rearrange("p (c n) -> p c n", c=NT)
                for c in range(NT):
                    pe.wait_ge(*a_st.at(L, c + 1))
                    pe.wait_ge(*a_tr_used.at(L, c + 1))
                    if c:
                        pe.wait_ge(*a_o_used.at(L, c))
                    for h in range(H):
                        lo, t = (h % 2) * HD, h // 2
                        o_ = ps[5][lo:lo + HD, t * P:(t + 1) * P]
                        at_ = AT[2 * (c // 2) + h % 2][:, (c % 2 * 2 + t) * P:(c % 2 * 2 + t + 1) * P]
                        mm(o_, v_[:, c, h * HD:(h + 1) * HD], at_, start=True, stop=False)
                        ins = mm(o_, st[lo:lo + HD, t, :], S(7)[lo:lo + HD, t, c * P:(c + 1) * P], start=False, stop=True)
                    ins.then_inc(*a_o.up())
                    for h in range(H):
                        lo, t = (h % 2) * HD, h // 2
                        ins = mm(ps[6][lo:lo + HD, t * HD:(t + 1) * HD], kh_[:, c, h * HD:(h + 1) * HD],
                                 v_[:, c, h * HD:(h + 1) * HD], start=True, stop=True)
                    ins.then_inc(*a_su.up())
                pe.wait_ge(*a_sq.at(L, 2))
                for t in range(FT):
                    mm(ps[4 + t][:, :], C("blk"), S(12, t), start=True, stop=True).then_inc(*a_ss.up())

                project(("bq", "bk", "bv", "biq", "bs"))
                pe.wait_ge(*y_ready.at(L, 1))
                pe.wait_ge(*act_took.at(L, TAKEN_BY["act"][INDEX[("bs", 0)]]))
                for tt in range(NT):
                    ins = pe.transpose(ps[7][:, tt * P:(tt + 1) * P], small[:, tt * P:(tt + 1) * P], C("ident"))
                ins.then_inc(*b_iwt.up())
                for r, (src, t, con_name) in enumerate(((0, 0, "roth"), (0, 1, "roth"), (1, 0, "roth"), (1, 1, "roth"),
                                                        (3, 0, "roti"), (3, 1, "roti"))):
                    if r >= 2:
                        pe.wait_ge(*b_rope.at(L, r - 1))
                    mm(ps[4 + r % 2][:, :], C(con_name), S(src, t), start=True, stop=True).then_inc(*b_rot.up())
                mm(ps[6][:, :], C("rep", 0, IDIM), small[0:IDIM, :], start=True, stop=True).then_inc(*b_rep.up())
                pe.wait_ge(*b_rope.at(L, 5))
                mm(ps[4][:, :], C("reprot", 0, IDIM), small[0:IDIM, :], start=True, stop=True).then_inc(*b_rot.up())
                pe.wait_ge(*b_rope.at(L, 7))
                n_ix = 0
                for b in range(1, NT):
                    for j in range(IH):
                        lo, t = (j % 4) * IDIM, j // 4
                        if n_ix >= 2:
                            pe.wait_ge(*b_relu.at(L, n_ix - 1))
                        mm(ps[4 + n_ix % 2][:, 0:(b + 1) * P], S(3)[lo:lo + IDIM, t, b * P:(b + 1) * P],
                           S(4, 0)[lo:lo + IDIM, 0:(b + 1) * P], start=True, stop=True).then_inc(*b_ix.up())
                        n_ix += 1
                pe.wait_ge(*b_relu.at(L, n_ix))
                pe.wait_ge(*b_iwc.at(L, 1))
                attention(0, S(0), S(1), slab[:, 2, :].rearrange("p (c n) -> p c n", c=NT), 1)

                project(("cr", "ck", "cv", "cl"))
                pe.wait_ge(*at_o.at(L, NT))
                pe.wait_ge(*c_act.at(L, 1))
                i_ = 0
                for lo, hi, buf in ((0, 32, S(3, 0)), (32, 64, S(3, 0)), (64, 128, S(3, 0))):
                    for t in range(FT):
                        if i_ >= 4:
                            pe.wait_ge(*c_sg.at(L, i_ - 3))
                        mm(ps[4 + i_ % 4][:, :], lora[lo:hi, t * P:(t + 1) * P], buf[lo:hi, :], start=True, stop=True)\
                            .then_inc(*c_lw.up())
                        i_ += 1
                pe.wait_ge(*c_sg.at(L, 4))
                for t in range(FT):
                    ins = mm(ps[6][0:32, :], v1w[:, t, :], S(2, t), start=t == 0, stop=t == 1)
                ins.then_inc(*c_vh.up())
                pe.wait_ge(*c_vhc.at(L, 1))
                pe.wait_ge(*c_sg.at(L, 6))
                for t in range(FT):
                    mm(ps[4 + t][:, :], v2w[:, t * P:(t + 1) * P], tmp[0:32, 0, :], start=True, stop=True)\
                        .then_inc(*c_vg.up())
                for t in range(FT):
                    pe.wait_ge(*c_sq.at(L, t + 1))
                    mm(ps[6 + t][:, :], C("blk"), S(10, t), start=True, stop=True).then_inc(*c_ss.up())
                for t in range(FT):
                    pe.wait_ge(*c_vgs.at(L, 2))
                    pe.wait_ge(*c_sq.at(L, 3 + t))
                    mm(ps[4 + t][:, :], C("blk"), S(4, t), start=True, stop=True).then_inc(*c_ss.up())
                pe.wait_ge(*c_til.at(L, 1))
                n_tr = 0
                for src in (14, 15, 2):
                    for half in range(2):
                        if n_tr >= 4:
                            pe.wait_ge(*c_tru.at(L, n_tr - 3))
                        for cc in range(2):
                            for t in range(FT):
                                ins = pe.transpose(ps[4 + n_tr % 4][:, cc * 256 + t * P:cc * 256 + (t + 1) * P],
                                                   S(src)[:, t, (2 * half + cc) * P:(2 * half + cc + 1) * P], C("ident"))
                        ins.then_inc(*c_tr.up())
                        n_tr += 1
                pe.wait_ge(*c_tru.at(L, 6))
                RT, AA, KK, BB = S(12), S(13), S(14), S(15)
                tm = [slab[:, 16 + i, :].rearrange("p (c n) -> p c n", c=NT) for i in range(3)]
                half = lambda i: slab[:, i // 2, (i % 2) * T:(i % 2 + 1) * T]
                Lm, X_, LTm, MTm, RBm, RKm, XT_, R_ = (half(i) for i in range(8))
                for c in range(NT):
                    cs = slice(c * P, (c + 1) * P)
                    for i, ops in enumerate((((BB, AA), (KK, AA)), ((BB, AA), (KK, AA)), ((BB, RT), (KK, RT)),
                                             ((BB, RT), (KK, RT)), ((AA, BB),), ((AA, BB),))):
                        lo = (i % 2) * HD
                        if i == 0 and c:
                            pe.wait_ge(*c_yu.at(L, c))
                            pe.wait_ge(*c_st.at(L, c + 1))
                        if i >= 4:
                            pe.wait_ge(*c_mu.at(L, 6 * c + i - 3))
                        for m, (a_, b_) in enumerate(ops):
                            for t in range(FT):
                                ins = mm(ps[4 + i % 4][:, (m * 2 + t) * P:(m * 2 + t + 1) * P], a_[lo:lo + HD, t, cs],
                                         b_[lo:lo + HD, t, cs], start=True, stop=True)
                        ins.then_inc(*c_m.up())
                    pe.wait_ge(*c_mu.at(L, 6 * c + 6))
                    pe.wait_ge(*c_x1.at(L, c + 1))
                    for lv in range(1, 7):
                        if lv > 1:
                            pe.wait_ge(*c_xxu.at(L, 11 * c + 2 * (lv - 1)))
                        for h in range(H):
                            hs = slice(h * P, (h + 1) * P)
                            ins = mm(ps[4][:, hs], LTm[:, hs], X_[:, hs], start=True, stop=True)
                        ins.then_inc(*c_pp.up())
                        pe.wait_ge(*c_ppu.at(L, 6 * c + lv))
                        PP = half(7 + lv)
                        if lv < 6:
                            for h in range(H):
                                hs = slice(h * P, (h + 1) * P)
                                ins = mm(ps[5][:, hs], XT_[:, hs], PP[:, hs], start=True, stop=True)
                            ins.then_inc(*c_xx.up())
                        for h in range(H):
                            hs = slice(h * P, (h + 1) * P)
                            ins = mm(ps[6][:, hs], PP[:, hs], XT_[:, hs], start=True, stop=True)
                        ins.then_inc(*c_xx.up())
                    pe.wait_ge(*c_st.at(L, c + 1))
                    for h in range(H):
                        lo, t, hs = (h % 2) * HD, h // 2, slice(h * HD, (h + 1) * HD)
                        o_ = ps[7 if h % 2 == 0 else 4][:, t * HD:(t + 1) * HD]
                        mm(o_, AA[lo:lo + HD, t, cs], st[lo:lo + HD, t, :], start=True, stop=False)
                        ins = mm(o_, MTm[:, h * P:(h + 1) * P], tm[2][:, c, hs], start=False, stop=True)
                    ins.then_inc(*c_b.up())
                    pe.wait_ge(*c_bu.at(L, c + 1))
                    pe.wait_ge(*c_xxu.at(L, 11 * c + 11))
                    for h in range(H):
                        hs = slice(h * HD, (h + 1) * HD)
                        ins = mm(ps[5][:, hs], XT_[:, h * P:(h + 1) * P], R_[:, hs], start=True, stop=True)
                    ins.then_inc(*c_u.up())
                    pe.wait_ge(*c_uu.at(L, c + 1))
                    pe.sem_inc(carrier, 1)
                    U_ = R_[:, 256:512]
                    for h in range(H):
                        lo, t, hs = (h % 2) * HD, h // 2, slice(h * HD, (h + 1) * HD)
                        o_ = ps[6][lo:lo + HD, t * P:(t + 1) * P]
                        mm(o_, st[lo:lo + HD, t, :], RT[lo:lo + HD, t, cs], start=True, stop=False)
                        mm(o_, U_[:, hs], RBm[:, h * P:(h + 1) * P], start=False, stop=False)
                        ins = mm(o_, tm[2][:, c, hs], RKm[:, h * P:(h + 1) * P], start=False, stop=True)
                    ins.then_inc(*c_y.up())
                    for h in range(H):
                        lo, t, hs = (h % 2) * HD, h // 2, slice(h * HD, (h + 1) * HD)
                        o_ = ps[7][lo:lo + HD, t * HD:(t + 1) * HD]
                        mm(o_, tm[1][:, c, hs], U_[:, hs], start=True, stop=False)
                        ins = mm(o_, tm[0][:, c, hs], tm[2][:, c, hs], start=False, stop=True)
                    ins.then_inc(*c_s.up())
                pe.wait_ge(*c_yu.at(L, NT))
                for t in range(FT):
                    mm(ps[4 + t][:, :], C("blk"), S(7, t), start=True, stop=True).then_inc(*c_mean.up())
                for t in range(FT):
                    pe.wait_ge(*c_csq.at(L, t + 1))
                    if t == 0:
                        pe.wait_ge(*c_st.at(L, NT + 1))
                    mm(ps[6 + t][:, :], C("blk"), S(10, t), start=True, stop=True).then_inc(*c_var.up())

                project(("dq", "dk", "dv"))
                pe.wait_ge(*y_ready.at(L, 2))
                pe.wait_ge(*d_c.at(L, 1))
                for h in range(H):
                    mm(ps[4 + h][:, :], con[SM_F:SM_F + H, CC["sel"] + h:CC["sel"] + h + 1].to_broadcast([H, P]),
                       S(5, 1)[SM_F:SM_F + H, :], start=True, stop=True).then_inc(*d_bc.up())
                pe.wait_ge(*d_bcu.at(L, H))
                pe.wait_ge(*act_took.at(L, TAKEN_BY["act"][INDEX[("dv", 1)]]))
                attention(1, S(0), S(1), slab[:, 2, :].rearrange("p (c n) -> p c n", c=NT), 3)

                for n in range(4):
                    pe.wait_ge(*(y_ready.at(L, n // 2 + 1) if n % 2 == 0 else at_o.at(L, (n // 2 + 1) * NT)))
                    for m in range(KT):
                        if m % 2 == 0:
                            slot = next_chunk()
                        dense_fm(INDEX[(f"gate{n}", m)], slot, m % 2, hk)
                        dense_fm(INDEX[(f"branch{n}", m)], slot, m % 2, lambda k, n=n: y[:, n, k, :], FT, CH)
                pe.wait_ge(*merged.at(L, 4 * KT))
                for m in range(KT):
                    if m % 2 == 0:
                        slot = next_chunk()
                    dense_fm(INDEX[("out", m)], slot, m % 2, lambda k: acc[:, k, :])
                    if m:
                        norm_sum(1, m - 1)
                norm_sum(1, KT - 1)
                norm_sums(2)
                pe.wait_ge(*h_ready.at(L, 2 * KT))
                chunk0 = chunk[0]
                assert chunk0 % 2 == 0 and MLP0 % 4 == 0
                pe.sem_inc(carrier, 1)
                with pe.Fori(0, QUARTERS) as q:
                    chunk[0], quarter[0] = chunk0, q
                    for j in range(16):
                        up = j < 8
                        m = j % 8
                        if m % 2 == 0:
                            slot = next_chunk()
                        if j < 4:
                            pe.wait_ge(*dve_took.at(L, q * 8 + (DVE0 - 8 + j + 5)))
                        elif j < 12:
                            pe.wait_ge(*act_took.at(L, q * 8 + (ACT0 + j - 3)))
                        else:
                            pe.wait_ge(*dve_took.at(L, q * 8 + (DVE0 + j - 11)))
                        if j == 8:
                            pe.wait_ge(*u_ready.at(L, q * 8 + 12))
                        for k in range(KT):
                            ins = mm(ps[j % 4][:, :], wsl[:, slot, k * 256 + (m % 2) * P:k * 256 + (m % 2 + 1) * P],
                                     (hn if up else u)[:, k, :], start=k == 0, stop=k == KT - 1)
                            if k == 0:
                                first_in_chunk(ins)
                        ins.then_inc(*dense_done.up(QUARTERS))
                norm_sums(3)

        @block.scalar
        def _(act):
            fn = act.activation

            def link(ins, sig=act_step):
                ins.then_inc(*sig.up())
                act.wait_ge(*sig.at(L, sig.count))

            act.wait_ge(once, ONCE)
            act.wait_ge(x_loaded, 16)
            act.wait_ge(cleared, 1)
            with act.Fori(0, LAYERS) as L:
                def take(name, i, outs):
                    d = INDEX[(name, i)]
                    act.wait_ge(*dense_done.at(L, issued(d)))
                    for n_, (o_, f_, sc_, bi_, in_) in enumerate(outs):
                        kw = {} if bi_ is None else {"bias": bi_}
                        ins = fn(o_, in_, f_, scale=sc_, **kw)
                    ins.then_inc(*act_took.up())

                def bank(name, i):
                    return ps[INDEX[(name, i)] % 4][:, :]

                def copy_out(name, slab_i, tm=False, scale=1.0):
                    for i in range(2):
                        o_ = S(slab_i, i)
                        take(name, i, [(o_, ACT.Copy, scale, None, bank(name, i))])

                def norm_rstd(j):
                    act.wait_ge(*var_ready.at(L, j + 1))
                    link(fn(rstd[:, 1, :], rstd[:, 0, :], ACT.Ln))
                    fn(rstd[:, 1, :], rstd[:, 1, :], ACT.Exp, scale=-0.5).then_inc(*rstd_done.up())

                def attention(which):
                    base = 16 * which

                    def transposed(i):
                        b = i // H
                        act.wait_ge(*at_tr.at(L, base + i + 1))
                        fn(S(16 + i % 4 // 2, i % 2)[:, 0:(b + 1) * P], ps[6][:, 0:(b + 1) * P], ACT.Copy)\
                            .then_inc(*at_pt.up())
                    for i in range(16):
                        b, h = divmod(i, H)
                        n = (b + 1) * P
                        buf = S(14 + i % 4 // 2, i % 2)
                        act.wait_ge(*at_mx.at(L, base + i + 1))
                        fn(buf[:, 0:n], buf[:, 0:n], ACT.Exp, bias=col[:, 1, i % 4:i % 4 + 1],
                           accum_out=col[:, 2, i % 4:i % 4 + 1]).then_inc(*at_ex.up())
                        if i:
                            transposed(i - 1)
                        if i and i % H == 0:
                            attn_out(i // H - 1)
                    transposed(15)
                    attn_out(NT - 1)

                def attn_out_of(which, b, o):
                    act.wait_ge(*at_pv.at(L, which * NT + b + 1))
                    fn(y[:, o, :, b * P:(b + 1) * P], ps[7][:, 0:256].rearrange("p (t n) -> p t n", t=FT), ACT.Copy)\
                        .then_inc(*at_o.up())

                act.wait_ge(*x_tiles.at(L, 1))
                act.dma_start(par[:, :], par_in[bass.ds(L, 1)].rearrange("a p n -> (a p) n")).then_inc(par_loaded.handle, 16)
                par_loaded.count += 16
                for m in range(KT):
                    if m >= 2:
                        act.wait_ge(*sumsq.at(L, m - 1))
                    fn(tmp[:, m % 2, :], x[:, m, :], ACT.Square).then_inc(*squared.up())
                norm_rstd(0)

                act.wait_ge(*lb_in.at(L, 1))
                fn(col[:, 7, 0:4], col[:, 6, 0:4], ACT.Exp).then_inc(*lb_exp.up())
                copy_out("aq", 0, scale=HD ** -0.5)
                for i in range(2):
                    take("af", i, [(S(2, i), ACT.Sigmoid, 1.0, None, bank("af", i)),
                                   (S(1, i), ACT.Sigmoid, -1.0, None, bank("af", i))])
                copy_out("ai", 4)
                for i in range(2):
                    take("ag", i, [(S(3, i), ACT.Copy, 1.0, None, bank("ag", i)),
                                   (S(12, i), ACT.Sigmoid, 1.0, None, bank("ag", i))])
                act.wait_ge(*a_prep.at(L, 1))
                fn(S(2), S(2), ACT.Ln).then_inc(*a_ln.up())
                E = slab[:, 5, :]
                for lv in range(1, 8):
                    act.wait_ge(*a_diff.at(L, lv))
                    fn(E, E, ACT.Exp).then_inc(*a_exp.up())
                act.wait_ge(*a_diff.at(L, 8))
                fn(slab[:, 6, :], slab[:, 2, :], ACT.Exp).then_inc(*a_exp.up())
                fn(slab[:, 8, :], slab[:, 8, :], ACT.Exp).then_inc(*a_exp.up())
                kh_ = slab[:, 9, :].rearrange("p (c n) -> p c n", c=NT)
                for c in range(NT):
                    act.wait_ge(*a_tr.at(L, c + 1))
                    fn(kh_[:, c, :], ps[4][:, 0:256], ACT.Copy).then_inc(*a_tr_used.up())
                for c in range(NT):
                    act.wait_ge(*a_o.at(L, c + 1))
                    fn(S(7 + 6)[:, :, c * P:(c + 1) * P], ps[5][:, 0:256].rearrange("p (t n) -> p t n", t=FT), ACT.Copy)\
                        .then_inc(*a_o_used.up())
                act.wait_ge(*a_o_used.at(L, NT))
                for t in range(FT):
                    fn(S(12, t), S(13, t), ACT.Square).then_inc(*a_sq.up())
                act.wait_ge(*a_var.at(L, 1))
                link(fn(slab[:, 6, :], slab[:, 6, :], ACT.Ln))
                fn(slab[:, 6, :], slab[:, 6, :], ACT.Exp, scale=-0.5).then_inc(*a_r.up())

                act.wait_ge(*y_ready.at(L, 1))
                copy_out("bq", 0)
                copy_out("bk", 1)
                copy_out("bv", 2)
                copy_out("biq", 3)
                take("bs", 0, [(small[:, :], ACT.Copy, 1.0, None, bank("bs", 0))])
                act.dma_start(slab[:, 5:7, :].rearrange("p a n -> p (a n)"), rope_in).then_inc(rope_in_.handle, 16)
                rope_in_.count += 16
                act.wait_ge(*b_iwt.at(L, 1))
                fn(iw[:, :, :], ps[7][:, :].rearrange("p (t n) -> p t n", t=NT)[:, :, SM_IW:SM_IW + IH], ACT.Copy,
                   scale=1.0 / 16.0).then_inc(*b_iwc.up())
                n_ix = 0
                for b in range(1, NT):
                    for j in range(IH):
                        n = (b + 1) * P
                        act.wait_ge(*b_ix.at(L, n_ix + 1))
                        if n_ix >= 2:
                            act.wait_ge(*b_acc.at(L, n_ix - 1))
                        fn(S(9, n_ix % 2)[:, 0:n], ps[4 + n_ix % 2][:, 0:n], ACT.Relu).then_inc(*b_relu.up())
                        n_ix += 1
                attn_out = lambda b: attn_out_of(0, b, 1)
                attention(0)

                copy_out("cr", 0)
                copy_out("ck", 1)
                copy_out("cv", 2)
                take("cl", 0, [(S(3, 0), ACT.Copy, 1.0, None, bank("cl", 0))])
                act.wait_ge(*c_mix.at(L, 1))
                fn(S(3, 0)[0:32, :], S(3, 0)[0:32, :], ACT.Tanh)
                fn(S(3, 0)[64:128, :], S(3, 0)[64:128, :], ACT.Sigmoid).then_inc(*c_act.up())
                for i_ in range(6):
                    t = i_ % 2
                    act.wait_ge(*c_lw.at(L, i_ + 1))
                    if i_ < 2:
                        ins = fn(S(6, t), ps[4 + i_ % 4][:, :], ACT.Sigmoid, bias=pcol("w0", t))
                    elif i_ < 4:
                        ins = fn(S(7, t), ps[4 + i_ % 4][:, :], ACT.Sigmoid, bias=pcol("a0", t))
                    else:
                        ins = fn(S(8, t), ps[4 + i_ % 4][:, :], ACT.Copy)
                    ins.then_inc(*c_sg.up())
                act.wait_ge(*c_vh.at(L, 1))
                fn(tmp[0:32, 0, :], ps[6][0:32, :], ACT.Copy).then_inc(*c_vhc.up())
                for t in range(FT):
                    act.wait_ge(*c_vg.at(L, t + 1))
                    fn(S(12, t), ps[4 + t][:, :], ACT.Sigmoid, bias=pcol("v0", t)).then_inc(*c_vgs.up())
                act.wait_ge(*c_kkv.at(L, 1))
                link(fn(slab[:, 10, :], slab[:, 10, :], ACT.Ln))
                fn(slab[:, 10, :], slab[:, 10, :], ACT.Exp, scale=-0.5).then_inc(*c_kkr.up())
                act.wait_ge(*c_ex.at(L, 1))
                fn(slab[:, 12, :], slab[:, 5, :], ACT.Exp)
                fn(slab[:, 14, :], slab[:, 5, :], ACT.Exp, scale=-1.0)
                fn(slab[:, 13, :], slab[:, 6, :], ACT.Exp)
                fn(col[:, 3, :], col[:, 4, :], ACT.Exp).then_inc(*c_exd.up())
                tmf = [slab[:, 16 + i, :] for i in range(3)]
                for n_tr in range(6):
                    act.wait_ge(*c_tr.at(L, n_tr + 1))
                    fn(tmf[n_tr // 2][:, (n_tr % 2) * T:(n_tr % 2 + 1) * T], ps[4 + n_tr % 4][:, :], ACT.Copy)\
                        .then_inc(*c_tru.up())
                half = lambda i: slab[:, i // 2, (i % 2) * T:(i % 2 + 1) * T]
                X_, XT_, R_ = half(1), half(6), half(7)
                for c in range(NT):
                    for k_ in range(11):
                        act.wait_ge(*c_xx.at(L, 11 * c + k_ + 1))
                        tgt, bk = (X_, 5) if k_ % 2 == 0 and k_ < 10 else (XT_, 6)
                        fn(tgt, ps[bk][:, :], ACT.Copy).then_inc(*c_xxu.up())
                    act.wait_ge(*c_b.at(L, c + 1))
                    rhs_ = R_[:, 0:256].rearrange("p (t two v) -> p t two v", two=2, v=HD)
                    fn(rhs_[:, :, 0, :], ps[7][:, 0:P].rearrange("p (t v) -> p t v", v=HD), ACT.Copy)
                    fn(rhs_[:, :, 1, :], ps[4][:, 0:P].rearrange("p (t v) -> p t v", v=HD), ACT.Copy).then_inc(*c_bu.up())
                    act.wait_ge(*c_u.at(L, c + 1))
                    fn(R_[:, 256:512], ps[5][:, 0:256], ACT.Copy).then_inc(*c_uu.up())
                    act.wait_ge(*c_y.at(L, c + 1))
                    fn(S(7)[:, :, c * P:(c + 1) * P], ps[6][:, 0:256].rearrange("p (t n) -> p t n", t=FT), ACT.Copy)\
                        .then_inc(*c_yu.up())
                act.wait_ge(*c_cen.at(L, 1))
                for t in range(FT):
                    fn(S(10, t), S(7, t), ACT.Square).then_inc(*c_csq.up())
                act.wait_ge(*c_vv.at(L, 1))
                link(fn(slab[:, 10, :], slab[:, 10, :], ACT.Ln))
                fn(slab[:, 10, :], slab[:, 10, :], ACT.Exp, scale=-0.5).then_inc(*c_rr.up())

                act.wait_ge(*y_ready.at(L, 2))
                copy_out("dq", 0)
                copy_out("dk", 1)
                copy_out("dv", 2)
                act.wait_ge(*d_abs.at(L, 1))
                s5 = S(5, 0)[SM_F:SM_F + H, :]
                link(fn(s5, s5, ACT.Exp, scale=-1.0))
                fn(s5, s5, ACT.Ln, bias=C("ones", SM_F, SM_F + H, 1)).then_inc(*d_ln.up())
                for h in range(H):
                    act.wait_ge(*d_bc.at(L, h + 1))
                    fn(S(6 + h // 2, h % 2), ps[4 + h][:, :], ACT.Copy).then_inc(*d_bcu.up())
                attn_out = lambda b: attn_out_of(1, b, 3)
                attention(1)

                for n in range(4):
                    for m in range(KT):
                        g_ = n * KT + m
                        if g_ >= 2:
                            act.wait_ge(*product.at(L, g_ - 1))
                        take(f"gate{n}", m, [(tmp[:, m % 2, :], ACT.Sigmoid, 1.0, None, bank(f"gate{n}", m))])
                for m in range(KT):
                    d = INDEX[("out", m)]
                    act.wait_ge(*dense_done.at(L, issued(d)))
                    if m >= 2:
                        act.wait_ge(*sumsq.at(L, KT + m - 1))
                    else:
                        act.wait_ge(*product.at(L, 4 * KT))
                    fn(tmp[:, m % 2, :], ps[d % 4][:, :], ACT.Square).then_inc(*squared.up())
                    fn(u[:, m, :], ps[d % 4][:, :], ACT.Copy).then_inc(*act_took.up())
                norm_rstd(1)
                for m in range(KT):
                    act.wait_ge(*x_tiles.at(L, 1 + m + 1))
                    if m >= 2:
                        act.wait_ge(*sumsq.at(L, 2 * KT + m - 1))
                    fn(tmp[:, m % 2, :], x[:, m, :], ACT.Square).then_inc(*squared.up())
                norm_rstd(2)
                with act.Fori(0, QUARTERS) as q:
                    for m in range(KT):
                        act.wait_ge(*dense_done.at(L, q * 16 + (REAL0 + m + 1)))
                        act.wait_ge(*u_ready.at(L, q * KT + m + 1))
                        fn(tmp[:, m % 4, :], ps[m % 4][:, :], ACT.Relu).then_inc(*act_took.up(QUARTERS))
                for m in range(KT):
                    act.wait_ge(*dve_took.at(L, DVE0 + 8 * 3 + m + 1))
                    if m >= 2:
                        act.wait_ge(*sumsq.at(L, 3 * KT + m - 1))
                    fn(tmp[:, m % 2, :], acc[:, m, :], ACT.Square).then_inc(*squared.up())
                norm_rstd(3)

        @block.gpsimd
        def _(pool):
            pool.memset(v1st[:, :, :], 0.0).then_inc(cleared, 1)
            pool.wait_ge(once, ONCE)
            with pool.Fori(0, LAYERS) as L:
                def carry_wait():
                    pool.sem_inc(carrier, 1)

                for n in range(4):
                    for m in range(KT):
                        i_ = n * KT + m
                        pool.wait_ge(*product.at(L, i_ + 1))
                        if n == 0:
                            if i_ == 0:
                                pool.wait_ge(*x_tiles.at(L, 1))
                            carry_wait()
                            pool.tensor_copy(acc[:, m, :], tmp[:, 2 + i_ % 2, :]).then_inc(*merged.up())
                        else:
                            pool.tensor_tensor(acc[:, m, :], acc[:, m, :], tmp[:, 2 + i_ % 2, :], ADD)\
                                .then_inc(*merged.up())
                pool.wait_ge(*dense_done.at(L, issued(INDEX[("out", KT - 1)])))
                carry_wait()
                pool.memset(acc[:, :, :], 0.0).then_inc(*acc0.up())
                pool.wait_ge(*acc0.at(L, 1))
                for _ in range(4):
                    pool.sem_inc(*u_ready.up())
                with pool.Fori(0, QUARTERS) as q:
                    for m in range(KT):
                        pool.wait_ge(*act_took.at(L, q * KT + (ACT0 + m + 1)))
                        if m == 0:
                            pool.wait_ge(*x_tiles.at(L, 1 + KT))
                        pool.tensor_tensor(u[:, m, :], tmp[:, m % 4, :], tmp[:, m % 4, :], MUL)\
                            .then_inc(*u_ready.up(QUARTERS))

        @block.vector
        def _(dve):
            tt, ts, stt = dve.tensor_tensor, dve.tensor_scalar, dve.scalar_tensor_tensor

            def link(ins, sig=dve_step):
                ins.then_inc(*sig.up())
                dve.wait_ge(*sig.at(L, sig.count))

            dve.wait_ge(once, ONCE)
            dve.wait_ge(x_loaded, 16)
            dve.wait_ge(cleared, 1)
            NM = 2 * len(LEVELS) * P
            dve.tensor_copy(msk[:, :], slab[:, 0:2, :].rearrange("p a n -> p (a n)")[:, 0:NM]).then_inc(masks_ready, 1)
            dve.wait_ge(masks_ready, 1)
            dve.sem_inc(x_tiles.handle, 1)
            with dve.Fori(0, LAYERS) as L:
                def carry_wait():
                    dve.sem_inc(carrier, 1)

                def norm_var(j):
                    dve.wait_ge(*sumsq.at(L, (j + 1) * KT))
                    ts(rstd[:, 0, :], ps[4][:, :], 1.0 / D, EPS, MUL, ADD).then_inc(*var_ready.up())
                    dve.wait_ge(*rstd_done.at(L, j + 1))

                def norm_h(j, gain):
                    norm_var(j)
                    for m in range(KT):
                        stt(hn[:, m, :], x[:, m, :], pcol(gain, m), rstd[:, 1, :], MUL, MUL).then_inc(*h_ready.up())

                def residual(j, src, gain):
                    norm_var(j)
                    for m in range(KT):
                        link(stt(src[:, m, :], src[:, m, :], pcol(gain, m), rstd[:, 1, :], MUL, MUL))
                        tt(x[:, m, :], x[:, m, :], src[:, m, :], ADD).then_inc(*x_tiles.up())

                def blocks(ap, n):
                    return ap.rearrange("p (b two n) -> p b two n", two=2, n=n)

                dve.wait_ge(*par_loaded.at(L, 16))
                norm_h(0, "pre")

                lb0, lb1 = par[:, PC["lb0"]:PC["lb0"] + FT], par[:, PC["lb1"]:PC["lb1"] + FT]
                link(tt(col[:, 5, 0:2], lb1, lb0, ALU.max))
                tt(col[:, 6, 0:2], lb0, col[:, 5, 0:2], SUB)
                tt(col[:, 6, 2:4], lb1, col[:, 5, 0:2], SUB).then_inc(*lb_in.up())
                dve.wait_ge(*lb_exp.at(L, 1))
                link(tt(col[:, 5, 2:4], col[:, 7, 0:2], col[:, 7, 2:4], ADD))
                link(dve.reciprocal(col[:, 5, 4:6], col[:, 5, 2:4]))
                link(stt(lb[:, 0, :], col[:, 7, 2:4], pcol("flag"), col[:, 5, 4:6], MUL, MUL))
                link(ts(lb[:, 1, :], lb[:, 0, :], -1.0, 1.0, MUL, ADD))
                dve.wait_ge(*act_took.at(L, TAKEN_BY["act"][INDEX[("ag", 1)]]))
                for t in range(FT):
                    ins = ts(S(1, t), S(1, t), lb[:, 1, t:t + 1], None, MUL)
                ins.then_inc(*a_ops.up())
                for t in range(FT):
                    ins = ts(S(2, t), S(2, t), lb[:, 1, t:t + 1], lb[:, 0, t:t + 1], MUL, ADD)
                link(ins)
                ts(slab[:, 2, :], slab[:, 2, :], 2.0 ** -63, None, ALU.max).then_inc(*a_prep.up())
                tt(slab[:, 3, :], slab[:, 3, :], slab[:, 12, :], MUL)
                link(dve.memset(st[:, :, :], 0.0), a_st)
                dve.wait_ge(*a_ln.at(L, 1))
                for t in range(FT):
                    carry_wait()
                    link(dve.tensor_tensor_scan(S(2, t), con[:, CC["seg"]:CC["seg"] + T], S(2, t), 0.0, MUL, ADD))
                b_, E, q_, k_ = (slab[:, i, :] for i in (2, 5, 0, 1))
                AT = [slab[:, 10 + c // 2, (c % 2) * T:(c % 2 + 1) * T] for c in range(NT)]

                def exponents(n):
                    bb, ee = blocks(b_, n), blocks(E, n)
                    nb = FT * T // (2 * n)
                    beta = bb[:, :, 0, n - 1:n].to_broadcast([P, nb, n])
                    tt(ee[:, :, 0, :], beta, bb[:, :, 0, :], SUB)
                    tt(ee[:, :, 1, :], bb[:, :, 1, :], beta, SUB).then_inc(*a_diff.up())

                for lv in range(8):
                    if lv < 7:
                        n = LEVELS[lv]
                    for c in range(NT):
                        dve.wait_ge(*a_sc.at(L, lv * NT + c + 1))
                        if lv == 0:
                            tt(heads(AT[c]), heads(ps[4 + c][:, :]), over_heads(C("ident")), MUL).then_inc(*a_sc_used.up())
                        else:
                            carry_wait()
                            dve.copy_predicated(heads(AT[c]), level(0, lv - 1), heads(ps[4 + c][:, :]))\
                                .then_inc(*a_sc_used.up())
                    if lv < 7:
                        exponents(n)
                        dve.wait_ge(*a_exp.at(L, lv + 1))
                        ee = blocks(E, n)
                        tt(ee[:, :, 0, :], ee[:, :, 0, :], blocks(k_, n)[:, :, 0, :], MUL)
                        tt(ee[:, :, 1, :], ee[:, :, 1, :], blocks(q_, n)[:, :, 1, :], MUL).then_inc(*a_ops.up())
                bc = b_.rearrange("p (b n) -> p b n", n=P)
                tt(slab[:, 8, :].rearrange("p (b n) -> p b n", n=P), bc[:, :, P - 1:P].to_broadcast([P, FT * NT, P]), bc, SUB)\
                    .then_inc(*a_diff.up())
                dve.wait_ge(*a_exp.at(L, 9))
                tt(slab[:, 7, :], slab[:, 6, :], q_, MUL)
                tt(slab[:, 8, :], slab[:, 8, :], k_, MUL).then_inc(*a_ops.up())
                for c in range(NT):
                    dve.wait_ge(*a_su.at(L, c + 1))
                    for t in range(FT):
                        ins = stt(st[:, t, :], st[:, t, :], S(6)[:, t, (c + 1) * P - 1:(c + 1) * P],
                                  ps[6][:, t * HD:(t + 1) * HD], MUL, ADD)
                    link(ins, a_st)
                dve.wait_ge(*a_ss.at(L, 2))
                for t in range(FT):
                    ins = ts(S(6, t), ps[4 + t][:, :], 1.0 / HD, EPS, MUL, ADD)
                ins.then_inc(*a_var.up())
                dve.wait_ge(*a_r.at(L, 1))
                link(tt(slab[:, 13, :], slab[:, 13, :], slab[:, 6, :], MUL))
                stt(y[:, 0, :, :], S(13), pcol("hgw"), S(3), MUL, MUL).then_inc(*y_ready.up())

                dve.wait_ge(*act_took.at(L, TAKEN_BY["act"][INDEX[("bs", 0)]]))
                dve.wait_ge(*rope_in_.at(L, 16))
                r_ = 0
                for src, cs in ((S(0), 5), (S(1), 5), (S(3), 6)):
                    for t in range(FT):
                        dve.wait_ge(*b_rot.at(L, r_ + 1))
                        link(tt(S(7, 0), ps[4 + r_ % 2][:, :], S(cs, 1), MUL))
                        link(tt(src[:, t, :], src[:, t, :], S(cs, 0), MUL))
                        link(tt(src[:, t, :], src[:, t, :], S(7, 0), ADD), b_rope)
                        r_ += 1
                dve.wait_ge(*b_rep.at(L, 1))
                dve.wait_ge(*b_rot.at(L, 7))
                link(tt(S(7, 0), ps[4][:, :], S(6, 1), MUL))
                link(tt(S(4, 0), ps[6][:, :], S(6, 0), MUL))
                link(tt(S(4, 0), S(4, 0), S(7, 0), ADD), b_rope)
                dve.wait_ge(*b_iwc.at(L, 1))
                n_ix = 0
                for b in range(1, NT):
                    n = (b + 1) * P
                    sc = slab[:, 10 + b // 2, (b % 2) * T:(b % 2) * T + n]
                    for j in range(IH):
                        dve.wait_ge(*b_relu.at(L, n_ix + 1))
                        r9 = S(9, n_ix % 2)[:, 0:n]
                        if j == 0:
                            ins = ts(sc, r9, iw[:, b, j:j + 1], None, MUL)
                        else:
                            ins = stt(sc, r9, iw[:, b, j:j + 1], sc, MUL, ADD)
                        link(ins, b_acc)
                        n_ix += 1
                    link(tt(sc[:, b * P:n], sc[:, b * P:n], C("cneg"), ADD))
                for r in range(TOPK // 8):
                    for b in range(1, NT):
                        n = (b + 1) * P
                        sc = slab[:, 10 + b // 2, (b % 2) * T:(b % 2) * T + n]
                        carry_wait()
                        ins = dve.max(col[:, b, :], sc)
                    link(ins)
                    carry_wait()
                    for b in range(1, NT):
                        n = (b + 1) * P
                        sc = slab[:, 10 + b // 2, (b % 2) * T:(b % 2) * T + n]
                        ins = dve.match_replace(sc, col[:, b, :], sc, TAKEN)
                    link(ins)
                for b in range(1, NT):
                    n = (b + 1) * P
                    sc = slab[:, 10 + b // 2, (b % 2) * T:(b % 2) * T + n]
                    ins = ts(sc, sc, -2e38, NEG, ALU.is_gt, MUL)
                link(ins)

                def softmax(which, bias):
                    base = 16 * which

                    def probs(i):
                        n = (i // H + 1) * P
                        buf = S(14 + i % 4 // 2, i % 2)[:, 0:n]
                        dve.wait_ge(*at_ex.at(L, base + i + 1))
                        link(dve.reciprocal(col[:, 6, i % 4:i % 4 + 1], col[:, 2, i % 4:i % 4 + 1]))
                        ts(buf, buf, col[:, 6, i % 4:i % 4 + 1], None, MUL).then_inc(*at_p.up())

                    for i in range(16):
                        b, h = divmod(i, H)
                        n = (b + 1) * P
                        buf = S(14 + i % 4 // 2, i % 2)[:, 0:n]
                        dve.wait_ge(*at_lg.at(L, base + i + 1))
                        if i >= 4:
                            dve.wait_ge(*at_tr.at(L, base + i - 3))
                        carry_wait()
                        link(dve.tensor_tensor_reduce(out=buf, in0=ps[4 + i % 2][:, 0:n], in1=bias(b, h, n), scale=HD ** -0.5,
                                                      scalar=-3e38, op0=ADD, op1=ALU.max, accum_out=col[:, 0, i % 4:i % 4 + 1]))
                        ts(col[:, 1, i % 4:i % 4 + 1], col[:, 0, i % 4:i % 4 + 1], -1.0, None, MUL).then_inc(*at_mx.up())
                        if i:
                            probs(i - 1)
                    probs(15)

                softmax(0, lambda b, h, n: C("cneg") if b == 0 else slab[:, 10 + b // 2, (b % 2) * T:(b % 2) * T + n])

                dve.wait_ge(*act_took.at(L, TAKEN_BY["act"][INDEX[("cl", 0)]]))
                for i, (s_, n_) in enumerate(((0, 2), (1, 2), (2, 2), (3, 1))):
                    src = S(s_)[:, 0:n_, :]
                    dd = S(4)[:, 0:n_, :]
                    tt(dd[:, :, 1:T], src[:, :, 0:T - 1], src[:, :, 1:T], SUB)
                    link(ts(dd[:, :, 0:1], src[:, :, 0:1], -1.0, None, MUL))
                    for t in range(n_):
                        ins = stt(src[:, t, :], dd[:, t, :], pcol("mu", 2 * i + t), src[:, t, :], MUL, ADD)
                    link(ins, c_mix if i == 3 else dve_step)
                for t in range(FT):
                    ins = ts(S(9, t), S(1, t), pcol("kk", t), None, MUL)
                link(ins)
                for t in range(FT):
                    tt(S(10, t), S(9, t), S(9, t), MUL).then_inc(*c_sq.up())
                dve.wait_ge(*c_sg.at(L, 4))
                link(ts(slab[:, 6, :], slab[:, 6, :], -float(np.exp(-0.5)), None, MUL))
                for t in range(FT):
                    carry_wait()
                    link(dve.tensor_tensor_scan(S(5, t), con[:, CC["seg"]:CC["seg"] + T], S(6, t), 0.0, MUL, ADD))
                link(ts(slab[:, 4, :], slab[:, 7, :], -1.0, None, ADD))
                for t in range(FT):
                    ins = ts(S(4, t), S(4, t), pcol("ka", t), 1.0, MUL, ADD)
                link(ins)
                link(tt(slab[:, 1, :], slab[:, 1, :], slab[:, 4, :], MUL))
                for t in range(FT):
                    stt(S(4, t), S(0, t), pcol("rk", t), S(1, t), MUL, MUL).then_inc(*c_sq.up())
                dve.wait_ge(*c_vgs.at(L, 2))
                link(tt(slab[:, 3, :], v1st[:, :, :].rearrange("p t n -> p (t n)"), slab[:, 2, :], SUB))
                link(stt(slab[:, 3, :], slab[:, 12, :], pcol("flag"), slab[:, 3, :], MUL, MUL))
                link(tt(slab[:, 2, :], slab[:, 2, :], slab[:, 3, :], ADD))
                dve.tensor_copy(v1st[:, :, :].rearrange("p t n -> p (t n)"), slab[:, 2, :])
                dve.wait_ge(*c_ss.at(L, 2))
                for t in range(FT):
                    ins = ts(S(10, t), ps[6 + t][:, :], 1e-24, None, ALU.max)
                ins.then_inc(*c_kkv.up())
                cc = slab[:, 5, :].rearrange("p (b n) -> p b n", n=P)
                mid = col[:, 0, :]
                end = col[:, 1, :]
                mid4 = mid.rearrange("p (t c) -> p t c", t=FT)
                fac4 = col[:, 4, :].rearrange("p (t c) -> p t c", t=FT)
                dve.tensor_copy(mid, cc[:, :, P // 2 - 1])
                link(dve.tensor_copy(end, cc[:, :, P - 1]))
                link(tt(cc, cc, mid[:, :, None].to_broadcast([P, FT * NT, P]), SUB))
                tt(slab[:, 6, :], slab[:, 5, :], slab[:, 6, :], SUB)
                link(tt(col[:, 4, :], end, mid, SUB))
                link(tt(fac4[:, :, 0:NT - 1], fac4[:, :, 0:NT - 1], mid4[:, :, 1:NT], ADD), c_ex)
                dve.wait_ge(*c_ss.at(L, 4))
                for t in range(FT):
                    tt(S(11, t), ps[4 + t][:, :], S(2, t), MUL)
                dve.wait_ge(*c_kkr.at(L, 1))
                dve.wait_ge(*c_exd.at(L, 1))
                link(tt(slab[:, 9, :], slab[:, 9, :], slab[:, 10, :], MUL))
                link(tt(slab[:, 7, :], slab[:, 7, :], slab[:, 9, :], MUL))
                tt(slab[:, 12, :], slab[:, 12, :], slab[:, 0, :], MUL)
                stt(slab[:, 13, :], slab[:, 13, :], -1.0, slab[:, 9, :], MUL, MUL)
                link(tt(slab[:, 15, :], slab[:, 14, :], slab[:, 7, :], MUL))
                link(tt(slab[:, 14, :], slab[:, 14, :], slab[:, 1, :], MUL), c_til)
                link(dve.memset(st[:, :, :], 0.0), c_st)
                half = lambda i: slab[:, i // 2, (i % 2) * T:(i % 2 + 1) * T]
                Lm, X_, LTm, MTm, RBm, RKm, XT_, R_ = (half(i) for i in range(8))
                dve.wait_ge(*c_tru.at(L, 6))
                for lv in range(1, 7):
                    ins = dve.tensor_copy(heads(half(7 + lv)), over_heads(C("ident")))
                link(ins)
                for c in range(NT):
                    def by_parity(ap, par):
                        return ap.rearrange("p (t two n) -> p t two n", two=2, n=P)[:, :, par, :]

                    for i in range(6):
                        dve.wait_ge(*c_m.at(L, 6 * c + i + 1))
                        if i < 4:
                            pair = slab[:, 1 + i // 2, :].rearrange("p (m t two n) -> p m t two n", m=2, two=2, n=P)
                            mask = C("slt" if i < 2 else "sle")[:, None, None, :].to_broadcast([P, 2, FT, P])
                            ins = tt(pair[:, :, :, i % 2, :], ps[4 + i][:, :].rearrange("p (m t n) -> p m t n", m=2, n=P),
                                     mask, MUL)
                        else:
                            ins = tt(by_parity(Lm, i % 2), ps[i][:, 0:256].rearrange("p (t n) -> p t n", n=P),
                                     C("sgt")[:, None, :].to_broadcast([P, FT, P]), MUL)
                        ins.then_inc(*c_mu.up())
                    dve.wait_ge(*c_mu.at(L, 6 * c + 6))
                    dve.tensor_copy(heads(X_), over_heads(C("ident")))
                    link(dve.tensor_copy(heads(XT_), over_heads(C("ident"))))
                    carry_wait()
                    dve.copy_predicated(heads(X_), level(1, 0), heads(Lm))
                    dve.copy_predicated(heads(XT_), level(0, 0), heads(LTm)).then_inc(*c_x1.up())
                    for lv in range(1, 7):
                        dve.wait_ge(*c_pp.at(L, 6 * c + lv))
                        carry_wait()
                        dve.copy_predicated(heads(half(7 + lv)), level(1, lv), heads(ps[4][:, :])).then_inc(*c_ppu.up())
                    dve.wait_ge(*c_s.at(L, c + 1))
                    for t in range(FT):
                        ins = tt(st[:, t, :], st[:, t, :], ps[7][:, t * HD:(t + 1) * HD], ADD)
                    link(ins)
                    for t in range(FT):
                        ins = ts(st[:, t, :], st[:, t, :], col[:, 3, t * NT + c:t * NT + c + 1], None, MUL)
                    link(ins, c_st)
                dve.wait_ge(*c_mean.at(L, 2))
                for t in range(FT):
                    ins = stt(S(7, t), ps[4 + t][:, :], -1.0 / HD, S(7, t), MUL, ADD)
                link(ins, c_cen)
                dve.wait_ge(*c_var.at(L, 2))
                for t in range(FT):
                    ins = ts(S(10, t), ps[6 + t][:, :], 1.0 / HD, GN_EPS, MUL, ADD)
                ins.then_inc(*c_vv.up())
                dve.wait_ge(*c_rr.at(L, 1))
                link(tt(slab[:, 7, :], slab[:, 7, :], slab[:, 10, :], MUL))
                for t in range(FT):
                    ins = ts(S(7, t), S(7, t), pcol("lnw", t), pcol("lnb", t), MUL, ADD)
                link(ins)
                link(tt(slab[:, 7, :], slab[:, 7, :], slab[:, 11, :], ADD))
                tt(y[:, 2, :, :], S(7), S(8), MUL).then_inc(*y_ready.up())

                f_, t5, c5 = small[SM_F:SM_F + H, :], S(5, 0)[SM_F:SM_F + H, :], S(5, 1)[SM_F:SM_F + H, :]
                link(ts(f_, f_, pcol("foxb", 0, SM_F, SM_F + H), None, ADD))
                stt(t5, f_, -1.0, f_, MUL, ALU.max).then_inc(*d_abs.up())
                link(ts(f_, f_, 0.0, None, ALU.min))
                dve.wait_ge(*d_ln.at(L, 1))
                link(tt(t5, t5, f_, SUB))
                carry_wait()
                dve.tensor_tensor_scan(c5, C("ones", SM_F, SM_F + H, P)[:, 0:1].to_broadcast([H, T]), t5, 0.0, MUL, ADD)\
                    .then_inc(*d_c.up())
                dve.wait_ge(*d_bcu.at(L, H))
                softmax(1, lambda b, h, n: S(6 + h // 2, h % 2)[:, 0:n])

                for n in range(4):
                    for m in range(KT):
                        i_ = n * KT + m
                        d = INDEX[(f"branch{n}", m)]
                        dve.wait_ge(*dense_done.at(L, issued(d)))
                        dve.wait_ge(*act_took.at(L, TAKEN_BY["act"][INDEX[(f"gate{n}", m)]]))
                        if i_ >= 2:
                            dve.wait_ge(*merged.at(L, i_ - 1))
                        ins = tt(tmp[:, 2 + i_ % 2, :], ps[d % 4][:, :], tmp[:, m % 2, :], MUL)
                        ins.then_inc(*product.up())
                residual(1, u, "post")
                norm_h(2, "mpre")
                dve.wait_ge(*acc0.at(L, 1))
                carry_wait()
                with dve.Fori(0, QUARTERS) as q:
                    for m in range(KT):
                        dve.wait_ge(*dense_done.at(L, q * 16 + (REAL0 + 8 + m + 1)))
                        tt(acc[:, m, :], acc[:, m, :], ps[m % 4][:, :], ADD).then_inc(*dve_took.up(QUARTERS))
                dve.wait_ge(*dve_took.at(L, DVE0 + 8 * QUARTERS))
                residual(3, acc, "mpost")

    return signals


def pack_weights(inputs):
    w_in, w_branch = np.asarray(inputs["w_in"]), np.asarray(inputs["w_branch"])
    w_out, w_up, w_down = (np.asarray(inputs[n]) for n in ("w_out", "w_up", "w_down"))

    def chunk(w):
        return w.reshape(-1, P, w.shape[1]).transpose(1, 0, 2).reshape(P, -1)
    proj = np.zeros((LAYERS, PROJ_CHUNKS, P, CH), np.float32)
    merge = np.zeros((LAYERS, MERGE_CHUNKS, P, CHM), np.float32)
    rest = np.zeros((LAYERS, REST_CHUNKS, P, CH), np.float32)
    for l in range(LAYERS):
        wl = w_in[l]
        small = np.zeros((D, 256), np.float32)
        small[:, SM_IK:SM_IK + IDIM] = wl[:, B_IK:B_IK + IDIM]
        small[:, SM_F:SM_F + H] = wl[:, D_F:D_F + H]
        small[:, SM_IW:SM_IW + IH] = wl[:, B_IW:B_IW + IH]
        hidden = np.zeros((D, 256), np.float32)
        hidden[:, 0:P] = wl[:, C_L:C_L + P]
        cols = [wl[:, c:c + 256] for c in (A_Q, A_F, A_I, A_G, B_Q, B_K, B_V, B_IQ)] + [small]
        cols += [wl[:, c:c + 256] for c in (C_R, C_K, C_V)] + [hidden] + [wl[:, c:c + 256] for c in (D_Q, D_K, D_V)]
        for i, w in enumerate(cols):
            proj[l, i] = chunk(w)
        for n in range(4):
            for i in range(KT // 2):
                merge[l, 4 * n + i, :, :CH] = chunk(wl[:, GATE + n * D + 256 * i:GATE + n * D + 256 * (i + 1)])
                merge[l, 4 * n + i, :, CH:] = chunk(w_branch[l, n][:, 256 * i:256 * (i + 1)])
        rows = [w_out[l][:, 256 * i:256 * (i + 1)] for i in range(4)]
        for q in range(QUARTERS):
            rows += [w_up[l][:, D * q + 256 * i:D * q + 256 * (i + 1)] for i in range(4)]
            rows += [w_down[l][D * q:D * (q + 1), 256 * i:256 * (i + 1)] for i in range(4)]
        for i, w in enumerate(rows):
            rest[l, i] = chunk(w)
    return proj.reshape(-1, P, CH), merge.reshape(-1, P, CHM), rest.reshape(-1, P, CH)


def pack_params(inputs):
    par = np.zeros((LAYERS, P, PAR), np.float32)
    a = {k: np.asarray(v) for k, v in inputs.items()}
    for l in range(LAYERS):
        g = max(l - 1, 0)

        def put(name, v):
            v = v.reshape(-1, P).T
            par[l, :, PC[name]:PC[name] + v.shape[1]] = v
        for name, key in (("pre", "norm_mix_pre"), ("post", "norm_mix_post"), ("mpre", "norm_mlp_pre"),
                          ("mpost", "norm_mlp_post"), ("mu", "rwkv_mu"), ("w0", "rwkv_w0"), ("a0", "rwkv_a0"),
                          ("kk", "rwkv_k_k"), ("ka", "rwkv_k_a"), ("rk", "rwkv_r_k"), ("lnw", "rwkv_ln_w"),
                          ("lnb", "rwkv_ln_b")):
            put(name, a[key][l])
        put("v0", a["rwkv_v0"][g])
        put("hgw", np.concatenate([a["hgrn_norm_w"][l]] * 2))
        put("lb0", a["hgrn_lb_logits"][0])
        put("lb1", a["hgrn_lb_logits"][1])
        par[l, SM_F:SM_F + H, PC["foxb"]] = a["fox_f_bias"][l]
        par[l, :, PC["flag"]] = min(l, 1)
        par[l, 0:32, NPAR:NPAR + 256] = a["rwkv_w2"][l]
        par[l, 32:64, NPAR:NPAR + 256] = a["rwkv_a2"][l]
        par[l, 64:128, NPAR:NPAR + 256] = a["rwkv_g2"][l]
        par[l, :, NPAR + 256:NPAR + 320] = a["rwkv_v1"][g].reshape(FT, P, 32).transpose(1, 0, 2).reshape(P, 64)
        par[l, 0:32, NPAR + 320:] = a["rwkv_v2"][g]
    return par


def kernel(**inputs):
    import concourse.bacc as bacc
    from concourse.bass_utils import run_bass_kernel_spmd

    nc = bacc.Bacc("TRN2", target_bir_lowering=False, num_devices=1)
    proj, merge, rest = pack_weights(inputs)
    con, msk, rope = constants()
    x = np.asarray(inputs["x"])[0].T.reshape(KT, P, T).transpose(1, 0, 2).reshape(P, KT * T)
    arrays = {"x_in": x, "wproj": proj, "wmerge": merge, "wrest": rest, "params": pack_params(inputs),
              "tables": con, "masks": msk, "rope": rope}
    arrays = {k: np.ascontiguousarray(v) for k, v in arrays.items()}
    args = [nc.dram_tensor(k, v.shape, mybir.dt.from_np(v.dtype), kind="ExternalInput").ap() for k, v in arrays.items()]
    args.append(nc.dram_tensor("out", (P, KT * T), mybir.dt.float32, kind="ExternalOutput").ap())
    trunk_kernel(nc, *args)
    r = run_bass_kernel_spmd(nc, [arrays], core_ids=[0])
    got = r.results[0]["out"]
    return got.reshape(P, KT, T).transpose(1, 0, 2).reshape(D, T).T.reshape(1, T, D)
```

```python
import numpy as np
import concourse.bass as bass
from concourse import mybir
from contextlib import ExitStack

LAYERS, T, D = 2, 512, 1024
P = 128
KT = D // P
W = D // 4
HD = 64
H = W // HD
NT = T // P
FT = W // P
IH, IDIM, TOPK = 8, 32, min(256, T // 4)
DFF = 4 * D
QUARTERS = 4
EPS, GN_EPS = 1e-6, 64e-5
NEG = -8e30
TAKEN = -3e38
CH = KT * P
CHM = CH + FT * P

A_Q, A_F, A_I, A_G = 0, 256, 512, 768
B_Q, B_K, B_V, B_IQ, B_IK, B_IW = 1024, 1280, 1536, 1792, 2048, 2080
C_R, C_K, C_V, C_L = 2088, 2344, 2600, 2856
D_Q, D_K, D_V, D_F, GATE = 2984, 3240, 3496, 3752, 3756
SM_IK, SM_F, SM_IW = 0, 32, 64

PROJ_A = (("aq", "fm", 2), ("af", "fm", 2), ("ai", "tm", 2), ("ag", "fm", 2))
PROJ_B = (("bs", "fm", 1), ("bq", "fm", 2), ("bk", "fm", 2), ("biq", "fm", 2), ("bv", "tm", 2))
PROJ_C = (("cr", "fm", 2), ("ck", "fm", 2), ("cv", "fm", 2), ("cl", "fm", 1))
PROJ_D = (("dq", "fm", 2), ("dk", "fm", 2), ("dv", "tm", 2))
DENSE = []
for proj, gates in ((PROJ_A + PROJ_B + PROJ_C, (0, 1)), (PROJ_D, (2, 3))):
    for name, kind, n in proj:
        DENSE += [(name, i, kind, "act") for i in range(n)]
    for n in gates:
        for m in range(KT):
            DENSE += [(f"gate{n}", m, "fm", "act"), (f"branch{n}", m, "fm", "dve")]
DENSE += [("out", m, "fm", "act") for m in range(KT)]
MLP0 = len(DENSE)
BANK0 = -MLP0 % 4
INDEX = {(n, i): k for k, (n, i, _, _) in enumerate(DENSE)}
TAKEN_BY = {e: [sum(x[3] == e for x in DENSE[:k + 1]) for k in range(MLP0)] for e in ("act", "dve")}
ACT0, DVE0 = TAKEN_BY["act"][-1], TAKEN_BY["dve"][-1]
CHUNK_OF = [sum(not x[0].startswith("branch") for x in DENSE[:k + 1]) - 1 for k in range(MLP0)]
LAST_OF_CHUNK = {c: k for k, c in enumerate(CHUNK_OF)}
MLP_CHUNK0 = CHUNK_OF[-1] + 1
CHUNKS = MLP_CHUNK0 + 16 * QUARTERS
NA, NB, NC, ND = (sum(n for _, _, n in x) for x in (PROJ_A, PROJ_B, PROJ_C, PROJ_D))
RUNS = (("proj", 0, 0, NA + NB + NC), ("merge", 0, NA + NB + NC, 2 * KT), ("proj", NA + NB + NC, NA + NB + NC + 2 * KT, ND),
        ("merge", 2 * KT, NA + NB + NC + ND + 2 * KT, 2 * KT), ("rest", 0, NA + NB + NC + ND + 4 * KT, KT + 16 * QUARTERS))
assert all(first % 2 == 0 and at % 2 == 0 and n % 2 == 0 for _, at, first, n in RUNS)


END, _n = [], 0
for name, _, _, _ in DENSE:
    _n += FT if name.startswith("branch") else KT
    END.append(_n)


def schedule():
    reach, taken, gated = {}, {}, {}
    at = 0

    def place(key, steps, limit):
        nonlocal at
        at = max(at, min(at + steps, END[INDEX[limit]]))
        reach[key], taken[key], gated[key] = at, at - TAKE_LAG, at - GATE_LAG

    def all_of(key, last):
        nonlocal at
        end = END[INDEX[last]]
        at = max(at, end)
        reach[key], taken[key], gated[key] = at, max(end, at - TAKE_LAG), max(end, at - GATE_LAG)

    all_of("A", ("ag", 1))
    for lv in range(8):
        place(("a_level", lv), FILL["a_level"][lv], ("cl", 0))
    for c in range(NT + 1):
        place(("a_keys", c), FILL["a_keys"], ("cl", 0))
    for c in range(NT):
        place(("a_chunk", c), FILL["a_chunk"], ("cl", 0))
    for i in range(2):
        place(("a_norm", i), FILL["a_norm"], ("cl", 0))
    all_of("B", ("bv", 1))
    for r in range(7):
        place(("b_rope", r), FILL["b_rope"], ("branch0", KT - 1))
    for i in range(3 * IH):
        place(("b_ix", i), FILL["b_ix"], ("branch0", KT - 1))
    for r in range(TOPK // 8):
        place(("b_topk", r), FILL["b_topk"], ("branch0", KT - 1))
    for i in range(16):
        for n in range(2):
            place(("b_att", i, n), FILL["b_att"][n], ("branch0", KT - 1))
    all_of("C", ("cl", 0))
    for i in range(4):
        place(("c_prep", i), FILL["c_prep"][i], ("branch1", KT - 1))
    for c in range(NT):
        place(("c_mask", c), FILL["c_mask"], ("dk", 1))
        for lv in range(1, 7):
            for n in range(2):
                place(("c_level", c, lv, n), FILL["c_level"][n], ("dk", 1))
        for i in range(3):
            place(("c_out", c, i), FILL["c_out"][i], ("dk", 1))
    for i in range(2):
        place(("c_norm", i), FILL["c_norm"], ("dv", 1))
    all_of("D", ("dv", 1))
    for i in range(2):
        place(("d_prep", i), FILL["d_prep"], ("branch2", KT - 1))
    for i in range(16):
        for n in range(2):
            place(("d_att", i, n), FILL["d_att"][n], ("branch2", KT - 1))
    all_of("rest", ("out", KT - 1))
    return reach, taken, gated


TAKE_LAG, GATE_LAG = 4, 8
FILL = {"a_level": (8, 8, 8, 8, 8, 8, 8, 8), "a_keys": 2, "a_chunk": 2, "a_norm": 4, "b_rope": 2, "b_ix": 1, "b_topk": 5,
        "b_att": (1, 1), "c_prep": (4, 4, 4, 20), "c_mask": 3, "c_level": (1, 1), "c_out": (2, 2, 2), "c_norm": 4,
        "d_prep": 4, "d_att": (2, 2)}
REACH, TAKEN_TO, GATED_TO = schedule()

PC, _n = {}, 0
for name, n in (("pre", 8), ("post", 8), ("mpre", 8), ("mpost", 8), ("hgw", 1), ("lb0", 2), ("lb1", 2),
                ("foxb", 1), ("mu", 7), ("w0", 2), ("a0", 2), ("kk", 2), ("ka", 2), ("rk", 2), ("lnw", 2),
                ("lnb", 2), ("v0", 2), ("flag", 1)):
    PC[name] = _n
    _n += n
NPAR = _n
PAR = NPAR + 256 + 64 + 256

CC, _n = {}, 0
for name, n in (("ident", P), ("ones", P), ("blk", P), ("roth", P), ("roti", P), ("rep", P), ("reprot", P),
                ("cneg", P), ("slt", P), ("sle", P), ("sgt", P), ("sel", H), ("seg", T)):
    CC[name] = _n
    _n += n
NCON = _n
LEVELS = [2 ** i for i in range(7)]


def constants():
    c = np.zeros((P, NCON), np.float32)
    i, j = np.arange(P)[:, None], np.arange(P)[None, :]
    put = lambda name, v: c.__setitem__((slice(None), slice(CC[name], CC[name] + v.shape[1])), v)
    put("ident", (i == j) * 1.0)
    put("ones", np.ones((P, P)))
    put("blk", (i // HD == j // HD) * 1.0)

    def rot(dim):
        half, r = dim // 2, j % dim
        return np.where((r < half) & (i == j + half), -1.0, 0.0) + np.where((r >= half) & (i == j - half), 1.0, 0.0)
    put("roth", rot(HD))
    put("roti", rot(IDIM))
    put("rep", (i == j % IDIM) * 1.0)
    put("reprot", (rot(IDIM)[:, :IDIM])[:, np.arange(P) % IDIM])
    put("cneg", np.where(j > i, NEG, 0.0))
    put("slt", (i < j) * 1.0)
    put("sle", (i <= j) * 1.0)
    put("sgt", (i > j) * 1.0)
    sel = np.zeros((P, H))
    for h in range(H):
        sel[SM_F + h, h] = 8.0
    put("sel", sel)
    put("seg", np.broadcast_to((np.arange(T) % P != 0) * 1.0, (P, T)))
    m = np.zeros((P, 2, len(LEVELS), P), np.float32)
    for k, n in enumerate(LEVELS):
        same = i // (2 * n) == j // (2 * n)
        m[:, 0, k] = same & (i % (2 * n) < n) & (j % (2 * n) >= n)
        m[:, 1, k] = m[:, 0, k].T
    rope = np.zeros((P, 4, T), np.float32)
    for k, dim in enumerate((HD, IDIM)):
        inv = (1.0 / (np.float32(10000.0) ** (np.arange(0, dim, 2, dtype=np.float32) / np.float32(dim)))).astype(np.float32)
        ang = np.arange(T, dtype=np.float32)[None, :] * inv[:, None]
        rope[:, 2 * k] = np.tile(np.cos(ang), (2 * P // dim, 1))
        rope[:, 2 * k + 1] = np.tile(np.sin(ang), (2 * P // dim, 1))
    return c, m.reshape(P, -1), rope.reshape(P, -1)


class Signal:

    def __init__(self, handle, name, per_layer):
        self.handle, self.name, self.per_layer, self.count = handle, name, per_layer, 0

    def at(self, layer, k):
        return self.handle, layer * self.per_layer + k

    def up(self, times=1):
        self.count += times
        return self.handle, 1


def trunk_kernel(nc, x_in, wproj, wmerge, wrest, par_in, con_in, mask_in, rope_in, out):
    f32, f32r, u8 = mybir.dt.float32, mybir.dt.float32r, mybir.dt.uint8
    ALU, ACT, AX = mybir.AluOpType, mybir.ActivationFunctionType, mybir.AxisListType
    nc.disable_value_cache = True
    MUL, ADD, SUB = ALU.mult, ALU.add, ALU.subtract
    ctx = ExitStack()
    with ctx:
        def sb(name, shape, dt=f32):
            return ctx.enter_context(nc.sbuf_tensor(name, shape, dt))

        signals = []

        def signal(name, per_layer):
            signals.append(Signal(ctx.enter_context(nc.semaphore(name)), name, per_layer))
            return signals[-1]

        x = sb("x", [P, KT, T])
        hn = [sb(f"hn_{n}", [P, KT, T], f32r) for n in ("hi", "lo")]
        y = [sb(f"y_{n}", [P, 2, FT, T], f32r) for n in ("hi", "lo")]
        wsl = sb("wsl", [P, 2, CHM])
        wsp = [sb(f"w_{n}", [P, 2, CHM], f32r) for n in ("hi", "lo")]
        slab0 = nc.sbuf_base
        slab = sb("slab", [P, 20, FT * T])
        assert nc.sbuf_base == slab0 + 20 * FT * T * 4
        acc = slab[:, 16:20, :].rearrange("p a (t n) -> p (a t) n", n=T)
        mix = slab[:, 0:4, :].rearrange("p a (t n) -> p (a t) n", n=T)
        u = [nc.alloc_sbuf_tensor_at(f"u_{n}", [P, KT, T], f32r, offset=slab0 + (8 + 4 * i) * FT * T * 4)
             for i, n in enumerate(("hi", "lo"))]
        con = sb("con", [P, NCON])
        msk = sb("msk", [P, 2 * len(LEVELS) * P], u8)
        par = sb("par", [P, PAR])
        tmp = sb("tmp", [P, 4, T])
        rstd = sb("rstd", [P, 2, T])
        small = sb("small", [P, T])
        iw = sb("iw", [P, NT, IH])
        st = sb("st", [P, FT, HD])
        lb = sb("lb", [P, 2, FT])
        col = sb("col", [P, 8, 8])
        v1st = sb("v1st", [P, FT, T])
        ps = [ctx.enter_context(nc.psum_tensor(f"bank{i}", [P, 512], f32)) for i in range(8)]

        def S(i, half=None):
            v = slab[:, i, :].rearrange("p (t n) -> p t n", t=FT)
            return v if half is None else v[:, half, :]

        def C(name, lo=0, hi=P, n=P):
            return con[lo:hi, CC[name]:CC[name] + n]

        def pcol(name, i=0, lo=0, hi=P):
            return par[lo:hi, PC[name] + i:PC[name] + i + 1]

        def heads(ap):
            return ap.rearrange("p (h t) -> p h t", h=H)

        def over_heads(ap):
            return ap[:, None, :].to_broadcast([P, H, P])

        def level(side, k):
            m = (side * len(LEVELS) + k) * P
            return over_heads(msk[:, m:m + P])

        def half(i):
            return slab[:, i // 2, (i % 2) * T:(i % 2 + 1) * T]

        c_halves = [half(i) for i in (24, 25, 26, 27, 28, 29, 31, 18, 19)]
        c_pairs = [slab[:, 12, :], slab[:, 13, :]]
        lora = par[:, NPAR:NPAR + 256]
        v1w = par[:, NPAR + 256:NPAR + 320].rearrange("p (t n) -> p t n", t=FT)
        v2w = par[0:32, NPAR + 320:NPAR + 576]

        once = ctx.enter_context(nc.semaphore("tables_loaded"))
        x_loaded = ctx.enter_context(nc.semaphore("x_loaded"))
        masks_ready = ctx.enter_context(nc.semaphore("masks_ready"))
        cleared = ctx.enter_context(nc.semaphore("buffers_cleared"))
        carrier = ctx.enter_context(nc.semaphore("wait_carrier"))
        stored = ctx.enter_context(nc.semaphore("out_stored"))
        rope_in_ = signal("rope_loaded", 16)
        w_arrived = [ctx.enter_context(nc.semaphore(f"weights_arrived_{s}")) for s in range(2)]
        par_loaded = signal("params_loaded", 16)
        x_tiles = signal("x_updated", 2 * KT)
        dense_done = signal("dense_done", MLP0 + 16 * QUARTERS)
        w_hi_done = signal("weights_hi_ready", CHUNKS)
        w_split = signal("weights_split", CHUNKS)
        act_took = signal("act_took_dense", ACT0 + 8 * QUARTERS)
        dve_took = signal("dve_took_dense", DVE0 + 8 * QUARTERS)
        dve_step = signal("dve_step", 278)
        act_step = signal("act_step", 8)
        squared = signal("squared", 4 * KT)
        sumsq = signal("sum_of_squares", 4 * KT)
        var_ready = signal("variance_ready", 4)
        rstd_done = signal("rstd_by_exp", 4)
        h_raw = signal("h_ready", 2 * KT)
        h_hi = signal("h_hi_ready", 2 * KT)
        h_ready = signal("h_split", 2 * KT)
        a_prep = signal("a_gate_logit_ready", 1)
        a_ln = signal("a_log_gate_ready", 1)
        a_diff = signal("a_decay_exponents_ready", 8)
        a_exp = signal("a_decays_ready", 9)
        a_ops = signal("a_level_operands_ready", 9)
        a_sc = signal("a_scores_ready", 8 * NT)
        a_sc_used = signal("a_scores_taken", 8 * NT)
        a_tr = signal("a_keys_transposed", 4)
        a_tr_used = signal("a_keys_taken", 4)
        a_o = signal("a_outputs_ready", NT)
        a_o_used = signal("a_outputs_taken", NT)
        a_su = signal("a_state_update_ready", NT)
        a_st = signal("a_state_ready", NT + 1)
        a_sq = signal("a_squared", 2)
        a_ss = signal("a_sum_ready", 2)
        a_var = signal("a_var_ready", 1)
        a_r = signal("a_rstd_ready", 1)
        y_ready = signal("y_ready", 2)
        lb_in = signal("bound_logits_ready", 1)
        lb_exp = signal("bound_exps_ready", 1)
        b_iwt = signal("b_index_weights_transposed", 1)
        b_rot = signal("b_rotated", 7)
        b_rep = signal("b_index_key_replicated", 1)
        b_rope = signal("b_rope_done", 7)
        b_ix = signal("b_index_scores_ready", IH * 3)
        b_relu = signal("b_relu_done", IH * 3)
        b_acc = signal("b_index_scores_used", IH * 3)
        b_iwc = signal("b_index_weights_copied", 1)
        at_lg = signal("logits_ready", 32)
        at_mx = signal("logits_masked", 32)
        at_ex = signal("exps_ready", 32)
        at_p = signal("probs_ready", 32)
        at_tr = signal("probs_transposed", 32)
        at_pt = signal("probs_taken", 32)
        at_pv = signal("attention_ready", 2 * NT)
        at_o = signal("attention_taken", 2 * NT)
        d_abs = signal("d_forget_logit_ready", 1)
        d_ln = signal("d_softplus_ready", 1)
        d_c = signal("d_cumulated", 1)
        d_bc = signal("d_cumulated_broadcast", H)
        d_bcu = signal("d_broadcast_taken", H)
        c_mix = signal("c_shifted", 1)
        c_act = signal("c_lora_hidden_ready", 1)
        c_lw = signal("c_lora_out_ready", 4)
        c_sg = signal("c_lora_out_taken", 4)
        c_g = signal("c_gate_ready", 2)
        c_vh = signal("c_value_hidden_ready", 1)
        c_vhc = signal("c_value_hidden_copied", 1)
        c_vg = signal("c_value_gate_ready", 2)
        c_vgs = signal("c_value_gate_taken", 2)
        c_sq = signal("c_squares_ready", 4)
        c_ss = signal("c_sums_ready", 4)
        c_kkv = signal("c_key_norm_ready", 1)
        c_kkr = signal("c_key_rnorm_ready", 1)
        c_ex = signal("c_exponents_ready", 1)
        c_exd = signal("c_exps_ready", 1)
        c_til = signal("c_operands_ready", 1)
        c_tr = signal("c_transposed", 6)
        c_tru = signal("c_transposes_taken", 6)
        c_m = signal("c_pairwise_ready", 6 * NT)
        c_mu = signal("c_pairwise_masked", 6 * NT)
        c_x1 = signal("c_inverse_started", NT)
        c_pp = signal("c_level_product_ready", 6 * NT)
        c_ppu = signal("c_level_product_masked", 6 * NT)
        c_xx = signal("c_level_inverse_ready", 11 * NT)
        c_xxu = signal("c_level_inverse_taken", 11 * NT)
        c_b = signal("c_rhs_ready", NT)
        c_bu = signal("c_rhs_taken", NT)
        c_u = signal("c_solution_ready", NT)
        c_uu = signal("c_solution_taken", NT)
        c_y = signal("c_outputs_ready", NT)
        c_yu = signal("c_outputs_taken", NT)
        c_s = signal("c_state_update_ready", NT)
        c_st = signal("c_state_ready", NT + 1)
        c_mean = signal("c_mean_ready", 2)
        c_cen = signal("c_centred", 1)
        c_csq = signal("c_centred_squared", 2)
        c_var = signal("c_variance_sum_ready", 2)
        c_vv = signal("c_variance_ready", 1)
        c_rr = signal("c_rstd_ready", 1)
        merged = signal("merged_ready", 4 * KT)
        product = dve_took
        m_split = signal("merged_split", KT)
        y_hi = signal("attention_hi_ready", 2 * NT)
        acc0 = signal("acc_cleared", 1)
        u_ready = signal("hidden_ready", 4 + 8 * QUARTERS)

        block = ctx.enter_context(nc.Block())
        ONCE = 16 * 2

        @block.sync
        def _(sp):
            sp.dma_start(con[:, :], con_in).then_inc(once, 16)
            NM = 2 * len(LEVELS) * P
            sp.dma_start(slab[:, 0:2, :].rearrange("p a n -> p (a n)")[:, 0:NM], mask_in).then_inc(once, 16)
            sp.dma_start(x[:, :, :].rearrange("p k t -> p (k t)"), x_in).then_inc(x_loaded, 16)
            with sp.Fori(0, LAYERS) as layer:
                for name, at, first, count in RUNS:
                    src, size, per_layer = {"proj": (wproj, CH, NA + NB + NC + ND), "merge": (wmerge, CHM, 4 * KT),
                                            "rest": (wrest, CH, KT + 16 * QUARTERS)}[name]
                    with sp.Fori(0, count // 2) as pair:
                        for s in range(2):
                            row = sp.snap(layer * per_layer + 2 * pair + (at + s))
                            need = sp.snap(layer * CHUNKS + 2 * pair + (first + s + 1))
                            sp.wait_ge(w_split.handle, need)
                            sp.dma_start(wsl[:, s, 0:size],
                                         src[bass.ds(row, 1)].rearrange("a p n -> (a p) n")).then_inc(w_arrived[s], 16)
            sp.wait_ge(x_tiles.handle, LAYERS * 2 * KT + 1)
            sp.dma_start(out, x[:, :, :].rearrange("p k t -> p (k t)")).then_inc(stored, 16)
            sp.wait_ge(stored, 16)

        @block.tensor
        def _(pe):
            pe.wait_ge(once, ONCE)
            pe.wait_ge(cleared, 1)
            mm = pe.matmul
            with pe.Fori(0, LAYERS) as L:
                step = [0]

                def product3(o_, stat, mov, first, last):
                    mm(o_, stat[0], mov[0], start=first, stop=False)
                    mm(o_, stat[0], mov[1], start=False, stop=False)
                    return mm(o_, stat[1], mov[0], start=False, stop=last)

                def weights(c, off, k):
                    w0 = off + k * P
                    return [w[:, c % 2, w0:w0 + P] for w in wsp]

                def begin(d):
                    name, i, _, _ = DENSE[d]
                    n = int(name[-1]) if name.startswith("branch") else None
                    if n is None:
                        pe.wait_ge(*w_split.at(L, CHUNK_OF[d] + 3))
                    elif i == 0:
                        pe.wait_ge(*(y_ready.at(L, n // 2 + 1) if n % 2 == 0 else at_o.at(L, (n // 2 + 1) * NT)))
                    if name == "out" and i == 0:
                        pe.wait_ge(*m_split.at(L, KT))
                    if d >= 4:
                        taker = DENSE[d - 4][3]
                        pe.wait_ge(*{"act": act_took, "dve": dve_took}[taker].at(L, TAKEN_BY[taker][d - 4]))

                def dense(place_):
                    for s_ in range(step[0], REACH[place_]):
                        d = sum(e <= s_ for e in END)
                        name, i, kind, _ = DENSE[d]
                        k = s_ - (END[d - 1] if d else 0)
                        if k == 0:
                            begin(d)
                        o_ = ps[(BANK0 + d) % 4]
                        if kind == "tm":
                            tt, first_k = k // 2, k % 2 * (KT // 2)
                            for k_ in range(first_k, first_k + KT // 2):
                                ins = product3(o_[:, tt * P:(tt + 1) * P], [h[:, k_, tt * P:(tt + 1) * P] for h in hn],
                                               weights(CHUNK_OF[d], 0, k_), k_ == 0, k_ == KT - 1)
                        elif name.startswith("branch"):
                            ins = product3(o_[:, :], weights(CHUNK_OF[d], CH, k), [v[:, int(name[-1]) % 2, k, :] for v in y],
                                           k == 0, k == FT - 1)
                        else:
                            ins = product3(o_[:, :], weights(CHUNK_OF[d], 0, k),
                                           [v[:, k, :] for v in (u if name == "out" else hn)], k == 0, k == KT - 1)
                        if s_ + 1 == END[d]:
                            ins.then_inc(*dense_done.up())
                            if name == "out" and i:
                                norm_sum(1, i - 1)
                    step[0] = REACH[place_]

                def norm_sum(j, m):
                    pe.wait_ge(*squared.at(L, j * KT + m + 1))
                    mm(ps[4][:, :], C("ones"), tmp[:, m % 2, :], start=m == 0, stop=m == KT - 1).then_inc(*sumsq.up())

                def norm_sums(j):
                    for m in range(KT):
                        norm_sum(j, m)

                def attention(which, q, k, v, pt):
                    base = 16 * which

                    def logits(i):
                        b, h = divmod(i, H)
                        lo = (h % 2) * HD
                        n = (b + 1) * P
                        if i >= 2:
                            pe.wait_ge(*at_mx.at(L, base + i - 1))
                        last = which == 0
                        ins = mm(ps[4 + i % 2][:, 0:n], q[lo:lo + HD, h // 2, b * P:(b + 1) * P],
                                 k[lo:lo + HD, h // 2, 0:n], start=True, stop=last)
                        if not last:
                            ins = mm(ps[4 + i % 2][:, b * P:n], C("ident"), C("cneg"), start=False, stop=True)
                        ins.then_inc(*at_lg.up())
                    logits(0)
                    for i in range(16):
                        b, h = divmod(i, H)
                        if i + 1 < 16:
                            logits(i + 1)
                        dense(("bd"[which] + "_att", i, 0))
                        pe.wait_ge(*at_p.at(L, base + i + 1))
                        if i:
                            pe.wait_ge(*at_pt.at(L, base + i))
                        for j in range(b + 1):
                            ins = pe.transpose(ps[6][:, j * P:(j + 1) * P], S(6 + i % 4 // 2, i % 2)[:, j * P:(j + 1) * P],
                                               C("ident"))
                        ins.then_inc(*at_tr.up())
                        dense(("bd"[which] + "_att", i, 1))
                        pe.wait_ge(*at_pt.at(L, base + i + 1))
                        if h == 0 and (b or which):
                            pe.wait_ge(*at_o.at(L, which * NT + b))
                        lo = (h % 2) * HD
                        for j in range(b + 1):
                            ins = mm(ps[7][lo:lo + HD, (h // 2) * P:(h // 2 + 1) * P], v[:, j, h * HD:(h + 1) * HD],
                                     S(pt + i % 4 // 2, i % 2)[:, j * P:(j + 1) * P], start=j == 0, stop=j == b)
                        if h == H - 1:
                            ins.then_inc(*at_pv.up())

                norm_sums(0)
                pe.wait_ge(*h_ready.at(L, KT))
                pe.wait_ge(*par_loaded.at(L, 16))

                dense("A")
                E, k_ = S(5), S(1)
                for lv in range(8):
                    dense(("a_level", lv))
                    pe.wait_ge(*a_ops.at(L, lv + 1))
                    kk_, qq_ = (k_, S(0)) if lv == 0 else (E, E)
                    for b in range(4):
                        lo = (b % 2) * HD
                        if lv:
                            pe.wait_ge(*a_sc_used.at(L, (lv - 1) * NT + b + 1))
                        for i in range(4):
                            c, t = 2 * (b // 2) + i // 2, i % 2
                            ins = mm(ps[4 + b][:, i * P:(i + 1) * P], kk_[lo:lo + HD, t, c * P:(c + 1) * P],
                                     qq_[lo:lo + HD, t, c * P:(c + 1) * P], start=True, stop=True)
                        ins.then_inc(*a_sc.up())
                dense(("a_keys", 0))
                pe.wait_ge(*a_ops.at(L, 9))
                for c in range(NT):
                    if c == 0:
                        pe.wait_ge(*a_sc_used.at(L, 8 * NT))
                    else:
                        pe.wait_ge(*a_tr_used.at(L, c))
                    for t in range(FT):
                        ins = pe.transpose(ps[4][:, t * P:(t + 1) * P], S(5)[:, t, c * P:(c + 1) * P], C("ident"))
                    ins.then_inc(*a_tr.up())
                    dense(("a_keys", c + 1))
                AT = [slab[:, 16 + c // 2, (c % 2) * T:(c % 2 + 1) * T] for c in range(NT)]
                v_ = slab[:, 4, :].rearrange("p (c n) -> p c n", c=NT)
                kh_ = slab[:, 7, :].rearrange("p (c n) -> p c n", c=NT)
                for c in range(NT):
                    pe.wait_ge(*a_st.at(L, c + 1))
                    pe.wait_ge(*a_tr_used.at(L, c + 1))
                    if c:
                        pe.wait_ge(*a_o_used.at(L, c))
                    for h in range(H):
                        lo, t = (h % 2) * HD, h // 2
                        o_ = ps[5][lo:lo + HD, t * P:(t + 1) * P]
                        at_ = AT[2 * (c // 2) + h % 2][:, (c % 2 * 2 + t) * P:(c % 2 * 2 + t + 1) * P]
                        mm(o_, v_[:, c, h * HD:(h + 1) * HD], at_, start=True, stop=False)
                        ins = mm(o_, st[lo:lo + HD, t, :], S(6)[lo:lo + HD, t, c * P:(c + 1) * P], start=False, stop=True)
                    ins.then_inc(*a_o.up())
                    for h in range(H):
                        lo, t = (h % 2) * HD, h // 2
                        ins = mm(ps[6][lo:lo + HD, t * HD:(t + 1) * HD], kh_[:, c, h * HD:(h + 1) * HD],
                                 v_[:, c, h * HD:(h + 1) * HD], start=True, stop=True)
                    ins.then_inc(*a_su.up())
                    dense(("a_chunk", c))
                dense(("a_norm", 0))
                pe.wait_ge(*a_sq.at(L, 2))
                for t in range(FT):
                    mm(ps[4 + t][:, :], C("blk"), S(19, t), start=True, stop=True).then_inc(*a_ss.up())
                dense(("a_norm", 1))

                dense("B")
                pe.wait_ge(*y_ready.at(L, 1))
                pe.wait_ge(*act_took.at(L, TAKEN_BY["act"][INDEX[("bs", 0)]]))
                for tt in range(NT):
                    ins = pe.transpose(ps[7][:, tt * P:(tt + 1) * P], small[:, tt * P:(tt + 1) * P], C("ident"))
                ins.then_inc(*b_iwt.up())
                for r, (src, t, con_name) in enumerate(((8, 0, "roth"), (8, 1, "roth"), (9, 0, "roth"), (9, 1, "roth"),
                                                        (11, 0, "roti"), (11, 1, "roti"))):
                    if r >= 2:
                        pe.wait_ge(*b_rope.at(L, r - 1))
                    mm(ps[4 + r % 2][:, :], C(con_name), S(src, t), start=True, stop=True).then_inc(*b_rot.up())
                    dense(("b_rope", r))
                mm(ps[6][:, :], C("rep", 0, IDIM), small[0:IDIM, :], start=True, stop=True).then_inc(*b_rep.up())
                pe.wait_ge(*b_rope.at(L, 5))
                mm(ps[4][:, :], C("reprot", 0, IDIM), small[0:IDIM, :], start=True, stop=True).then_inc(*b_rot.up())
                dense(("b_rope", 6))
                pe.wait_ge(*b_rope.at(L, 7))
                n_ix = 0
                for b in range(1, NT):
                    for j in range(IH):
                        lo, t = (j % 4) * IDIM, j // 4
                        if n_ix >= 2:
                            pe.wait_ge(*b_relu.at(L, n_ix - 1))
                        mm(ps[4 + n_ix % 2][:, 0:(b + 1) * P], S(11)[lo:lo + IDIM, t, b * P:(b + 1) * P],
                           S(2, 1)[lo:lo + IDIM, 0:(b + 1) * P], start=True, stop=True).then_inc(*b_ix.up())
                        n_ix += 1
                        dense(("b_ix", n_ix - 1))
                pe.wait_ge(*b_relu.at(L, n_ix))
                pe.wait_ge(*b_iwc.at(L, 1))
                dense(("b_topk", TOPK // 8 - 1))
                attention(0, S(8), S(9), slab[:, 10, :].rearrange("p (c n) -> p c n", c=NT), 0)

                dense("C")
                pe.wait_ge(*at_o.at(L, NT))
                pe.wait_ge(*c_act.at(L, 1))
                i_ = 0
                for lo, hi in ((0, 32), (32, 64)):
                    for t in range(FT):
                        mm(ps[4 + i_ % 4][:, :], lora[lo:hi, t * P:(t + 1) * P], S(15, 0)[lo:hi, :], start=True, stop=True)\
                            .then_inc(*c_lw.up())
                        i_ += 1
                dense(("c_prep", 0))
                pe.wait_ge(*c_sg.at(L, 4))
                for t in range(FT):
                    ins = mm(ps[6][0:32, :], v1w[:, t, :], S(14, t), start=t == 0, stop=t == 1)
                ins.then_inc(*c_vh.up())
                dense(("c_prep", 1))
                pe.wait_ge(*c_vhc.at(L, 1))
                for t in range(FT):
                    mm(ps[4 + t][:, :], v2w[:, t * P:(t + 1) * P], S(11, 0)[0:32, :], start=True, stop=True)\
                        .then_inc(*c_vg.up())
                for t in range(FT):
                    pe.wait_ge(*c_sq.at(L, t + 1))
                    mm(ps[6 + t][:, :], C("blk"), S(5, t), start=True, stop=True).then_inc(*c_ss.up())
                dense(("c_prep", 2))
                for t in range(FT):
                    pe.wait_ge(*c_vgs.at(L, 2))
                    pe.wait_ge(*c_sq.at(L, 3 + t))
                    mm(ps[4 + t][:, :], C("blk"), S(0, t), start=True, stop=True).then_inc(*c_ss.up())
                dense(("c_prep", 3))
                pe.wait_ge(*c_til.at(L, 1))
                n_tr = 0
                for src in (8, 5, 14):
                    for half in range(2):
                        if n_tr >= 4:
                            pe.wait_ge(*c_tru.at(L, n_tr - 3))
                        for cc in range(2):
                            for t in range(FT):
                                ins = pe.transpose(ps[4 + n_tr % 4][:, cc * 256 + t * P:cc * 256 + (t + 1) * P],
                                                   S(src)[:, t, (2 * half + cc) * P:(2 * half + cc + 1) * P], C("ident"))
                        ins.then_inc(*c_tr.up())
                        n_tr += 1
                pe.wait_ge(*c_tru.at(L, 6))
                RT, AA, KK, BB = S(6), S(7), S(8), S(5)
                tm = [slab[:, i, :].rearrange("p (c n) -> p c n", c=NT) for i in (1, 2, 4)]
                LTm, MTm, RBm, RKm, X_, XT_, R_, *PPs = c_halves
                for c in range(NT):
                    cs = slice(c * P, (c + 1) * P)
                    for i, ops in enumerate((((BB, AA), (KK, AA)), ((BB, AA), (KK, AA)), ((BB, RT), (KK, RT)),
                                             ((BB, RT), (KK, RT)), ((AA, BB),), ((AA, BB),))):
                        lo = (i % 2) * HD
                        if i == 0 and c:
                            pe.wait_ge(*c_yu.at(L, c))
                            pe.wait_ge(*c_st.at(L, c + 1))
                        if i >= 4:
                            pe.wait_ge(*c_mu.at(L, 6 * c + i - 3))
                        for m, (a_, b_) in enumerate(ops):
                            for t in range(FT):
                                ins = mm(ps[4 + i % 4][:, (m * 2 + t) * P:(m * 2 + t + 1) * P], a_[lo:lo + HD, t, cs],
                                         b_[lo:lo + HD, t, cs], start=True, stop=True)
                        ins.then_inc(*c_m.up())
                    dense(("c_mask", c))
                    pe.wait_ge(*c_mu.at(L, 6 * c + 6))
                    pe.wait_ge(*c_x1.at(L, c + 1))
                    for lv in range(1, 7):
                        if lv > 1:
                            pe.wait_ge(*c_xxu.at(L, 11 * c + 2 * (lv - 1)))
                        for h in range(H):
                            hs = slice(h * P, (h + 1) * P)
                            ins = mm(ps[4][:, hs], LTm[:, hs], X_[:, hs], start=True, stop=True)
                        ins.then_inc(*c_pp.up())
                        dense(("c_level", c, lv, 0))
                        pe.wait_ge(*c_ppu.at(L, 6 * c + lv))
                        PP = PPs[lv % 2]
                        if lv < 6:
                            for h in range(H):
                                hs = slice(h * P, (h + 1) * P)
                                ins = mm(ps[5][:, hs], XT_[:, hs], PP[:, hs], start=True, stop=True)
                            ins.then_inc(*c_xx.up())
                        for h in range(H):
                            hs = slice(h * P, (h + 1) * P)
                            ins = mm(ps[6][:, hs], PP[:, hs], XT_[:, hs], start=True, stop=True)
                        ins.then_inc(*c_xx.up())
                        dense(("c_level", c, lv, 1))
                    pe.wait_ge(*c_st.at(L, c + 1))
                    for h in range(H):
                        lo, t, hs = (h % 2) * HD, h // 2, slice(h * HD, (h + 1) * HD)
                        o_ = ps[7 if h % 2 == 0 else 4][:, t * HD:(t + 1) * HD]
                        mm(o_, AA[lo:lo + HD, t, cs], st[lo:lo + HD, t, :], start=True, stop=False)
                        ins = mm(o_, MTm[:, h * P:(h + 1) * P], tm[2][:, c, hs], start=False, stop=True)
                    ins.then_inc(*c_b.up())
                    dense(("c_out", c, 0))
                    pe.wait_ge(*c_bu.at(L, c + 1))
                    pe.wait_ge(*c_xxu.at(L, 11 * c + 11))
                    for h in range(H):
                        hs = slice(h * HD, (h + 1) * HD)
                        ins = mm(ps[5][:, hs], XT_[:, h * P:(h + 1) * P], R_[:, hs], start=True, stop=True)
                    ins.then_inc(*c_u.up())
                    dense(("c_out", c, 1))
                    pe.wait_ge(*c_uu.at(L, c + 1))
                    pe.sem_inc(carrier, 1)
                    U_ = R_[:, 256:512]
                    for h in range(H):
                        lo, t, hs = (h % 2) * HD, h // 2, slice(h * HD, (h + 1) * HD)
                        o_ = ps[6][lo:lo + HD, t * P:(t + 1) * P]
                        mm(o_, st[lo:lo + HD, t, :], RT[lo:lo + HD, t, cs], start=True, stop=False)
                        mm(o_, U_[:, hs], RBm[:, h * P:(h + 1) * P], start=False, stop=False)
                        ins = mm(o_, tm[2][:, c, hs], RKm[:, h * P:(h + 1) * P], start=False, stop=True)
                    ins.then_inc(*c_y.up())
                    for h in range(H):
                        lo, t, hs = (h % 2) * HD, h // 2, slice(h * HD, (h + 1) * HD)
                        o_ = ps[7][lo:lo + HD, t * HD:(t + 1) * HD]
                        mm(o_, tm[1][:, c, hs], U_[:, hs], start=True, stop=False)
                        ins = mm(o_, tm[0][:, c, hs], tm[2][:, c, hs], start=False, stop=True)
                    ins.then_inc(*c_s.up())
                    dense(("c_out", c, 2))
                pe.wait_ge(*c_yu.at(L, NT))
                pe.wait_ge(*c_st.at(L, NT + 1))
                for t in range(FT):
                    mm(ps[4 + t][:, :], C("blk"), S(3, t), start=True, stop=True).then_inc(*c_mean.up())
                dense(("c_norm", 0))
                for t in range(FT):
                    pe.wait_ge(*c_csq.at(L, t + 1))
                    if t == 0:
                        pe.wait_ge(*c_st.at(L, NT + 1))
                    mm(ps[6 + t][:, :], C("blk"), S(5, t), start=True, stop=True).then_inc(*c_var.up())
                dense(("c_norm", 1))
                for t in range(FT):
                    pe.wait_ge(*c_cen.at(L, 1))
                    mm(ps[4 + t][:, :], lora[64:128, t * P:(t + 1) * P], S(15, 0)[64:128, :], start=True, stop=True)\
                        .then_inc(*c_g.up())

                dense("D")
                pe.wait_ge(*y_ready.at(L, 2))
                dense(("d_prep", 0))
                pe.wait_ge(*d_c.at(L, 1))
                for h in range(H):
                    mm(ps[4 + h][:, :], con[SM_F:SM_F + H, CC["sel"] + h:CC["sel"] + h + 1].to_broadcast([H, P]),
                       S(13, 1)[SM_F:SM_F + H, :], start=True, stop=True).then_inc(*d_bc.up())
                dense(("d_prep", 1))
                pe.wait_ge(*d_bcu.at(L, H))
                pe.wait_ge(*act_took.at(L, TAKEN_BY["act"][INDEX[("dv", 1)]]))
                attention(1, S(10), S(11), slab[:, 12, :].rearrange("p (c n) -> p c n", c=NT), 8)

                dense("rest")
                norm_sum(1, KT - 1)
                norm_sums(2)
                pe.wait_ge(*h_ready.at(L, 2 * KT))
                pe.sem_inc(carrier, 1)
                with pe.Fori(0, QUARTERS) as q:
                    for j in range(16):
                        up = j < 8
                        pe.wait_ge(*w_split.at(L, q * 16 + (MLP_CHUNK0 + j + 3)))
                        if j < 4:
                            pe.wait_ge(*dve_took.at(L, q * 8 + (DVE0 - 8 + j + 5)))
                        elif j < 12:
                            pe.wait_ge(*act_took.at(L, q * 8 + (ACT0 + j - 3)))
                        else:
                            pe.wait_ge(*dve_took.at(L, q * 8 + (DVE0 + j - 11)))
                        if j == 8:
                            pe.wait_ge(*u_ready.at(L, q * 8 + 12))
                        for k in range(KT):
                            ins = product3(ps[j % 4][:, :], weights(j, 0, k), [v[:, k, :] for v in (hn if up else u)],
                                           k == 0, k == KT - 1)
                        ins.then_inc(*dense_done.up(QUARTERS))
                norm_sums(3)

        @block.scalar
        def _(act):
            fn = act.activation

            def link(ins, sig=act_step):
                ins.then_inc(*sig.up())
                act.wait_ge(*sig.at(L, sig.count))

            act.wait_ge(once, ONCE)
            act.wait_ge(x_loaded, 16)
            act.wait_ge(cleared, 1)
            with act.Fori(0, LAYERS) as L:
                def hi_part(c):
                    act.wait_ge(w_arrived[c % 2], L * (8 * CHUNKS) + 16 * (c // 2 + 1))
                    if c >= 2:
                        act.wait_ge(*dense_done.at(L, LAST_OF_CHUNK[c - 2] + 1))
                    size = CHM if DENSE[LAST_OF_CHUNK[c]][0].startswith("branch") else CH
                    fn(wsp[0][:, c % 2, 0:size], wsl[:, c % 2, 0:size], ACT.Copy).then_inc(*w_hi_done.up())

                def copy(o_, scale=1.0):
                    return lambda b_: fn(o_, b_, ACT.Copy, scale=scale)

                def tokens(slab_i, i):
                    return lambda b_: fn(slab[:, slab_i, :].rearrange("p (c n) -> p c n", c=NT)[:, :, i * P:(i + 1) * P],
                                         b_.rearrange("p (c n) -> p c n", c=NT), ACT.Copy)

                def forget(i):
                    def go(b_):
                        fn(S(2, i), b_, ACT.Sigmoid)
                        return fn(S(1, i), b_, ACT.Sigmoid, scale=-1.0)
                    return go

                def out_gate(i):
                    def go(b_):
                        fn(S(3, i), b_, ACT.Copy)
                        return fn(S(19, i), b_, ACT.Sigmoid)
                    return go

                to_sbuf = {"aq": lambda i: copy(S(0, i), HD ** -0.5), "af": forget, "ai": lambda i: tokens(4, i),
                           "ag": out_gate, "bs": lambda i: copy(small[:, :]), "bq": lambda i: copy(S(8, i)),
                           "bk": lambda i: copy(S(9, i)), "biq": lambda i: copy(S(11, i)), "bv": lambda i: tokens(10, i),
                           "cr": lambda i: copy(S(12, i)), "ck": lambda i: copy(S(13, i)), "cv": lambda i: copy(S(14, i)),
                           "cl": lambda i: copy(S(15, 0)), "dq": lambda i: copy(S(10, i)), "dk": lambda i: copy(S(11, i)),
                           "dv": lambda i: tokens(12, i)}
                place = [0]

                def take(place_):
                    while place[0] < MLP0:
                        d = place[0]
                        name, i, _, _ = DENSE[d]
                        gate = name.startswith("gate")
                        if END[d + gate] > TAKEN_TO[place_]:
                            break
                        act.wait_ge(*dense_done.at(L, d + 1))
                        b_ = ps[(BANK0 + d) % 4][:, :]
                        if gate:
                            g_ = TAKEN_BY["dve"][d + 1]
                            if g_ > 2:
                                act.wait_ge(*product.at(L, g_ - 2))
                            ins = fn(tmp[:, g_ % 2, :], b_, ACT.Sigmoid)
                        elif name == "out":
                            if i >= 2:
                                act.wait_ge(*sumsq.at(L, KT + i - 1))
                            else:
                                act.wait_ge(*product.at(L, 4 * KT))
                            fn(tmp[:, i % 2, :], b_, ACT.Square).then_inc(*squared.up())
                            ins = fn(mix[:, i, :], b_, ACT.Copy)
                        else:
                            ins = to_sbuf[name](i)(b_)
                        ins.then_inc(*act_took.up())
                        if gate:
                            act.wait_ge(*dense_done.at(L, d + 2))
                        if CHUNK_OF[d] + 2 < MLP_CHUNK0:
                            hi_part(CHUNK_OF[d] + 2)
                        place[0] = d + 1 + gate

                def norm_hi(j):
                    for m in range(KT):
                        act.wait_ge(*h_raw.at(L, j * KT + m + 1))
                        fn(hn[0][:, m, :], tmp[:, 2 + m % 2, :], ACT.Copy).then_inc(*h_hi.up())

                def norm_rstd(j):
                    act.wait_ge(*var_ready.at(L, j + 1))
                    link(fn(rstd[:, 1, :], rstd[:, 0, :], ACT.Ln))
                    fn(rstd[:, 1, :], rstd[:, 1, :], ACT.Exp, scale=-0.5).then_inc(*rstd_done.up())

                def attention(which, pt):
                    base = 16 * which

                    def transposed(i):
                        b = i // H
                        act.wait_ge(*at_tr.at(L, base + i + 1))
                        fn(S(pt + i % 4 // 2, i % 2)[:, 0:(b + 1) * P], ps[6][:, 0:(b + 1) * P], ACT.Copy)\
                            .then_inc(*at_pt.up())
                        take(("bd"[which] + "_att", i, 1))
                    for i in range(16):
                        b, h = divmod(i, H)
                        n = (b + 1) * P
                        buf = S(6 + i % 4 // 2, i % 2)
                        act.wait_ge(*at_mx.at(L, base + i + 1))
                        fn(buf[:, 0:n], buf[:, 0:n], ACT.Exp, bias=col[:, 1, i % 4:i % 4 + 1],
                           accum_out=col[:, 2, i % 4:i % 4 + 1]).then_inc(*at_ex.up())
                        if i:
                            transposed(i - 1)
                        if i and i % H == 0:
                            attn_out(which, i // H - 1)
                    transposed(15)
                    attn_out(which, NT - 1)

                def attn_out(which, b):
                    act.wait_ge(*at_pv.at(L, which * NT + b + 1))
                    if b == 0 and which:
                        act.wait_ge(*dense_done.at(L, INDEX[("branch1", KT - 1)] + 1))
                    fn(y[0][:, 1, :, b * P:(b + 1) * P], ps[7][:, 0:256].rearrange("p (t n) -> p t n", t=FT), ACT.Copy)\
                        .then_inc(*y_hi.up())

                act.wait_ge(*x_tiles.at(L, 1))
                act.dma_start(par[:, :], par_in[bass.ds(L, 1)].rearrange("a p n -> (a p) n")).then_inc(par_loaded.handle, 16)
                par_loaded.count += 16
                hi_part(0)
                hi_part(1)
                for m in range(KT):
                    if m >= 2:
                        act.wait_ge(*sumsq.at(L, m - 1))
                    fn(tmp[:, m % 2, :], x[:, m, :], ACT.Square).then_inc(*squared.up())
                norm_rstd(0)
                norm_hi(0)

                act.wait_ge(*lb_in.at(L, 1))
                fn(col[:, 7, 0:4], col[:, 6, 0:4], ACT.Exp).then_inc(*lb_exp.up())
                take("A")
                act.wait_ge(*a_prep.at(L, 1))
                fn(S(2), S(2), ACT.Ln).then_inc(*a_ln.up())
                E = slab[:, 5, :]
                take(("a_level", 0))
                for lv in range(1, 8):
                    act.wait_ge(*a_diff.at(L, lv))
                    fn(E, E, ACT.Exp).then_inc(*a_exp.up())
                    take(("a_level", lv))
                act.wait_ge(*a_diff.at(L, 8))
                fn(slab[:, 6, :], slab[:, 2, :], ACT.Exp).then_inc(*a_exp.up())
                fn(slab[:, 5, :], slab[:, 5, :], ACT.Exp).then_inc(*a_exp.up())
                kh_ = slab[:, 7, :].rearrange("p (c n) -> p c n", c=NT)
                for c in range(NT):
                    act.wait_ge(*a_tr.at(L, c + 1))
                    fn(kh_[:, c, :], ps[4][:, 0:256], ACT.Copy).then_inc(*a_tr_used.up())
                    take(("a_keys", c + 1))
                for c in range(NT):
                    act.wait_ge(*a_o.at(L, c + 1))
                    fn(S(18)[:, :, c * P:(c + 1) * P], ps[5][:, 0:256].rearrange("p (t n) -> p t n", t=FT), ACT.Copy)\
                        .then_inc(*a_o_used.up())
                    take(("a_chunk", c))
                act.wait_ge(*a_o_used.at(L, NT))
                for t in range(FT):
                    fn(S(19, t), S(18, t), ACT.Square).then_inc(*a_sq.up())
                take(("a_norm", 0))
                act.wait_ge(*a_var.at(L, 1))
                link(fn(slab[:, 0, :], slab[:, 0, :], ACT.Ln))
                fn(slab[:, 0, :], slab[:, 0, :], ACT.Exp, scale=-0.5).then_inc(*a_r.up())

                take("B")
                act.wait_ge(*y_ready.at(L, 1))
                act.dma_start(slab[:, 0:2, :].rearrange("p a n -> p (a n)"), rope_in).then_inc(rope_in_.handle, 16)
                rope_in_.count += 16
                take(("b_rope", 0))
                act.wait_ge(*b_iwt.at(L, 1))
                fn(iw[:, :, :], ps[7][:, :].rearrange("p (t n) -> p t n", t=NT)[:, :, SM_IW:SM_IW + IH], ACT.Copy,
                   scale=1.0 / 16.0).then_inc(*b_iwc.up())
                for r in range(1, 7):
                    take(("b_rope", r))
                n_ix = 0
                for b in range(1, NT):
                    for j in range(IH):
                        n = (b + 1) * P
                        act.wait_ge(*b_ix.at(L, n_ix + 1))
                        if n_ix >= 2:
                            act.wait_ge(*b_acc.at(L, n_ix - 1))
                        fn(S(3, n_ix % 2)[:, 0:n], ps[4 + n_ix % 2][:, 0:n], ACT.Relu).then_inc(*b_relu.up())
                        n_ix += 1
                        take(("b_ix", n_ix - 1))
                take(("b_topk", TOPK // 8 - 1))
                attention(0, 0)

                take("C")
                act.wait_ge(*c_mix.at(L, 1))
                fn(S(15, 0)[0:32, :], S(15, 0)[0:32, :], ACT.Tanh)
                fn(S(15, 0)[64:128, :], S(15, 0)[64:128, :], ACT.Sigmoid).then_inc(*c_act.up())
                for i_ in range(4):
                    t = i_ % 2
                    act.wait_ge(*c_lw.at(L, i_ + 1))
                    if i_ < 2:
                        ins = fn(S(2, t), ps[4 + i_ % 4][:, :], ACT.Sigmoid, bias=pcol("w0", t))
                    else:
                        ins = fn(S(3, t), ps[4 + i_ % 4][:, :], ACT.Sigmoid, bias=pcol("a0", t))
                    ins.then_inc(*c_sg.up())
                take(("c_prep", 0))
                act.wait_ge(*c_vh.at(L, 1))
                fn(S(11, 0)[0:32, :], ps[6][0:32, :], ACT.Copy).then_inc(*c_vhc.up())
                take(("c_prep", 1))
                for t in range(FT):
                    act.wait_ge(*c_vg.at(L, t + 1))
                    fn(S(6, t), ps[4 + t][:, :], ACT.Sigmoid, bias=pcol("v0", t)).then_inc(*c_vgs.up())
                take(("c_prep", 2))
                act.wait_ge(*c_kkv.at(L, 1))
                link(fn(slab[:, 5, :], slab[:, 5, :], ACT.Ln))
                fn(slab[:, 5, :], slab[:, 5, :], ACT.Exp, scale=-0.5).then_inc(*c_kkr.up())
                act.wait_ge(*c_ex.at(L, 1))
                fn(slab[:, 6, :], slab[:, 1, :], ACT.Exp)
                fn(slab[:, 8, :], slab[:, 1, :], ACT.Exp, scale=-1.0)
                fn(slab[:, 7, :], slab[:, 2, :], ACT.Exp)
                fn(col[:, 3, :], col[:, 4, :], ACT.Exp).then_inc(*c_exd.up())
                take(("c_prep", 3))
                tmf = [slab[:, i, :] for i in (1, 2, 4)]
                for n_tr in range(6):
                    act.wait_ge(*c_tr.at(L, n_tr + 1))
                    fn(tmf[n_tr // 2][:, (n_tr % 2) * T:(n_tr % 2 + 1) * T], ps[4 + n_tr % 4][:, :], ACT.Copy)\
                        .then_inc(*c_tru.up())
                X_, XT_, R_ = c_halves[4:7]
                for c in range(NT):
                    take(("c_mask", c))
                    for k_ in range(11):
                        act.wait_ge(*c_xx.at(L, 11 * c + k_ + 1))
                        tgt, bk = (X_, 5) if k_ % 2 == 0 and k_ < 10 else (XT_, 6)
                        fn(tgt, ps[bk][:, :], ACT.Copy).then_inc(*c_xxu.up())
                        if k_ % 2 or k_ == 10:
                            take(("c_level", c, k_ // 2 + 1, 1))
                    act.wait_ge(*c_b.at(L, c + 1))
                    rhs_ = R_[:, 0:256].rearrange("p (t two v) -> p t two v", two=2, v=HD)
                    fn(rhs_[:, :, 0, :], ps[7][:, 0:P].rearrange("p (t v) -> p t v", v=HD), ACT.Copy)
                    fn(rhs_[:, :, 1, :], ps[4][:, 0:P].rearrange("p (t v) -> p t v", v=HD), ACT.Copy).then_inc(*c_bu.up())
                    take(("c_out", c, 0))
                    act.wait_ge(*c_u.at(L, c + 1))
                    fn(R_[:, 256:512], ps[5][:, 0:256], ACT.Copy).then_inc(*c_uu.up())
                    take(("c_out", c, 1))
                    act.wait_ge(*c_y.at(L, c + 1))
                    fn(S(3)[:, :, c * P:(c + 1) * P], ps[6][:, 0:256].rearrange("p (t n) -> p t n", t=FT), ACT.Copy)\
                        .then_inc(*c_yu.up())
                    take(("c_out", c, 2))
                take(("c_norm", 0))
                act.wait_ge(*c_cen.at(L, 1))
                for t in range(FT):
                    fn(S(5, t), S(3, t), ACT.Square).then_inc(*c_csq.up())
                take(("c_norm", 1))
                act.wait_ge(*c_vv.at(L, 1))
                link(fn(slab[:, 5, :], slab[:, 5, :], ACT.Ln))
                fn(slab[:, 5, :], slab[:, 5, :], ACT.Exp, scale=-0.5).then_inc(*c_rr.up())

                take("D")
                act.wait_ge(*d_abs.at(L, 1))
                s5 = S(13, 0)[SM_F:SM_F + H, :]
                link(fn(s5, s5, ACT.Exp, scale=-1.0))
                fn(s5, s5, ACT.Ln, bias=C("ones", SM_F, SM_F + H, 1)).then_inc(*d_ln.up())
                take(("d_prep", 0))
                for h in range(H):
                    act.wait_ge(*d_bc.at(L, h + 1))
                    fn(S(14 + h // 2, h % 2), ps[4 + h][:, :], ACT.Copy).then_inc(*d_bcu.up())
                take(("d_prep", 1))
                attention(1, 8)

                take("rest")
                norm_rstd(1)
                for m in range(KT):
                    act.wait_ge(*x_tiles.at(L, 1 + m + 1))
                    if m >= 2:
                        act.wait_ge(*sumsq.at(L, 2 * KT + m - 1))
                    fn(tmp[:, m % 2, :], x[:, m, :], ACT.Square).then_inc(*squared.up())
                norm_rstd(2)
                norm_hi(1)
                with act.Fori(0, QUARTERS) as q:
                    for j in range(16):
                        c = MLP_CHUNK0 + j
                        act.wait_ge(w_arrived[c % 2], L * (8 * CHUNKS) + q * 128 + 16 * (c // 2 + 1))
                        act.wait_ge(*dense_done.at(L, q * 16 + (MLP0 + j - 1)))
                        fn(wsp[0][:, j % 2, 0:CH], wsl[:, j % 2, 0:CH], ACT.Copy).then_inc(*w_hi_done.up(QUARTERS))
                        if 2 <= j < 10:
                            m = j - 2
                            act.wait_ge(*u_ready.at(L, q * KT + m + 1))
                            fn(tmp[:, m % 4, :], ps[m % 4][:, :], ACT.Relu).then_inc(*act_took.up(QUARTERS))
                for m in range(KT):
                    act.wait_ge(*dve_took.at(L, DVE0 + 8 * 3 + m + 1))
                    if m >= 2:
                        act.wait_ge(*sumsq.at(L, 3 * KT + m - 1))
                    fn(tmp[:, m % 2, :], acc[:, m, :], ACT.Square).then_inc(*squared.up())
                norm_rstd(3)

        @block.gpsimd
        def _(pool):
            pool.memset(v1st[:, :, :], 0.0).then_inc(cleared, 1)
            pool.wait_ge(once, ONCE)
            pool.sem_inc(w_split.handle, 2)
            with pool.Fori(0, LAYERS) as L:
                def carry_wait():
                    pool.sem_inc(carrier, 1)

                def lo_part(c):
                    pool.wait_ge(*w_hi_done.at(L, c + 1))
                    size = CHM if DENSE[LAST_OF_CHUNK[c]][0].startswith("branch") else CH
                    raw, (hi, lo) = wsl[:, c % 2, 0:size], (w[:, c % 2, 0:size] for w in wsp)
                    pool.tensor_tensor(lo, raw, hi.bitcast(f32), SUB).then_inc(*w_split.up())

                for c in range(MLP_CHUNK0):
                    lo_part(c)
                    for d in range(MLP0):
                        if DENSE[d][0].startswith("branch") and CHUNK_OF[d] == c - 2:
                            i_ = TAKEN_BY["dve"][d] - 1
                            pool.wait_ge(*product.at(L, i_ + 1))
                            m = DENSE[d][1]
                            if DENSE[d][0] == "branch0":
                                carry_wait()
                                pool.tensor_copy(acc[:, m, :], tmp[:, 2 + i_ % 2, :]).then_inc(*merged.up())
                            else:
                                pool.tensor_tensor(acc[:, m, :], acc[:, m, :], tmp[:, 2 + i_ % 2, :], ADD)\
                                    .then_inc(*merged.up())
                pool.wait_ge(*m_split.at(L, KT))
                carry_wait()
                pool.memset(acc[:, :, :], 0.0).then_inc(*acc0.up())
                pool.wait_ge(*acc0.at(L, 1))
                for _ in range(4):
                    pool.sem_inc(*u_ready.up())
                with pool.Fori(0, QUARTERS) as q:
                    for j in range(16):
                        pool.wait_ge(*w_hi_done.at(L, q * 16 + (MLP_CHUNK0 + j + 1)))
                        pool.tensor_tensor(wsp[1][:, j % 2, 0:CH], wsl[:, j % 2, 0:CH], wsp[0][:, j % 2, 0:CH].bitcast(f32), SUB)\
                            .then_inc(*w_split.up(QUARTERS))

        @block.vector
        def _(dve):
            tt, ts, stt = dve.tensor_tensor, dve.tensor_scalar, dve.scalar_tensor_tensor

            def link(ins, sig=dve_step):
                ins.then_inc(*sig.up())
                dve.wait_ge(*sig.at(L, sig.count))

            dve.wait_ge(once, ONCE)
            dve.wait_ge(x_loaded, 16)
            dve.wait_ge(cleared, 1)
            NM = 2 * len(LEVELS) * P
            dve.tensor_copy(msk[:, :], slab[:, 0:2, :].rearrange("p a n -> p (a n)")[:, 0:NM]).then_inc(masks_ready, 1)
            dve.wait_ge(masks_ready, 1)
            dve.sem_inc(x_tiles.handle, 1)
            with dve.Fori(0, LAYERS) as L:
                def carry_wait():
                    dve.sem_inc(carrier, 1)

                def norm_var(j):
                    dve.wait_ge(*sumsq.at(L, (j + 1) * KT))
                    ts(rstd[:, 0, :], ps[4][:, :], 1.0 / D, EPS, MUL, ADD).then_inc(*var_ready.up())
                    dve.wait_ge(*rstd_done.at(L, j + 1))

                def norm_h(j, gain):
                    norm_var(j)
                    for m in range(KT):
                        n_ = j // 2 * KT + m
                        if m >= 2:
                            dve.wait_ge(*h_ready.at(L, n_ - 1))
                        stt(tmp[:, 2 + m % 2, :], x[:, m, :], pcol(gain, m), rstd[:, 1, :], MUL, MUL).then_inc(*h_raw.up())
                        if m:
                            norm_lo(n_ - 1)
                    norm_lo(n_)

                def norm_lo(n_):
                    m = n_ % KT
                    dve.wait_ge(*h_hi.at(L, n_ + 1))
                    tt(hn[1][:, m, :], tmp[:, 2 + m % 2, :], hn[0][:, m, :].bitcast(f32), SUB).then_inc(*h_ready.up())

                def residual(j, src, gain):
                    norm_var(j)
                    for m in range(KT):
                        link(stt(src[:, m, :], src[:, m, :], pcol(gain, m), rstd[:, 1, :], MUL, MUL))
                        tt(x[:, m, :], x[:, m, :], src[:, m, :], ADD).then_inc(*x_tiles.up())

                def split(src, hi, lo, sig):
                    link(dve.tensor_copy(hi, src))
                    tt(lo, src, hi.bitcast(f32), SUB).then_inc(*sig.up())

                place = [0]

                def gated(place_):
                    while place[0] < MLP0 and END[place[0]] <= GATED_TO[place_]:
                        d = place[0]
                        if DENSE[d][3] == "dve":
                            g_ = TAKEN_BY["dve"][d]
                            dve.wait_ge(*dense_done.at(L, d + 1))
                            dve.wait_ge(*act_took.at(L, TAKEN_BY["act"][d]))
                            if g_ > 2:
                                dve.wait_ge(*merged.at(L, g_ - 2))
                            tt(tmp[:, 2 + (g_ - 1) % 2, :], ps[(BANK0 + d) % 4][:, :], tmp[:, g_ % 2, :], MUL)\
                                .then_inc(*product.up())
                        place[0] += 1

                def blocks(ap, n):
                    return ap.rearrange("p (b two n) -> p b two n", two=2, n=n)

                dve.wait_ge(*par_loaded.at(L, 16))
                norm_h(0, "pre")

                lb0, lb1 = par[:, PC["lb0"]:PC["lb0"] + FT], par[:, PC["lb1"]:PC["lb1"] + FT]
                link(tt(col[:, 5, 0:2], lb1, lb0, ALU.max))
                tt(col[:, 6, 0:2], lb0, col[:, 5, 0:2], SUB)
                tt(col[:, 6, 2:4], lb1, col[:, 5, 0:2], SUB).then_inc(*lb_in.up())
                dve.wait_ge(*lb_exp.at(L, 1))
                link(tt(col[:, 5, 2:4], col[:, 7, 0:2], col[:, 7, 2:4], ADD))
                link(dve.reciprocal(col[:, 5, 4:6], col[:, 5, 2:4]))
                link(stt(lb[:, 0, :], col[:, 7, 2:4], pcol("flag"), col[:, 5, 4:6], MUL, MUL))
                link(ts(lb[:, 1, :], lb[:, 0, :], -1.0, 1.0, MUL, ADD))
                dve.wait_ge(*act_took.at(L, TAKEN_BY["act"][INDEX[("ag", 1)]]))
                for t in range(FT):
                    ins = ts(S(1, t), S(1, t), lb[:, 1, t:t + 1], None, MUL)
                ins.then_inc(*a_ops.up())
                for t in range(FT):
                    ins = ts(S(2, t), S(2, t), lb[:, 1, t:t + 1], lb[:, 0, t:t + 1], MUL, ADD)
                link(ins)
                ts(slab[:, 2, :], slab[:, 2, :], 2.0 ** -63, None, ALU.max).then_inc(*a_prep.up())
                tt(slab[:, 3, :], slab[:, 3, :], slab[:, 19, :], MUL)
                link(dve.memset(st[:, :, :], 0.0), a_st)
                dve.wait_ge(*a_ln.at(L, 1))
                for t in range(FT):
                    carry_wait()
                    link(dve.tensor_tensor_scan(S(2, t), con[:, CC["seg"]:CC["seg"] + T], S(2, t), 0.0, MUL, ADD))
                b_, E, q_, k_ = (slab[:, i, :] for i in (2, 5, 0, 1))
                AT = [slab[:, 16 + c // 2, (c % 2) * T:(c % 2 + 1) * T] for c in range(NT)]

                def exponents(n):
                    bb, ee = blocks(b_, n), blocks(E, n)
                    nb = FT * T // (2 * n)
                    beta = bb[:, :, 0, n - 1:n].to_broadcast([P, nb, n])
                    tt(ee[:, :, 0, :], beta, bb[:, :, 0, :], SUB)
                    tt(ee[:, :, 1, :], bb[:, :, 1, :], beta, SUB).then_inc(*a_diff.up())

                for lv in range(8):
                    if lv < 7:
                        n = LEVELS[lv]
                    for c in range(NT):
                        dve.wait_ge(*a_sc.at(L, lv * NT + c + 1))
                        if lv == 0:
                            tt(heads(AT[c]), heads(ps[4 + c][:, :]), over_heads(C("ident")), MUL).then_inc(*a_sc_used.up())
                        else:
                            carry_wait()
                            dve.copy_predicated(heads(AT[c]), level(0, lv - 1), heads(ps[4 + c][:, :]))\
                                .then_inc(*a_sc_used.up())
                    if lv < 7:
                        exponents(n)
                        dve.wait_ge(*a_exp.at(L, lv + 1))
                        ee = blocks(E, n)
                        tt(ee[:, :, 0, :], ee[:, :, 0, :], blocks(k_, n)[:, :, 0, :], MUL)
                        tt(ee[:, :, 1, :], ee[:, :, 1, :], blocks(q_, n)[:, :, 1, :], MUL).then_inc(*a_ops.up())
                bc = b_.rearrange("p (b n) -> p b n", n=P)
                tt(slab[:, 5, :].rearrange("p (b n) -> p b n", n=P), bc[:, :, P - 1:P].to_broadcast([P, FT * NT, P]), bc, SUB)\
                    .then_inc(*a_diff.up())
                dve.wait_ge(*a_exp.at(L, 9))
                link(dve.tensor_copy(col[:, 3, :], slab[:, 6, :].rearrange("p (b n) -> p b n", n=P)[:, :, P - 1]))
                tt(slab[:, 6, :], slab[:, 6, :], q_, MUL)
                tt(slab[:, 5, :], slab[:, 5, :], k_, MUL).then_inc(*a_ops.up())
                for c in range(NT):
                    dve.wait_ge(*a_su.at(L, c + 1))
                    for t in range(FT):
                        ins = stt(st[:, t, :], st[:, t, :], col[:, 3, t * NT + c:t * NT + c + 1],
                                  ps[6][:, t * HD:(t + 1) * HD], MUL, ADD)
                    link(ins, a_st)
                dve.wait_ge(*a_ss.at(L, 2))
                for t in range(FT):
                    ins = ts(S(0, t), ps[4 + t][:, :], 1.0 / HD, EPS, MUL, ADD)
                ins.then_inc(*a_var.up())
                dve.wait_ge(*a_r.at(L, 1))
                link(tt(slab[:, 18, :], slab[:, 18, :], slab[:, 0, :], MUL))
                link(stt(slab[:, 18, :], slab[:, 18, :], pcol("hgw"), slab[:, 3, :], MUL, MUL))
                split(S(18), y[0][:, 0, :, :], y[1][:, 0, :, :], y_ready)

                gated("B")
                dve.wait_ge(*act_took.at(L, TAKEN_BY["act"][INDEX[("bv", 1)]]))
                dve.wait_ge(*rope_in_.at(L, 16))
                r_ = 0
                for src, cs in ((S(8), 0), (S(9), 0), (S(11), 1)):
                    for t in range(FT):
                        dve.wait_ge(*b_rot.at(L, r_ + 1))
                        link(tt(S(2, 0), ps[4 + r_ % 2][:, :], S(cs, 1), MUL))
                        link(tt(src[:, t, :], src[:, t, :], S(cs, 0), MUL))
                        link(tt(src[:, t, :], src[:, t, :], S(2, 0), ADD), b_rope)
                        gated(("b_rope", r_))
                        r_ += 1
                dve.wait_ge(*b_rep.at(L, 1))
                dve.wait_ge(*b_rot.at(L, 7))
                link(tt(S(2, 0), ps[4][:, :], S(1, 1), MUL))
                link(tt(S(2, 1), ps[6][:, :], S(1, 0), MUL))
                link(tt(S(2, 1), S(2, 1), S(2, 0), ADD), b_rope)
                dve.wait_ge(*b_iwc.at(L, 1))

                def scores(b):
                    return S(4 + (b - 1) // 2, (b - 1) % 2)[:, 0:(b + 1) * P]

                n_ix = 0
                for b in range(1, NT):
                    n = (b + 1) * P
                    sc = scores(b)
                    for j in range(IH):
                        dve.wait_ge(*b_relu.at(L, n_ix + 1))
                        r9 = S(3, n_ix % 2)[:, 0:n]
                        if j == 0:
                            ins = ts(sc, r9, iw[:, b, j:j + 1], None, MUL)
                        else:
                            ins = stt(sc, r9, iw[:, b, j:j + 1], sc, MUL, ADD)
                        link(ins, b_acc)
                        n_ix += 1
                        gated(("b_ix", n_ix - 1))
                    link(tt(sc[:, b * P:n], sc[:, b * P:n], C("cneg"), ADD))
                for r in range(TOPK // 8):
                    for b in range(1, NT):
                        n = (b + 1) * P
                        sc = scores(b)
                        carry_wait()
                        ins = dve.max(col[:, b, :], sc)
                    link(ins)
                    carry_wait()
                    for b in range(1, NT):
                        n = (b + 1) * P
                        sc = scores(b)
                        ins = dve.match_replace(sc, col[:, b, :], sc, TAKEN)
                    link(ins)
                    gated(("b_topk", r))
                for b in range(1, NT):
                    n = (b + 1) * P
                    sc = scores(b)
                    ins = ts(sc, sc, -2e38, NEG, ALU.is_gt, MUL)
                link(ins)

                def softmax(which, bias):
                    base = 16 * which

                    def out_lo(b):
                        dve.wait_ge(*y_hi.at(L, which * NT + b + 1))
                        tb = slice(b * P, (b + 1) * P)
                        tt(y[1][:, 1, :, tb], ps[7][:, 0:256].rearrange("p (t n) -> p t n", t=FT),
                           y[0][:, 1, :, tb].bitcast(f32), SUB).then_inc(*at_o.up())

                    def probs(i):
                        n = (i // H + 1) * P
                        buf = S(6 + i % 4 // 2, i % 2)[:, 0:n]
                        dve.wait_ge(*at_ex.at(L, base + i + 1))
                        link(dve.reciprocal(col[:, 6, i % 4:i % 4 + 1], col[:, 2, i % 4:i % 4 + 1]))
                        ts(buf, buf, col[:, 6, i % 4:i % 4 + 1], None, MUL).then_inc(*at_p.up())

                    for i in range(16):
                        b, h = divmod(i, H)
                        n = (b + 1) * P
                        buf = S(6 + i % 4 // 2, i % 2)[:, 0:n]
                        dve.wait_ge(*at_lg.at(L, base + i + 1))
                        if i >= 4:
                            dve.wait_ge(*at_tr.at(L, base + i - 3))
                        carry_wait()
                        link(dve.tensor_tensor_reduce(out=buf, in0=ps[4 + i % 2][:, 0:n], in1=bias(b, h, n), scale=HD ** -0.5,
                                                      scalar=-3e38, op0=ADD, op1=ALU.max, accum_out=col[:, 0, i % 4:i % 4 + 1]))
                        ts(col[:, 1, i % 4:i % 4 + 1], col[:, 0, i % 4:i % 4 + 1], -1.0, None, MUL).then_inc(*at_mx.up())
                        if i:
                            probs(i - 1)
                            gated(("bd"[which] + "_att", i - 1, 1))
                        if i % H == 1 and i > 1:
                            out_lo(i // H - 1)
                    probs(15)
                    gated(("bd"[which] + "_att", 15, 1))
                    out_lo(NT - 1)

                softmax(0, lambda b, h, n: C("cneg") if b == 0 else scores(b))

                gated("C")
                dve.wait_ge(*act_took.at(L, TAKEN_BY["act"][INDEX[("cl", 0)]]))
                for i, (s_, n_) in enumerate(((12, 2), (13, 2), (14, 2), (15, 1))):
                    src = S(s_)[:, 0:n_, :]
                    dd = S(0)[:, 0:n_, :]
                    tt(dd[:, :, 1:T], src[:, :, 0:T - 1], src[:, :, 1:T], SUB)
                    link(ts(dd[:, :, 0:1], src[:, :, 0:1], -1.0, None, MUL))
                    for t in range(n_):
                        ins = stt(src[:, t, :], dd[:, t, :], pcol("mu", 2 * i + t), src[:, t, :], MUL, ADD)
                    link(ins, c_mix if i == 3 else dve_step)
                for t in range(FT):
                    ins = ts(S(4, t), S(13, t), pcol("kk", t), None, MUL)
                link(ins)
                for t in range(FT):
                    tt(S(5, t), S(4, t), S(4, t), MUL).then_inc(*c_sq.up())
                gated(("c_prep", 0))
                dve.wait_ge(*c_sg.at(L, 4))
                link(ts(slab[:, 2, :], slab[:, 2, :], -float(np.exp(-0.5)), None, MUL))
                for t in range(FT):
                    carry_wait()
                    link(dve.tensor_tensor_scan(S(1, t), con[:, CC["seg"]:CC["seg"] + T], S(2, t), 0.0, MUL, ADD))
                link(ts(slab[:, 0, :], slab[:, 3, :], -1.0, None, ADD))
                for t in range(FT):
                    ins = ts(S(0, t), S(0, t), pcol("ka", t), 1.0, MUL, ADD)
                link(ins)
                link(tt(slab[:, 13, :], slab[:, 13, :], slab[:, 0, :], MUL))
                for t in range(FT):
                    stt(S(0, t), S(12, t), pcol("rk", t), S(13, t), MUL, MUL).then_inc(*c_sq.up())
                gated(("c_prep", 1))
                dve.wait_ge(*c_vgs.at(L, 2))
                link(tt(slab[:, 7, :], v1st[:, :, :].rearrange("p t n -> p (t n)"), slab[:, 14, :], SUB))
                link(stt(slab[:, 7, :], slab[:, 6, :], pcol("flag"), slab[:, 7, :], MUL, MUL))
                link(tt(slab[:, 14, :], slab[:, 14, :], slab[:, 7, :], ADD))
                dve.tensor_copy(v1st[:, :, :].rearrange("p t n -> p (t n)"), slab[:, 14, :])
                dve.wait_ge(*c_ss.at(L, 2))
                for t in range(FT):
                    ins = ts(S(5, t), ps[6 + t][:, :], 1e-24, None, ALU.max)
                ins.then_inc(*c_kkv.up())
                cc = slab[:, 1, :].rearrange("p (b n) -> p b n", n=P)
                mid = col[:, 0, :]
                end = col[:, 1, :]
                mid4 = mid.rearrange("p (t c) -> p t c", t=FT)
                fac4 = col[:, 4, :].rearrange("p (t c) -> p t c", t=FT)
                dve.tensor_copy(mid, cc[:, :, P // 2 - 1])
                link(dve.tensor_copy(end, cc[:, :, P - 1]))
                link(tt(cc, cc, mid[:, :, None].to_broadcast([P, FT * NT, P]), SUB))
                tt(slab[:, 2, :], slab[:, 1, :], slab[:, 2, :], SUB)
                link(tt(col[:, 4, :], end, mid, SUB))
                link(tt(fac4[:, :, 0:NT - 1], fac4[:, :, 0:NT - 1], mid4[:, :, 1:NT], ADD), c_ex)
                gated(("c_prep", 2))
                dve.wait_ge(*c_ss.at(L, 4))
                for t in range(FT):
                    tt(S(0, t), ps[4 + t][:, :], S(14, t), MUL)
                dve.wait_ge(*c_kkr.at(L, 1))
                dve.wait_ge(*c_exd.at(L, 1))
                link(tt(slab[:, 4, :], slab[:, 4, :], slab[:, 5, :], MUL))
                link(tt(slab[:, 3, :], slab[:, 3, :], slab[:, 4, :], MUL))
                tt(slab[:, 6, :], slab[:, 6, :], slab[:, 12, :], MUL)
                stt(slab[:, 7, :], slab[:, 7, :], -1.0, slab[:, 4, :], MUL, MUL)
                link(tt(slab[:, 5, :], slab[:, 8, :], slab[:, 3, :], MUL))
                link(tt(slab[:, 8, :], slab[:, 8, :], slab[:, 13, :], MUL), c_til)
                link(dve.memset(st[:, :, :], 0.0), c_st)
                gated(("c_prep", 3))
                LTm, MTm, RBm, RKm, X_, XT_, R_, *PPs = c_halves
                dve.wait_ge(*c_tru.at(L, 6))
                link(dve.tensor_copy(heads(PPs[1]), over_heads(C("ident"))))
                for c in range(NT):
                    def by_parity(ap, par):
                        return ap.rearrange("p (t two n) -> p t two n", two=2, n=P)[:, :, par, :]

                    gated(("c_mask", c))
                    dve.wait_ge(*c_m.at(L, 6 * c + 1))
                    dve.tensor_copy(heads(X_), over_heads(C("ident")))
                    link(dve.tensor_copy(heads(XT_), over_heads(C("ident"))))
                    for i in range(6):
                        dve.wait_ge(*c_m.at(L, 6 * c + i + 1))
                        if i < 4:
                            pair = c_pairs[i // 2].rearrange("p (m t two n) -> p m t two n", m=2, two=2, n=P)
                            mask = C("slt" if i < 2 else "sle")[:, None, None, :].to_broadcast([P, 2, FT, P])
                            ins = tt(pair[:, :, :, i % 2, :], ps[4 + i][:, :].rearrange("p (m t n) -> p m t n", m=2, n=P),
                                     mask, MUL)
                        else:
                            carry_wait()
                            m0 = len(LEVELS) * P
                            ins = dve.copy_predicated(by_parity(X_, i % 2), msk[:, m0:m0 + P][:, None, :].to_broadcast([P, FT, P]),
                                                      ps[i][:, 0:256].rearrange("p (t n) -> p t n", n=P))
                        ins.then_inc(*c_mu.up())
                    dve.wait_ge(*c_mu.at(L, 6 * c + 2))
                    carry_wait()
                    dve.copy_predicated(heads(XT_), level(0, 0), heads(LTm)).then_inc(*c_x1.up())
                    for lv in range(1, 7):
                        dve.wait_ge(*c_pp.at(L, 6 * c + lv))
                        carry_wait()
                        dve.copy_predicated(heads(PPs[lv % 2]), level(1, lv), heads(ps[4][:, :])).then_inc(*c_ppu.up())
                        link(dve.tensor_copy(heads(PPs[(lv + 1) % 2]), over_heads(C("ident"))))
                        gated(("c_level", c, lv, 1))
                    gated(("c_out", c, 1))
                    dve.wait_ge(*c_s.at(L, c + 1))
                    for t in range(FT):
                        ins = tt(st[:, t, :], st[:, t, :], ps[7][:, t * HD:(t + 1) * HD], ADD)
                    link(ins)
                    for t in range(FT):
                        ins = ts(st[:, t, :], st[:, t, :], col[:, 3, t * NT + c:t * NT + c + 1], None, MUL)
                    link(ins, c_st)
                    gated(("c_out", c, 2))
                dve.wait_ge(*c_mean.at(L, 2))
                for t in range(FT):
                    ins = stt(S(3, t), ps[4 + t][:, :], -1.0 / HD, S(3, t), MUL, ADD)
                link(ins, c_cen)
                dve.wait_ge(*c_var.at(L, 2))
                for t in range(FT):
                    ins = ts(S(5, t), ps[6 + t][:, :], 1.0 / HD, GN_EPS, MUL, ADD)
                ins.then_inc(*c_vv.up())
                dve.wait_ge(*c_rr.at(L, 1))
                link(tt(slab[:, 3, :], slab[:, 3, :], slab[:, 5, :], MUL))
                for t in range(FT):
                    ins = ts(S(3, t), S(3, t), pcol("lnw", t), pcol("lnb", t), MUL, ADD)
                link(ins)
                link(tt(slab[:, 3, :], slab[:, 3, :], slab[:, 0, :], ADD))
                dve.wait_ge(*c_g.at(L, 2))
                for t in range(FT):
                    ins = tt(S(3, t), ps[4 + t][:, :], S(3, t), MUL)
                link(ins)
                gated("D")
                dve.wait_ge(*dense_done.at(L, INDEX[("branch0", KT - 1)] + 1))
                split(S(3), y[0][:, 0, :, :], y[1][:, 0, :, :], y_ready)

                f_, t5, c5 = small[SM_F:SM_F + H, :], S(13, 0)[SM_F:SM_F + H, :], S(13, 1)[SM_F:SM_F + H, :]
                link(ts(f_, f_, pcol("foxb", 0, SM_F, SM_F + H), None, ADD))
                stt(t5, f_, -1.0, f_, MUL, ALU.max).then_inc(*d_abs.up())
                link(ts(f_, f_, 0.0, None, ALU.min))
                dve.wait_ge(*d_ln.at(L, 1))
                link(tt(t5, t5, f_, SUB))
                carry_wait()
                dve.tensor_tensor_scan(c5, C("ones", SM_F, SM_F + H, P)[:, 0:1].to_broadcast([H, T]), t5, 0.0, MUL, ADD)\
                    .then_inc(*d_c.up())
                gated(("d_prep", 1))
                dve.wait_ge(*d_bcu.at(L, H))
                softmax(1, lambda b, h, n: S(14 + h // 2, h % 2)[:, 0:n])

                gated("rest")
                for m in range(KT):
                    dve.wait_ge(*merged.at(L, 3 * KT + m + 1))
                    split(acc[:, m, :], u[0][:, m, :], u[1][:, m, :], m_split)
                residual(1, mix, "post")
                norm_h(2, "mpre")
                dve.wait_ge(*acc0.at(L, 1))
                carry_wait()
                with dve.Fori(0, QUARTERS) as q:
                    for m in range(KT):
                        r_ = tmp[:, m % 4, :]
                        dve.wait_ge(*act_took.at(L, q * KT + (ACT0 + m + 1)))
                        def chained(ins, sig=dve_step):
                            per_quarter = 8 * 2 if sig is dve_step else 8
                            base_ = sig.count
                            ins.then_inc(*sig.up())
                            dve.wait_ge(*sig.at(L, q * per_quarter + base_ + 1))
                        chained(tt(r_, r_, r_, MUL))
                        chained(dve.tensor_copy(u[0][:, m, :], r_))
                        tt(u[1][:, m, :], r_, u[0][:, m, :].bitcast(f32), SUB).then_inc(*u_ready.up(QUARTERS))
                    for m in range(KT):
                        dve.wait_ge(*dense_done.at(L, q * 16 + (MLP0 + 8 + m + 1)))
                        tt(acc[:, m, :], acc[:, m, :], ps[m % 4][:, :], ADD).then_inc(*dve_took.up(QUARTERS))
                dve_step.count += 3 * 16
                dve.wait_ge(*dve_took.at(L, DVE0 + 8 * QUARTERS))
                residual(3, acc, "mpost")

    return signals


def pack_weights(inputs):
    w_in, w_branch = np.asarray(inputs["w_in"]), np.asarray(inputs["w_branch"])
    w_out, w_up, w_down = (np.asarray(inputs[n]) for n in ("w_out", "w_up", "w_down"))

    def chunk(w):
        return w.reshape(-1, P, w.shape[1]).transpose(1, 0, 2).reshape(P, -1)
    proj, merge, rest = [], [], []
    for l in range(LAYERS):
        wl = w_in[l]
        small = np.zeros((D, P), np.float32)
        small[:, SM_IK:SM_IK + IDIM] = wl[:, B_IK:B_IK + IDIM]
        small[:, SM_F:SM_F + H] = wl[:, D_F:D_F + H]
        small[:, SM_IW:SM_IW + IH] = wl[:, B_IW:B_IW + IH]
        first = {"aq": A_Q, "af": A_F, "ai": A_I, "ag": A_G, "bq": B_Q, "bk": B_K, "bv": B_V, "biq": B_IQ, "cr": C_R,
                 "ck": C_K, "cv": C_V, "cl": C_L, "dq": D_Q, "dk": D_K, "dv": D_V}
        for name, _, n in PROJ_A + PROJ_B + PROJ_C + PROJ_D:
            proj += [chunk(small if name == "bs" else wl[:, first[name] + P * i:first[name] + P * (i + 1)]) for i in range(n)]
        for n in range(4):
            for i in range(KT):
                cs = slice(P * i, P * (i + 1))
                merge.append(np.concatenate([chunk(wl[:, GATE + n * D:][:, cs]), chunk(w_branch[l, n][:, cs])], axis=1))
        rest += [chunk(w_out[l][:, P * i:P * (i + 1)]) for i in range(KT)]
        for q in range(QUARTERS):
            rest += [chunk(w_up[l][:, D * q + P * i:D * q + P * (i + 1)]) for i in range(KT)]
            rest += [chunk(w_down[l][D * q:D * (q + 1), P * i:P * (i + 1)]) for i in range(KT)]
    return np.stack(proj), np.stack(merge), np.stack(rest)


def pack_params(inputs):
    par = np.zeros((LAYERS, P, PAR), np.float32)
    a = {k: np.asarray(v) for k, v in inputs.items()}
    for l in range(LAYERS):
        g = max(l - 1, 0)

        def put(name, v):
            v = v.reshape(-1, P).T
            par[l, :, PC[name]:PC[name] + v.shape[1]] = v
        for name, key in (("pre", "norm_mix_pre"), ("post", "norm_mix_post"), ("mpre", "norm_mlp_pre"),
                          ("mpost", "norm_mlp_post"), ("mu", "rwkv_mu"), ("w0", "rwkv_w0"), ("a0", "rwkv_a0"),
                          ("kk", "rwkv_k_k"), ("ka", "rwkv_k_a"), ("rk", "rwkv_r_k"), ("lnw", "rwkv_ln_w"),
                          ("lnb", "rwkv_ln_b")):
            put(name, a[key][l])
        put("v0", a["rwkv_v0"][g])
        put("hgw", np.concatenate([a["hgrn_norm_w"][l]] * 2))
        put("lb0", a["hgrn_lb_logits"][0])
        put("lb1", a["hgrn_lb_logits"][1])
        par[l, SM_F:SM_F + H, PC["foxb"]] = a["fox_f_bias"][l]
        par[l, :, PC["flag"]] = min(l, 1)
        par[l, 0:32, NPAR:NPAR + 256] = a["rwkv_w2"][l]
        par[l, 32:64, NPAR:NPAR + 256] = a["rwkv_a2"][l]
        par[l, 64:128, NPAR:NPAR + 256] = a["rwkv_g2"][l]
        par[l, :, NPAR + 256:NPAR + 320] = a["rwkv_v1"][g].reshape(FT, P, 32).transpose(1, 0, 2).reshape(P, 64)
        par[l, 0:32, NPAR + 320:] = a["rwkv_v2"][g]
    return par


def kernel(**inputs):
    import concourse.bacc as bacc
    from concourse.bass_utils import run_bass_kernel_spmd

    nc = bacc.Bacc("TRN2", target_bir_lowering=False, num_devices=1)
    proj, merge, rest = pack_weights(inputs)
    con, msk, rope = constants()
    x = np.asarray(inputs["x"])[0].T.reshape(KT, P, T).transpose(1, 0, 2).reshape(P, KT * T)
    arrays = {"x_in": x, "wproj": proj, "wmerge": merge, "wrest": rest, "params": pack_params(inputs),
              "tables": con, "masks": msk, "rope": rope}
    arrays = {k: np.ascontiguousarray(v) for k, v in arrays.items()}
    args = [nc.dram_tensor(k, v.shape, mybir.dt.from_np(v.dtype), kind="ExternalInput").ap() for k, v in arrays.items()]
    args.append(nc.dram_tensor("out", (P, KT * T), mybir.dt.float32, kind="ExternalOutput").ap())
    trunk_kernel(nc, *args)
    r = run_bass_kernel_spmd(nc, [arrays], core_ids=[0])
    got = r.results[0]["out"]
    return got.reshape(P, KT, T).transpose(1, 0, 2).reshape(D, T).T.reshape(1, T, D)
```

```python
import numpy as np
import concourse.bass as bass
from concourse import mybir
from contextlib import ExitStack

LAYERS, T, D = 2, 512, 1024
P = 128
KT = D // P
W = D // 4
HD = 64
H = W // HD
NT = T // P
FT = W // P
IH, IDIM, TOPK = 8, 32, min(256, T // 4)
QUARTERS = 4
EPS, GN_EPS = 1e-6, 64e-5
NEG = -8e30
TAKEN = -3e38
CH = KT * P
CHM = CH + FT * P

A_Q, A_F, A_I, A_G = 0, 256, 512, 768
B_Q, B_K, B_V, B_IQ, B_IK, B_IW = 1024, 1280, 1536, 1792, 2048, 2080
C_R, C_K, C_V, C_L = 2088, 2344, 2600, 2856
D_Q, D_K, D_V, D_F, GATE = 2984, 3240, 3496, 3752, 3756
SM_IK, SM_F, SM_IW = 0, 32, 64

PROJ_A = (("aq", "fm", 2), ("af", "fm", 2), ("ai", "tm", 2), ("ag", "fm", 2))
PROJ_B = (("bs", "fm", 1), ("bq", "fm", 2), ("bk", "fm", 2), ("biq", "fm", 2), ("bv", "tm", 2))
PROJ_C = (("cr", "fm", 2), ("ck", "fm", 2), ("cv", "fm", 2), ("cl", "fm", 1))
PROJ_D = (("dq", "fm", 2), ("dk", "fm", 2), ("dv", "tm", 2))
DENSE = []
for proj, gates in ((PROJ_A + PROJ_B + PROJ_C, (0, 1)), (PROJ_D, (2, 3))):
    for name, kind, n in proj:
        DENSE += [(name, i, kind, "act") for i in range(n)]
    for n in gates:
        for m in range(KT):
            DENSE += [(f"gate{n}", m, "fm", "act"), (f"branch{n}", m, "fm", "dve")]
DENSE += [("out", m, "fm", "act") for m in range(KT)]
MLP0 = len(DENSE)
BANK0 = -MLP0 % 4
INDEX = {(n, i): k for k, (n, i, _, _) in enumerate(DENSE)}
TAKEN_BY = {e: [sum(x[3] == e for x in DENSE[:k + 1]) for k in range(MLP0)] for e in ("act", "dve")}
ACT0, DVE0 = TAKEN_BY["act"][-1], TAKEN_BY["dve"][-1]
CHUNK_OF = [sum(not x[0].startswith("branch") for x in DENSE[:k + 1]) - 1 for k in range(MLP0)]
LAST_OF_CHUNK = {c: k for k, c in enumerate(CHUNK_OF)}
MLP_CHUNK0 = CHUNK_OF[-1] + 1
CHUNKS = MLP_CHUNK0 + 16 * QUARTERS
NA, NB, NC, ND = (sum(n for _, _, n in x) for x in (PROJ_A, PROJ_B, PROJ_C, PROJ_D))
RUNS = (("proj", 0, 0, NA + NB + NC), ("merge", 0, NA + NB + NC, 2 * KT), ("proj", NA + NB + NC, NA + NB + NC + 2 * KT, ND),
        ("merge", 2 * KT, NA + NB + NC + ND + 2 * KT, 2 * KT), ("rest", 0, NA + NB + NC + ND + 4 * KT, KT + 16 * QUARTERS))
assert all(first % 2 == 0 and at % 2 == 0 and n % 2 == 0 for _, at, first, n in RUNS)


END, _n = [], 0
for name, _, _, _ in DENSE:
    _n += FT if name.startswith("branch") else KT
    END.append(_n)


def schedule():
    reach, taken, gated = {}, {}, {}
    at = 0

    def place(key, steps, limit):
        nonlocal at
        at = max(at, min(at + steps, END[INDEX[limit]]))
        reach[key], taken[key], gated[key] = at, at - TAKE_LAG, at - GATE_LAG

    def all_of(key, last):
        nonlocal at
        end = END[INDEX[last]]
        at = max(at, end)
        reach[key], taken[key], gated[key] = at, max(end, at - TAKE_LAG), max(end, at - GATE_LAG)

    all_of("A", ("ag", 1))
    for lv in range(8):
        place(("a_level", lv), FILL["a_level"][lv], ("cl", 0))
    for c in range(NT + 1):
        place(("a_keys", c), FILL["a_keys"], ("cl", 0))
    for c in range(NT):
        place(("a_chunk", c), FILL["a_chunk"], ("cl", 0))
    for i in range(2):
        place(("a_norm", i), FILL["a_norm"], ("cl", 0))
    all_of("B", ("bv", 1))
    for r in range(7):
        place(("b_rope", r), FILL["b_rope"], ("branch0", KT - 1))
    for i in range(3 * IH):
        place(("b_ix", i), FILL["b_ix"], ("branch0", KT - 1))
    for r in range(TOPK // 8):
        place(("b_topk", r), FILL["b_topk"], ("branch0", KT - 1))
    for i in range(16):
        for n in range(2):
            place(("b_att", i, n), FILL["b_att"][n], ("branch0", KT - 1))
    all_of("C", ("cl", 0))
    place("c_start", FILL["c_start"], ("branch1", KT - 1))
    for i in range(4):
        place(("c_prep", i), FILL["c_prep"][i], ("branch1", KT - 1))
    for c in range(NT):
        place(("c_mask", c), FILL["c_mask"], ("dk", 1))
        for lv in range(1, 7):
            for n in range(2):
                place(("c_level", c, lv, n), FILL["c_level"][n], ("dk", 1))
        for i in range(3):
            place(("c_out", c, i), FILL["c_out"][i], ("dk", 1))
    for i in range(2):
        place(("c_norm", i), FILL["c_norm"], ("dv", 1))
    all_of("D", ("dv", 1))
    for i in range(2):
        place(("d_prep", i), FILL["d_prep"], ("branch2", KT - 1))
    for i in range(16):
        for n in range(2):
            place(("d_att", i, n), FILL["d_att"][n], ("branch2", KT - 1))
    all_of("rest", ("out", KT - 1))
    return reach, taken, gated


TAKE_LAG, GATE_LAG = 4, 8
FILL = {"a_level": (8, 8, 8, 8, 8, 8, 8, 8), "a_keys": 2, "a_chunk": 2, "a_norm": 4, "b_rope": 2, "b_ix": 1, "b_topk": 5,
        "b_att": (1, 1), "c_start": 8, "c_prep": (2, 2, 0, 12), "c_mask": 3, "c_level": (1, 1), "c_out": (2, 2, 2), "c_norm": 4,
        "d_prep": 20, "d_att": (0, 0)}
REACH, TAKEN_TO, GATED_TO = schedule()

PC, _n = {}, 0
for name, n in (("pre", 8), ("post", 8), ("mpre", 8), ("mpost", 8), ("hgw", 1), ("lb0", 2), ("lb1", 2),
                ("foxb", 1), ("mu", 7), ("w0", 2), ("a0", 2), ("kk", 2), ("ka", 2), ("rk", 2), ("lnw", 2),
                ("lnb", 2), ("v0", 2), ("flag", 1)):
    PC[name] = _n
    _n += n
NPAR = _n
PAR = NPAR + 256 + 64 + 256

CC, _n = {}, 0
for name, n in (("ident", P), ("ones", P), ("blk", P), ("roth", P), ("roti", P), ("rep", P), ("reprot", P),
                ("cneg", P), ("slt", P), ("sle", P), ("sgt", P), ("sel", H), ("seg", T), ("eps", 1)):
    CC[name] = _n
    _n += n
NCON = _n
LEVELS = [2 ** i for i in range(7)]


def constants():
    c = np.zeros((P, NCON), np.float32)
    i, j = np.arange(P)[:, None], np.arange(P)[None, :]
    put = lambda name, v: c.__setitem__((slice(None), slice(CC[name], CC[name] + v.shape[1])), v)
    put("ident", (i == j) * 1.0)
    put("ones", np.ones((P, P)))
    put("blk", (i // HD == j // HD) * 1.0)

    def rot(dim):
        half, r = dim // 2, j % dim
        return np.where((r < half) & (i == j + half), -1.0, 0.0) + np.where((r >= half) & (i == j - half), 1.0, 0.0)
    put("roth", rot(HD))
    put("roti", rot(IDIM))
    put("rep", (i == j % IDIM) * 1.0)
    put("reprot", (rot(IDIM)[:, :IDIM])[:, np.arange(P) % IDIM])
    put("cneg", np.where(j > i, NEG, 0.0))
    put("slt", (i < j) * 1.0)
    put("sle", (i <= j) * 1.0)
    put("sgt", (i > j) * 1.0)
    sel = np.zeros((P, H))
    for h in range(H):
        sel[SM_F + h, h] = 8.0
    put("sel", sel)
    put("eps", np.full((P, 1), EPS))
    put("seg", np.broadcast_to((np.arange(T) % P != 0) * 1.0, (P, T)))
    m = np.zeros((P, 2, len(LEVELS), P), np.float32)
    for k, n in enumerate(LEVELS):
        same = i // (2 * n) == j // (2 * n)
        m[:, 0, k] = same & (i % (2 * n) < n) & (j % (2 * n) >= n)
        m[:, 1, k] = m[:, 0, k].T
    rope = np.zeros((P, 4, T), np.float32)
    for k, dim in enumerate((HD, IDIM)):
        inv = (1.0 / (np.float32(10000.0) ** (np.arange(0, dim, 2, dtype=np.float32) / np.float32(dim)))).astype(np.float32)
        ang = np.arange(T, dtype=np.float32)[None, :] * inv[:, None]
        rope[:, 2 * k] = np.tile(np.cos(ang), (2 * P // dim, 1))
        rope[:, 2 * k + 1] = np.tile(np.sin(ang), (2 * P // dim, 1))
    return c, m.reshape(P, -1), rope.reshape(P, -1)


class Signal:

    def __init__(self, handle, name, per_layer):
        self.handle, self.name, self.per_layer, self.count = handle, name, per_layer, 0

    def at(self, layer, k):
        return self.handle, layer * self.per_layer + k

    def up(self, times=1):
        self.count += times
        return self.handle, 1


def trunk_kernel(nc, x_in, wproj, wmerge, wrest, par_in, con_in, mask_in, rope_in, out):
    f32, f32r, u8 = mybir.dt.float32, mybir.dt.float32r, mybir.dt.uint8
    ALU, ACT = mybir.AluOpType, mybir.ActivationFunctionType
    nc.disable_value_cache = True
    MUL, ADD, SUB = ALU.mult, ALU.add, ALU.subtract
    ctx = ExitStack()
    with ctx:
        def sb(name, shape, dt=f32):
            return ctx.enter_context(nc.sbuf_tensor(name, shape, dt))

        signals = []

        def signal(name, per_layer):
            signals.append(Signal(ctx.enter_context(nc.semaphore(name)), name, per_layer))
            return signals[-1]

        x = sb("x", [P, KT, T])
        hn = [sb(f"hn_{n}", [P, KT, T], f32r) for n in ("hi", "lo")]
        y = [sb(f"y_{n}", [P, 2, FT, T], f32r) for n in ("hi", "lo")]
        wsl = sb("wsl", [P, 2, CHM])
        wsp = [sb(f"w_{n}", [P, 2, CHM], f32r) for n in ("hi", "lo")]
        slab0 = nc.sbuf_base
        slab = sb("slab", [P, 20, FT * T])
        assert nc.sbuf_base == slab0 + 20 * FT * T * 4
        acc = slab[:, 16:20, :].rearrange("p a (t n) -> p (a t) n", n=T)
        mix = slab[:, 0:4, :].rearrange("p a (t n) -> p (a t) n", n=T)
        u = [nc.alloc_sbuf_tensor_at(f"u_{n}", [P, KT, T], f32r, offset=slab0 + (8 + 4 * i) * FT * T * 4)
             for i, n in enumerate(("hi", "lo"))]
        con = sb("con", [P, NCON])
        msk = sb("msk", [P, 2 * len(LEVELS) * P], u8)
        par = sb("par", [P, PAR])
        tmp = sb("tmp", [P, 4, T])
        rstd = sb("rstd", [P, T])
        small = sb("small", [P, T])
        iw = sb("iw", [P, NT, IH])
        st = sb("st", [P, FT, HD])
        lb = sb("lb", [P, 2, FT])
        col = sb("col", [P, 8, 8])
        v1st = sb("v1st", [P, FT, T])
        ps = [ctx.enter_context(nc.psum_tensor(f"bank{i}", [P, 512], f32)) for i in range(8)]

        def S(i, half=None):
            v = slab[:, i, :].rearrange("p (t n) -> p t n", t=FT)
            return v if half is None else v[:, half, :]

        def C(name, lo=0, hi=P, n=P):
            return con[lo:hi, CC[name]:CC[name] + n]

        def pcol(name, i=0, lo=0, hi=P):
            return par[lo:hi, PC[name] + i:PC[name] + i + 1]

        def heads(ap):
            return ap.rearrange("p (h t) -> p h t", h=H)

        def over_heads(ap):
            return ap[:, None, :].to_broadcast([P, H, P])

        def halves(ap, n, half):
            return ap.rearrange("p (b two n) -> p b two n", two=2, n=n)[:, :, half, :]

        def packed(ap, n):
            return ap.rearrange("p (b n) -> p b n", n=n)

        def level_half(side, k, n, half):
            m = (side * len(LEVELS) + k) * P
            v = halves(msk[:, m:m + P], n, half)
            return v[:, None, :, :].to_broadcast([P, H, P // (2 * n), n])

        def level(side, k):
            m = (side * len(LEVELS) + k) * P
            return over_heads(msk[:, m:m + P])

        def half(i):
            return slab[:, i // 2, (i % 2) * T:(i % 2 + 1) * T]

        c_halves = [half(i) for i in (24, 25, 26, 27, 28, 29, 31, 18, 19)]
        c_pairs = [slab[:, 12, :], slab[:, 13, :]]
        lora = par[:, NPAR:NPAR + 256]
        v1w = par[:, NPAR + 256:NPAR + 320].rearrange("p (t n) -> p t n", t=FT)
        v2w = par[0:32, NPAR + 320:NPAR + 576]

        once = ctx.enter_context(nc.semaphore("tables_loaded"))
        masks_loaded = ctx.enter_context(nc.semaphore("masks_loaded"))
        x_loaded = [ctx.enter_context(nc.semaphore(f"x_loaded_{i}")) for i in range(4)]
        masks_ready = ctx.enter_context(nc.semaphore("masks_ready"))
        cleared = ctx.enter_context(nc.semaphore("buffers_cleared"))
        carrier = ctx.enter_context(nc.semaphore("wait_carrier"))
        stored = ctx.enter_context(nc.semaphore("out_stored"))
        rope_in_ = signal("rope_loaded", 16)
        w_arrived = [ctx.enter_context(nc.semaphore(f"weights_arrived_{s}")) for s in range(2)]
        par_loaded = signal("params_loaded", 16)
        x_tiles = signal("x_updated", 2 * KT)
        X0 = KT + 1
        dense_done = signal("dense_done", MLP0 + 16 * QUARTERS)
        w_hi_done = signal("weights_hi_ready", CHUNKS)
        w_split = signal("weights_split", CHUNKS)
        act_took = signal("act_took_dense", ACT0 + 8 * QUARTERS)
        dve_took = signal("dve_took_dense", DVE0 + 8 * QUARTERS)
        dve_step = signal("dve_step", 244)
        act_step = signal("act_step", 8)
        squared = signal("squared", 4 * KT)
        sumsq = signal("sum_of_squares", 2 * KT + 2)
        SUMMED = (KT, KT + 1, 2 * KT + 1, 2 * KT + 2)
        added = signal("squares_added", 2 * (KT - 1))
        rstd_done = signal("rstd_by_exp", 4)
        h_raw = signal("h_ready", 2 * KT)
        h_hi = signal("h_hi_ready", 2 * KT)
        h_ready = signal("h_even_split", KT)
        h_odd = signal("h_odd_split", KT)
        a_prep = signal("a_gate_logit_ready", 1)
        a_ln = signal("a_log_gate_ready", 1)
        a_diff = signal("a_decay_exponents_ready", 8)
        a_exp = signal("a_decays_ready", 9)
        a_ops = signal("a_level_operands_ready", 9)
        a_sc = signal("a_scores_ready", 8 * NT)
        a_sc_used = signal("a_scores_taken", 8 * NT)
        a_tr = signal("a_keys_transposed", 4)
        a_tr_used = signal("a_keys_taken", 4)
        a_o = signal("a_outputs_ready", NT)
        a_o_used = signal("a_outputs_taken", NT)
        a_su = signal("a_state_update_ready", NT)
        a_st = signal("a_state_ready", NT + 1)
        a_sq = signal("a_squared", 2)
        a_ss = signal("a_sum_ready", 2)
        a_var = signal("a_var_ready", 1)
        a_r = signal("a_rstd_ready", 1)
        y_ready = signal("y_ready", 2)
        lb_in = signal("bound_logits_ready", 1)
        lb_exp = signal("bound_exps_ready", 1)
        b_iwt = signal("b_index_weights_transposed", 1)
        b_rot = signal("b_rotated", 7)
        b_rep = signal("b_index_key_replicated", 1)
        b_rope = signal("b_rope_done", 7)
        b_ix = signal("b_index_scores_ready", IH * 3)
        b_relu = signal("b_relu_done", IH * 3)
        b_acc = signal("b_index_scores_used", IH * 3)
        b_iwc = signal("b_index_weights_copied", 1)
        at_lg = signal("logits_ready", 32)
        at_mx = signal("logits_masked", 32)
        at_ex = signal("exps_ready", 32)
        at_p = signal("probs_ready", 32)
        at_tr = signal("probs_transposed", 32)
        at_pt = signal("probs_taken", 32)
        at_pv = signal("attention_ready", 2 * NT)
        at_o = signal("attention_taken", 2 * NT)
        d_abs = signal("d_forget_logit_ready", 1)
        d_ln = signal("d_softplus_ready", 1)
        d_c = signal("d_cumulated", 1)
        d_bc = signal("d_cumulated_broadcast", H)
        d_bcu = signal("d_broadcast_taken", H)
        c_mix = signal("c_shifted", 2)
        c_act = signal("c_lora_hidden_ready", 1)
        c_lw = signal("c_lora_out_ready", 4)
        c_sg = signal("c_lora_out_taken", 4)
        c_g = signal("c_gate_ready", 2)
        c_vh = signal("c_value_hidden_ready", 1)
        c_vhc = signal("c_value_hidden_copied", 1)
        c_vg = signal("c_value_gate_ready", 2)
        c_vgs = signal("c_value_gate_taken", 2)
        c_sq = signal("c_squares_ready", 4)
        c_ss = signal("c_sums_ready", 4)
        c_kkv = signal("c_key_norm_ready", 1)
        c_kkr = signal("c_key_rnorm_ready", 1)
        c_ex = signal("c_exponents_ready", 1)
        c_exd = signal("c_exps_ready", 1)
        c_til = signal("c_operands_ready", 1)
        c_tr = signal("c_transposed", 6)
        c_tru = signal("c_transposes_taken", 6)
        c_m = signal("c_pairwise_ready", 6 * NT)
        c_mu = signal("c_pairwise_masked", 6 * NT)
        c_x1 = signal("c_inverse_started", NT)
        c_pp = signal("c_level_product_ready", 6 * NT)
        c_ppu = signal("c_level_product_masked", 6 * NT)
        c_xx = signal("c_level_inverse_ready", 11 * NT)
        c_xxu = signal("c_level_inverse_taken", 11 * NT)
        c_b = signal("c_rhs_ready", NT)
        c_bu = signal("c_rhs_taken", NT)
        c_u = signal("c_solution_ready", NT)
        c_uu = signal("c_solution_taken", NT)
        c_y = signal("c_outputs_ready", NT)
        c_yu = signal("c_outputs_taken", NT)
        c_s = signal("c_state_update_ready", NT)
        c_st = signal("c_state_ready", NT + 1)
        c_mean = signal("c_mean_ready", 2)
        c_cen = signal("c_centred", 1)
        c_csq = signal("c_centred_squared", 2)
        c_var = signal("c_variance_sum_ready", 2)
        c_vv = signal("c_variance_ready", 1)
        c_rr = signal("c_rstd_ready", 1)
        merged = signal("merged_ready", 4 * KT)
        product = dve_took
        m_split = signal("merged_split", KT)
        y_hi = signal("attention_hi_ready", 2 * NT)
        acc0 = signal("acc_cleared", 1)
        u_ready = signal("hidden_ready", 4 + 8 * QUARTERS)

        block = ctx.enter_context(nc.Block())
        ONCE = 16

        @block.sync
        def _(sp):
            sp.dma_start(con[:, :], con_in).then_inc(once, 16)
            NM = 2 * len(LEVELS) * P
            for i in range(4):
                sp.dma_start(x[:, 2 * i:2 * i + 2, :].rearrange("p k t -> p (k t)"), x_in[:, 2 * i * T:(2 * i + 2) * T])\
                    .then_inc(x_loaded[i], 16)
            sp.dma_start(slab[:, 0:2, :].rearrange("p a n -> p (a n)")[:, 0:NM], mask_in).then_inc(masks_loaded, 16)
            with sp.Fori(0, LAYERS) as layer:
                for name, at, first, count in RUNS:
                    src, size, per_layer = {"proj": (wproj, CH, NA + NB + NC + ND), "merge": (wmerge, CHM, 4 * KT),
                                            "rest": (wrest, CH, KT + 16 * QUARTERS)}[name]
                    with sp.Fori(0, count // 2) as pair:
                        for s in range(2):
                            row = sp.snap(layer * per_layer + 2 * pair + (at + s))
                            need = sp.snap(layer * CHUNKS + 2 * pair + (first + s + 1))
                            sp.wait_ge(w_split.handle, need)
                            sp.dma_start(wsl[:, s, 0:size],
                                         src[bass.ds(row, 1)].rearrange("a p n -> (a p) n")).then_inc(w_arrived[s], 16)
            for s in range(2):
                sp.wait_ge(w_split.handle, LAYERS * CHUNKS + s + 1)
                sp.dma_start(wsl[:, s, 0:CH], wproj[s:s + 1].rearrange("a p n -> (a p) n")).then_inc(w_arrived[s], 16)
            sp.wait_ge(x_tiles.handle, LAYERS * 2 * KT + X0)
            sp.dma_start(out, x[:, :, :].rearrange("p k t -> p (k t)")).then_inc(stored, 16)
            sp.wait_ge(stored, 16)

        @block.tensor
        def _(pe):
            pe.wait_ge(once, ONCE)
            pe.wait_ge(cleared, 1)
            mm = pe.matmul
            with pe.Fori(0, LAYERS) as L:
                step = [0]

                def product3(o_, stat, mov, first, last):
                    mm(o_, stat[0], mov[0], start=first, stop=False)
                    mm(o_, stat[0], mov[1], start=False, stop=False)
                    return mm(o_, stat[1], mov[0], start=False, stop=last)

                def weights(c, off, k):
                    w0 = off + k * P
                    return [w[:, c % 2, w0:w0 + P] for w in wsp]

                def begin(d):
                    name, i, _, _ = DENSE[d]
                    n = int(name[-1]) if name.startswith("branch") else None
                    if n is None:
                        pe.wait_ge(*w_split.at(L, CHUNK_OF[d] + 3))
                    elif i == 0:
                        pe.wait_ge(*(y_ready.at(L, n // 2 + 1) if n % 2 == 0 else at_o.at(L, (n // 2 + 1) * NT)))
                    if d >= 4:
                        taker = DENSE[d - 4][3]
                        pe.wait_ge(*{"act": act_took, "dve": dve_took}[taker].at(L, TAKEN_BY[taker][d - 4]))

                def dense(place_):
                    for s_ in range(step[0], REACH[place_]):
                        d = sum(e <= s_ for e in END)
                        name, i, kind, _ = DENSE[d]
                        k = s_ - (END[d - 1] if d else 0)
                        if k == 0:
                            begin(d)
                        if d == 0:
                            pe.wait_ge(*(h_odd if k % 2 else h_ready).at(L, k // 2 + 1))
                        if name == "out" and i == 0:
                            pe.wait_ge(*m_split.at(L, k + 1))
                        o_ = ps[(BANK0 + d) % 4]
                        if kind == "tm":
                            tt, first_k = k // 2, k % 2 * (KT // 2)
                            for k_ in range(first_k, first_k + KT // 2):
                                ins = product3(o_[:, tt * P:(tt + 1) * P], [h[:, k_, tt * P:(tt + 1) * P] for h in hn],
                                               weights(CHUNK_OF[d], 0, k_), k_ == 0, k_ == KT - 1)
                        elif name.startswith("branch"):
                            ins = product3(o_[:, :], weights(CHUNK_OF[d], CH, k), [v[:, int(name[-1]) % 2, k, :] for v in y],
                                           k == 0, k == FT - 1)
                        else:
                            ins = product3(o_[:, :], weights(CHUNK_OF[d], 0, k),
                                           [v[:, k, :] for v in (u if name == "out" else hn)], k == 0, k == KT - 1)
                        if s_ + 1 == END[d]:
                            ins.then_inc(*dense_done.up())
                    step[0] = REACH[place_]

                def norm_sum(j, m):
                    pe.wait_ge(*squared.at(L, j * KT + m + 1))
                    mm(ps[4][:, :], C("ones"), tmp[:, m % 2, :], start=m == 0, stop=m == KT - 1).then_inc(*sumsq.up())

                def norm_total(j):
                    pe.wait_ge(*added.at(L, (j + 1) // 2 * (KT - 1)))
                    mm(ps[4][:, :], C("ones"), rstd[:, :], start=True, stop=True).then_inc(*sumsq.up())

                def norm_sums(j):
                    for m in range(KT):
                        norm_sum(j, m)

                def attention(which, q, k, v, pt):
                    base = 16 * which

                    def logits(i):
                        b, h = divmod(i, H)
                        lo = (h % 2) * HD
                        n = (b + 1) * P
                        if i >= 2:
                            pe.wait_ge(*at_mx.at(L, base + i - 1))
                        last = which == 0
                        ins = mm(ps[4 + i % 2][:, 0:n], q[lo:lo + HD, h // 2, b * P:(b + 1) * P],
                                 k[lo:lo + HD, h // 2, 0:n], start=True, stop=last)
                        if not last:
                            ins = mm(ps[4 + i % 2][:, b * P:n], C("ident"), C("cneg"), start=False, stop=True)
                        ins.then_inc(*at_lg.up())

                    def outputs(i):
                        b, h = divmod(i, H)
                        pe.wait_ge(*at_pt.at(L, base + i + 1))
                        if h == 0 and (b >= 2 or which):
                            pe.wait_ge(*at_o.at(L, which * NT + b - 1))
                        lo, o0 = (h % 2) * HD, b % 2 * 256 + h // 2 * P
                        for j in range(b + 1):
                            ins = mm(ps[7][lo:lo + HD, o0:o0 + P], v[:, j, h * HD:(h + 1) * HD],
                                     S(pt + i % 4 // 2, i % 2)[:, j * P:(j + 1) * P], start=j == 0, stop=j == b)
                        if h == H - 1:
                            ins.then_inc(*at_pv.up())
                    logits(0)
                    logits(1)
                    for i in range(16):
                        if i + 2 < 16:
                            logits(i + 2)
                        dense(("bd"[which] + "_att", i, 0))
                        pe.wait_ge(*at_p.at(L, base + i + 1))
                        if i:
                            pe.wait_ge(*at_pt.at(L, base + i))
                        for j in range(i // H + 1):
                            ins = pe.transpose(ps[6][:, j * P:(j + 1) * P], S(6 + i % 4 // 2, i % 2)[:, j * P:(j + 1) * P],
                                               C("ident"))
                        ins.then_inc(*at_tr.up())
                        if i:
                            outputs(i - 1)
                        dense(("bd"[which] + "_att", i, 1))
                    outputs(15)

                norm_sums(0)
                pe.wait_ge(*par_loaded.at(L, 16))

                dense("A")
                E, k_ = S(5), S(1)
                for lv in range(8):
                    dense(("a_level", lv))
                    pe.wait_ge(*a_ops.at(L, lv + 1))
                    for b in range(4):
                        lo = (b % 2) * HD
                        if lv:
                            pe.wait_ge(*a_sc_used.at(L, (lv - 1) * NT + b + 1))
                        for i in range(4):
                            c, t = 2 * (b // 2) + i // 2, i % 2
                            cs = slice(c * P, (c + 1) * P)
                            if lv == 0:
                                ins = mm(ps[4 + b][:, i * P:(i + 1) * P], k_[lo:lo + HD, t, cs], S(0)[lo:lo + HD, t, cs],
                                         start=True, stop=True)
                            else:
                                n = LEVELS[lv - 1]
                                ins = mm(packed(ps[4 + b][:, i * HD:(i + 1) * HD], n), E[lo:lo + HD, t, cs],
                                         halves(E[lo:lo + HD, t, cs], n, 1), start=True, stop=True)
                        ins.then_inc(*a_sc.up())
                dense(("a_keys", 0))
                pe.wait_ge(*a_ops.at(L, 9))
                for c in range(NT):
                    if c == 0:
                        pe.wait_ge(*a_sc_used.at(L, 8 * NT))
                    else:
                        pe.wait_ge(*a_tr_used.at(L, c))
                    for t in range(FT):
                        ins = pe.transpose(ps[4][:, t * P:(t + 1) * P], S(5)[:, t, c * P:(c + 1) * P], C("ident"))
                    ins.then_inc(*a_tr.up())
                    dense(("a_keys", c + 1))
                AT = [slab[:, 16 + c // 2, (c % 2) * T:(c % 2 + 1) * T] for c in range(NT)]
                v_ = slab[:, 4, :].rearrange("p (c n) -> p c n", c=NT)
                kh_ = slab[:, 7, :].rearrange("p (c n) -> p c n", c=NT)
                for c in range(NT):
                    pe.wait_ge(*a_st.at(L, c + 1))
                    pe.wait_ge(*a_tr_used.at(L, c + 1))
                    if c:
                        pe.wait_ge(*a_o_used.at(L, c))
                    for h in range(H):
                        lo, t = (h % 2) * HD, h // 2
                        o_ = ps[5][lo:lo + HD, t * P:(t + 1) * P]
                        at_ = AT[2 * (c // 2) + h % 2][:, (c % 2 * 2 + t) * P:(c % 2 * 2 + t + 1) * P]
                        mm(o_, v_[:, c, h * HD:(h + 1) * HD], at_, start=True, stop=False)
                        ins = mm(o_, st[lo:lo + HD, t, :], S(6)[lo:lo + HD, t, c * P:(c + 1) * P], start=False, stop=True)
                    ins.then_inc(*a_o.up())
                    for h in range(H):
                        lo, t = (h % 2) * HD, h // 2
                        ins = mm(ps[6][lo:lo + HD, t * HD:(t + 1) * HD], kh_[:, c, h * HD:(h + 1) * HD],
                                 v_[:, c, h * HD:(h + 1) * HD], start=True, stop=True)
                    ins.then_inc(*a_su.up())
                    dense(("a_chunk", c))
                dense(("a_norm", 0))
                pe.wait_ge(*a_sq.at(L, 2))
                for t in range(FT):
                    mm(ps[4 + t][:, :], C("blk"), S(19, t), start=True, stop=True).then_inc(*a_ss.up())
                dense(("a_norm", 1))

                dense("B")
                pe.wait_ge(*a_var.at(L, 1))
                pe.wait_ge(*act_took.at(L, TAKEN_BY["act"][INDEX[("bs", 0)]]))
                for tt in range(NT):
                    ins = pe.transpose(ps[7][:, tt * P:(tt + 1) * P], small[:, tt * P:(tt + 1) * P], C("ident"))
                ins.then_inc(*b_iwt.up())
                for r, (src, t, con_name) in enumerate(((8, 0, "roth"), (8, 1, "roth"), (9, 0, "roth"), (9, 1, "roth"),
                                                        (11, 0, "roti"), (11, 1, "roti"))):
                    if r >= 2:
                        pe.wait_ge(*b_rope.at(L, r - 1))
                    mm(ps[4 + r % 2][:, :], C(con_name), S(src, t), start=True, stop=True).then_inc(*b_rot.up())
                    dense(("b_rope", r))
                mm(ps[6][:, :], C("rep", 0, IDIM), small[0:IDIM, :], start=True, stop=True).then_inc(*b_rep.up())
                pe.wait_ge(*b_rope.at(L, 5))
                mm(ps[4][:, :], C("reprot", 0, IDIM), small[0:IDIM, :], start=True, stop=True).then_inc(*b_rot.up())
                dense(("b_rope", 6))
                pe.wait_ge(*b_rope.at(L, 7))
                n_ix = 0
                for b in range(1, NT):
                    for j in range(IH):
                        lo, t = (j % 4) * IDIM, j // 4
                        if n_ix >= 2:
                            pe.wait_ge(*b_relu.at(L, n_ix - 1))
                        mm(ps[4 + n_ix % 2][:, 0:(b + 1) * P], S(11)[lo:lo + IDIM, t, b * P:(b + 1) * P],
                           S(0, 1)[lo:lo + IDIM, 0:(b + 1) * P], start=True, stop=True).then_inc(*b_ix.up())
                        n_ix += 1
                        dense(("b_ix", n_ix - 1))
                pe.wait_ge(*b_relu.at(L, n_ix))
                pe.wait_ge(*b_iwc.at(L, 1))
                dense(("b_topk", TOPK // 8 - 1))
                attention(0, S(8), S(9), slab[:, 10, :].rearrange("p (c n) -> p c n", c=NT), 0)

                dense("C")
                pe.wait_ge(*at_o.at(L, NT))
                dense("c_start")
                pe.wait_ge(*c_act.at(L, 1))
                i_ = 0
                for lo, hi in ((0, 32), (32, 64)):
                    for t in range(FT):
                        mm(ps[4 + i_ % 4][:, :], lora[lo:hi, t * P:(t + 1) * P], S(15, 0)[lo:hi, :], start=True, stop=True)\
                            .then_inc(*c_lw.up())
                        i_ += 1
                dense(("c_prep", 0))
                pe.wait_ge(*c_sg.at(L, 4))
                pe.wait_ge(*c_mix.at(L, 2))
                for t in range(FT):
                    ins = mm(ps[6][0:32, :], v1w[:, t, :], S(14, t), start=t == 0, stop=t == 1)
                ins.then_inc(*c_vh.up())
                dense(("c_prep", 1))
                pe.wait_ge(*c_vhc.at(L, 1))
                for t in range(FT):
                    mm(ps[4 + t][:, :], v2w[:, t * P:(t + 1) * P], S(11, 0)[0:32, :], start=True, stop=True)\
                        .then_inc(*c_vg.up())
                for t in range(FT):
                    pe.wait_ge(*c_sq.at(L, t + 1))
                    mm(ps[6 + t][:, :], C("blk"), S(5, t), start=True, stop=True).then_inc(*c_ss.up())
                dense(("c_prep", 2))
                for t in range(FT):
                    pe.wait_ge(*c_vgs.at(L, 2))
                    pe.wait_ge(*c_sq.at(L, 3 + t))
                    mm(ps[4 + t][:, :], C("blk"), S(0, t), start=True, stop=True).then_inc(*c_ss.up())
                dense(("c_prep", 3))
                pe.wait_ge(*c_til.at(L, 1))
                n_tr = 0
                for src in (8, 5, 14):
                    for half in range(2):
                        if n_tr >= 4:
                            pe.wait_ge(*c_tru.at(L, n_tr - 3))
                        for cc in range(2):
                            for t in range(FT):
                                ins = pe.transpose(ps[4 + n_tr % 4][:, cc * 256 + t * P:cc * 256 + (t + 1) * P],
                                                   S(src)[:, t, (2 * half + cc) * P:(2 * half + cc + 1) * P], C("ident"))
                        ins.then_inc(*c_tr.up())
                        n_tr += 1
                pe.wait_ge(*c_tru.at(L, 6))
                RT, AA, KK, BB = S(6), S(7), S(8), S(5)
                tm = [slab[:, i, :].rearrange("p (c n) -> p c n", c=NT) for i in (1, 2, 4)]
                LTm, MTm, RBm, RKm, X_, XT_, R_, *PPs = c_halves
                for c in range(NT):
                    cs = slice(c * P, (c + 1) * P)
                    for i, ops in enumerate((((BB, AA), (KK, AA)), ((BB, AA), (KK, AA)), ((BB, RT), (KK, RT)),
                                             ((BB, RT), (KK, RT)), ((AA, BB),), ((AA, BB),))):
                        lo = (i % 2) * HD
                        if i == 0 and c:
                            pe.wait_ge(*c_yu.at(L, c))
                            pe.wait_ge(*c_st.at(L, c + 1))
                        if i >= 4:
                            pe.wait_ge(*c_mu.at(L, 6 * c + i - 3))
                        for m, (a_, b_) in enumerate(ops):
                            for t in range(FT):
                                ins = mm(ps[4 + i % 4][:, (m * 2 + t) * P:(m * 2 + t + 1) * P], a_[lo:lo + HD, t, cs],
                                         b_[lo:lo + HD, t, cs], start=True, stop=True)
                        ins.then_inc(*c_m.up())
                    dense(("c_mask", c))
                    pe.wait_ge(*c_mu.at(L, 6 * c + 6))
                    pe.wait_ge(*c_x1.at(L, c + 1))
                    for lv in range(1, 7):
                        if lv > 1:
                            pe.wait_ge(*c_xxu.at(L, 11 * c + 2 * (lv - 1)))
                        n = LEVELS[lv]
                        for h in range(H):
                            hs, hh = slice(h * P, (h + 1) * P), slice(h * HD, (h + 1) * HD)
                            ins = mm(packed(ps[4][:, hh], n), LTm[:, hs], halves(X_[:, hs], n, 0), start=True, stop=True)
                        ins.then_inc(*c_pp.up())
                        dense(("c_level", c, lv, 0))
                        pe.wait_ge(*c_ppu.at(L, 6 * c + lv))
                        PP = PPs[lv % 2]
                        if lv < 6:
                            for h in range(H):
                                hs, hh = slice(h * P, (h + 1) * P), slice(h * HD, (h + 1) * HD)
                                ins = mm(packed(ps[5][:, hh], n), XT_[:, hs], halves(PP[:, hs], n, 0), start=True, stop=True)
                            ins.then_inc(*c_xx.up())
                        for h in range(H):
                            hs, hh = slice(h * P, (h + 1) * P), slice(h * HD, (h + 1) * HD)
                            ins = mm(packed(ps[6][:, hh], n), PP[:, hs], halves(XT_[:, hs], n, 1), start=True, stop=True)
                        ins.then_inc(*c_xx.up())
                        dense(("c_level", c, lv, 1))
                    pe.wait_ge(*c_st.at(L, c + 1))
                    for h in range(H):
                        lo, t, hs = (h % 2) * HD, h // 2, slice(h * HD, (h + 1) * HD)
                        o_ = ps[7 if h % 2 == 0 else 4][:, t * HD:(t + 1) * HD]
                        mm(o_, AA[lo:lo + HD, t, cs], st[lo:lo + HD, t, :], start=True, stop=False)
                        ins = mm(o_, MTm[:, h * P:(h + 1) * P], tm[2][:, c, hs], start=False, stop=True)
                    ins.then_inc(*c_b.up())
                    dense(("c_out", c, 0))
                    pe.wait_ge(*c_bu.at(L, c + 1))
                    pe.wait_ge(*c_xxu.at(L, 11 * c + 11))
                    for h in range(H):
                        hs = slice(h * HD, (h + 1) * HD)
                        ins = mm(ps[5][:, hs], XT_[:, h * P:(h + 1) * P], R_[:, hs], start=True, stop=True)
                    ins.then_inc(*c_u.up())
                    dense(("c_out", c, 1))
                    pe.wait_ge(*c_uu.at(L, c + 1))
                    pe.sem_inc(carrier, 1)
                    U_ = R_[:, 256:512]
                    for h in range(H):
                        lo, t, hs = (h % 2) * HD, h // 2, slice(h * HD, (h + 1) * HD)
                        o_ = ps[6][lo:lo + HD, t * P:(t + 1) * P]
                        mm(o_, st[lo:lo + HD, t, :], RT[lo:lo + HD, t, cs], start=True, stop=False)
                        mm(o_, U_[:, hs], RBm[:, h * P:(h + 1) * P], start=False, stop=False)
                        ins = mm(o_, tm[2][:, c, hs], RKm[:, h * P:(h + 1) * P], start=False, stop=True)
                    ins.then_inc(*c_y.up())
                    for h in range(H):
                        lo, t, hs = (h % 2) * HD, h // 2, slice(h * HD, (h + 1) * HD)
                        o_ = ps[7][lo:lo + HD, t * HD:(t + 1) * HD]
                        mm(o_, tm[1][:, c, hs], U_[:, hs], start=True, stop=False)
                        ins = mm(o_, tm[0][:, c, hs], tm[2][:, c, hs], start=False, stop=True)
                    ins.then_inc(*c_s.up())
                    dense(("c_out", c, 2))
                pe.wait_ge(*c_yu.at(L, NT))
                pe.wait_ge(*c_st.at(L, NT + 1))
                for t in range(FT):
                    mm(ps[4 + t][:, :], C("blk"), S(3, t), start=True, stop=True).then_inc(*c_mean.up())
                dense(("c_norm", 0))
                for t in range(FT):
                    pe.wait_ge(*c_csq.at(L, t + 1))
                    if t == 0:
                        pe.wait_ge(*c_st.at(L, NT + 1))
                    mm(ps[6 + t][:, :], C("blk"), S(5, t), start=True, stop=True).then_inc(*c_var.up())
                dense(("c_norm", 1))
                for t in range(FT):
                    pe.wait_ge(*c_cen.at(L, 1))
                    mm(ps[4 + t][:, :], lora[64:128, t * P:(t + 1) * P], S(15, 0)[64:128, :], start=True, stop=True)\
                        .then_inc(*c_g.up())

                dense("D")
                pe.wait_ge(*y_ready.at(L, 2))
                dense(("d_prep", 0))
                pe.wait_ge(*d_c.at(L, 1))
                for h in range(H):
                    mm(ps[4 + h][:, :], con[SM_F:SM_F + H, CC["sel"] + h:CC["sel"] + h + 1].to_broadcast([H, P]),
                       S(13, 1)[SM_F:SM_F + H, :], start=True, stop=True).then_inc(*d_bc.up())
                dense(("d_prep", 1))
                pe.wait_ge(*d_bcu.at(L, H))
                pe.wait_ge(*act_took.at(L, TAKEN_BY["act"][INDEX[("dv", 1)]]))
                attention(1, S(10), S(11), slab[:, 12, :].rearrange("p (c n) -> p c n", c=NT), 8)

                dense("rest")
                norm_total(1)
                norm_sums(2)
                pe.sem_inc(carrier, 1)
                with pe.Fori(0, QUARTERS) as q:
                    for j in range(16):
                        up = j < 8
                        pe.wait_ge(*w_split.at(L, q * 16 + (MLP_CHUNK0 + j + 3)))
                        if j < 4:
                            pe.wait_ge(*dve_took.at(L, q * 8 + (DVE0 - 8 + j + 5)))
                        elif j < 12:
                            pe.wait_ge(*act_took.at(L, q * 8 + (ACT0 + j - 3)))
                        else:
                            pe.wait_ge(*dve_took.at(L, q * 8 + (DVE0 + j - 11)))
                        for k in range(KT):
                            if j == 0:
                                pe.wait_ge(*(h_odd if k % 2 else h_ready).at(L, (KT + k) // 2 + 1))
                            if j == 8:
                                pe.wait_ge(*u_ready.at(L, q * 8 + (4 + k + 1)))
                            ins = product3(ps[j % 4][:, :], weights(j, 0, k), [v[:, k, :] for v in (hn if up else u)],
                                           k == 0, k == KT - 1)
                        ins.then_inc(*dense_done.up(QUARTERS))
                norm_total(3)

        @block.scalar
        def _(act):
            fn = act.activation

            def link(ins, sig=act_step):
                ins.then_inc(*sig.up())
                act.wait_ge(*sig.at(L, sig.count))

            act.wait_ge(once, ONCE)
            act.wait_ge(cleared, 1)
            with act.Fori(0, LAYERS) as L:
                def hi_part(c):
                    act.wait_ge(w_arrived[c % 2], L * (8 * CHUNKS) + 16 * (c // 2 + 1))
                    act.wait_ge(*dense_done.at(L, LAST_OF_CHUNK[c - 2] + 1))
                    size = CHM if c in LAST_OF_CHUNK and DENSE[LAST_OF_CHUNK[c]][0].startswith("branch") else CH
                    fn(wsp[0][:, c % 2, 0:size], wsl[:, c % 2, 0:size], ACT.Copy).then_inc(*w_hi_done.up())

                def copy(o_, scale=1.0):
                    return lambda b_: fn(o_, b_, ACT.Copy, scale=scale)

                def tokens(slab_i, i):
                    return lambda b_: fn(slab[:, slab_i, :].rearrange("p (c n) -> p c n", c=NT)[:, :, i * P:(i + 1) * P],
                                         b_.rearrange("p (c n) -> p c n", c=NT), ACT.Copy)

                def forget(i):
                    def go(b_):
                        fn(S(2, i), b_, ACT.Sigmoid)
                        return fn(S(1, i), b_, ACT.Sigmoid, scale=-1.0)
                    return go

                def out_gate(i):
                    def go(b_):
                        fn(S(3, i), b_, ACT.Copy)
                        return fn(S(19, i), b_, ACT.Sigmoid)
                    return go

                to_sbuf = {"aq": lambda i: copy(S(0, i), HD ** -0.5), "af": forget, "ai": lambda i: tokens(4, i),
                           "ag": out_gate, "bs": lambda i: copy(small[:, :]), "bq": lambda i: copy(S(8, i)),
                           "bk": lambda i: copy(S(9, i)), "biq": lambda i: copy(S(11, i)), "bv": lambda i: tokens(10, i),
                           "cr": lambda i: copy(S(12, i)), "ck": lambda i: copy(S(13, i)), "cv": lambda i: copy(S(14, i)),
                           "cl": lambda i: copy(S(15, 0)), "dq": lambda i: copy(S(10, i)), "dk": lambda i: copy(S(11, i)),
                           "dv": lambda i: tokens(12, i)}
                place = [0]

                def take(place_):
                    while place[0] < MLP0:
                        d = place[0]
                        name, i, _, _ = DENSE[d]
                        gate = name.startswith("gate")
                        if END[d + gate] > TAKEN_TO[place_]:
                            break
                        act.wait_ge(*dense_done.at(L, d + 1))
                        b_ = ps[(BANK0 + d) % 4][:, :]
                        if gate:
                            g_ = TAKEN_BY["dve"][d + 1]
                            if g_ > 2:
                                act.wait_ge(*product.at(L, g_ - 2))
                            ins = fn(tmp[:, g_ % 2, :], b_, ACT.Sigmoid)
                        elif name == "out":
                            if i >= 3:
                                act.wait_ge(*added.at(L, i - 2))
                            elif i:
                                act.wait_ge(*product.at(L, 4 * KT))
                            fn(tmp[:, i % 2, :] if i else rstd[:, :], b_, ACT.Square).then_inc(*squared.up())
                            ins = fn(mix[:, i, :], b_, ACT.Copy)
                        else:
                            ins = to_sbuf[name](i)(b_)
                        ins.then_inc(*act_took.up())
                        if gate:
                            act.wait_ge(*dense_done.at(L, d + 2))
                        if CHUNK_OF[d] + 1 < MLP_CHUNK0:
                            hi_part(CHUNK_OF[d] + 2)
                        place[0] = d + 1 + gate

                def norm_hi(j):
                    for m in range(KT):
                        act.wait_ge(*h_raw.at(L, j * KT + m + 1))
                        fn(hn[0][:, m, :], tmp[:, m % 4, :], ACT.Copy).then_inc(*h_hi.up())

                def norm_rstd(j):
                    act.wait_ge(*sumsq.at(L, SUMMED[j]))
                    link(fn(rstd[:, :], ps[4][:, :], ACT.Ln, scale=1.0 / D, bias=C("eps", n=1)))
                    fn(rstd[:, :], rstd[:, :], ACT.Exp, scale=-0.5).then_inc(*rstd_done.up())

                def attention(which, pt):
                    base = 16 * which

                    def transposed(i):
                        b = i // H
                        act.wait_ge(*at_tr.at(L, base + i + 1))
                        fn(S(pt + i % 4 // 2, i % 2)[:, 0:(b + 1) * P], ps[6][:, 0:(b + 1) * P], ACT.Copy)\
                            .then_inc(*at_pt.up())
                        take(("bd"[which] + "_att", i, 1))
                    for i in range(16):
                        b, h = divmod(i, H)
                        n = (b + 1) * P
                        buf = S(6 + i % 4 // 2, i % 2)
                        act.wait_ge(*at_mx.at(L, base + i + 1))
                        fn(buf[:, 0:n], buf[:, 0:n], ACT.Exp, scale=-1.0, bias=col[:, 1, i % 4:i % 4 + 1],
                           accum_out=col[:, 2, i % 4:i % 4 + 1]).then_inc(*at_ex.up())
                        if i:
                            transposed(i - 1)
                        if i % H == 1 and i > 1:
                            attn_out(which, i // H - 1)
                    transposed(15)
                    attn_out(which, NT - 1)

                def attn_out(which, b):
                    act.wait_ge(*at_pv.at(L, which * NT + b + 1))
                    if b == 0 and which:
                        act.wait_ge(*dense_done.at(L, INDEX[("branch1", KT - 1)] + 1))
                    fn(y[0][:, 1, :, b * P:(b + 1) * P], ps[7][:, b % 2 * 256:b % 2 * 256 + 256].rearrange("p (t n) -> p t n", t=FT),
                       ACT.Copy).then_inc(*y_hi.up())

                for m in range(KT):
                    act.wait_ge(*x_tiles.at(L, m + 2))
                    if m >= 2:
                        act.wait_ge(*sumsq.at(L, m - 1))
                    fn(tmp[:, m % 2, :], x[:, m, :], ACT.Square).then_inc(*squared.up())
                act.wait_ge(*x_tiles.at(L, X0))
                act.dma_start(par[:, :], par_in[bass.ds(L, 1)].rearrange("a p n -> (a p) n")).then_inc(par_loaded.handle, 16)
                par_loaded.count += 16
                norm_rstd(0)
                norm_hi(0)

                act.wait_ge(*lb_in.at(L, 1))
                fn(col[:, 7, 0:4], col[:, 6, 0:4], ACT.Exp).then_inc(*lb_exp.up())
                take("A")
                act.wait_ge(*a_prep.at(L, 1))
                fn(S(2), S(2), ACT.Ln).then_inc(*a_ln.up())
                E = slab[:, 5, :]
                take(("a_level", 0))
                for lv in range(1, 8):
                    act.wait_ge(*a_diff.at(L, lv))
                    fn(E, E, ACT.Exp).then_inc(*a_exp.up())
                    take(("a_level", lv))
                act.wait_ge(*a_diff.at(L, 8))
                fn(slab[:, 6, :], slab[:, 2, :], ACT.Exp).then_inc(*a_exp.up())
                fn(slab[:, 5, :], slab[:, 5, :], ACT.Exp).then_inc(*a_exp.up())
                act.wait_ge(*a_ops.at(L, 9))
                act.dma_start(slab[:, 1:3, :].rearrange("p a n -> p (a n)"), rope_in).then_inc(rope_in_.handle, 16)
                rope_in_.count += 16
                kh_ = slab[:, 7, :].rearrange("p (c n) -> p c n", c=NT)
                for c in range(NT):
                    act.wait_ge(*a_tr.at(L, c + 1))
                    fn(kh_[:, c, :], ps[4][:, 0:256], ACT.Copy).then_inc(*a_tr_used.up())
                    take(("a_keys", c + 1))
                for c in range(NT):
                    act.wait_ge(*a_o.at(L, c + 1))
                    fn(S(18)[:, :, c * P:(c + 1) * P], ps[5][:, 0:256].rearrange("p (t n) -> p t n", t=FT), ACT.Copy)\
                        .then_inc(*a_o_used.up())
                    take(("a_chunk", c))
                act.wait_ge(*a_o_used.at(L, NT))
                for t in range(FT):
                    fn(S(19, t), S(18, t), ACT.Square).then_inc(*a_sq.up())
                take(("a_norm", 0))
                act.wait_ge(*a_var.at(L, 1))
                link(fn(slab[:, 0, :], slab[:, 0, :], ACT.Ln))
                fn(slab[:, 0, :], slab[:, 0, :], ACT.Exp, scale=-0.5).then_inc(*a_r.up())

                take("B")
                take(("b_rope", 0))
                act.wait_ge(*b_iwt.at(L, 1))
                fn(iw[:, :, :], ps[7][:, :].rearrange("p (t n) -> p t n", t=NT)[:, :, SM_IW:SM_IW + IH], ACT.Copy,
                   scale=1.0 / 16.0).then_inc(*b_iwc.up())
                for r in range(1, 7):
                    take(("b_rope", r))
                n_ix = 0
                for b in range(1, NT):
                    for j in range(IH):
                        n = (b + 1) * P
                        act.wait_ge(*b_ix.at(L, n_ix + 1))
                        if n_ix >= 2:
                            act.wait_ge(*b_acc.at(L, n_ix - 1))
                        fn(S(3, n_ix % 2)[:, 0:n], ps[4 + n_ix % 2][:, 0:n], ACT.Relu).then_inc(*b_relu.up())
                        n_ix += 1
                        take(("b_ix", n_ix - 1))
                take(("b_topk", TOPK // 8 - 1))
                attention(0, 0)

                take("C")
                act.wait_ge(*c_mix.at(L, 1))
                fn(S(15, 0)[0:32, :], S(15, 0)[0:32, :], ACT.Tanh)
                fn(S(15, 0)[64:128, :], S(15, 0)[64:128, :], ACT.Sigmoid).then_inc(*c_act.up())
                for i_ in range(4):
                    t = i_ % 2
                    act.wait_ge(*c_lw.at(L, i_ + 1))
                    if i_ < 2:
                        ins = fn(S(2, t), ps[4 + i_ % 4][:, :], ACT.Sigmoid, bias=pcol("w0", t))
                    else:
                        ins = fn(S(3, t), ps[4 + i_ % 4][:, :], ACT.Sigmoid, bias=pcol("a0", t))
                    ins.then_inc(*c_sg.up())
                take(("c_prep", 0))
                act.wait_ge(*c_vh.at(L, 1))
                fn(S(11, 0)[0:32, :], ps[6][0:32, :], ACT.Copy).then_inc(*c_vhc.up())
                take(("c_prep", 1))
                for t in range(FT):
                    act.wait_ge(*c_vg.at(L, t + 1))
                    fn(S(6, t), ps[4 + t][:, :], ACT.Sigmoid, bias=pcol("v0", t)).then_inc(*c_vgs.up())
                take(("c_prep", 2))
                act.wait_ge(*c_kkv.at(L, 1))
                link(fn(slab[:, 5, :], slab[:, 5, :], ACT.Ln))
                fn(slab[:, 5, :], slab[:, 5, :], ACT.Exp, scale=-0.5).then_inc(*c_kkr.up())
                act.wait_ge(*c_ex.at(L, 1))
                fn(slab[:, 6, :], slab[:, 1, :], ACT.Exp)
                fn(slab[:, 8, :], slab[:, 1, :], ACT.Exp, scale=-1.0)
                fn(slab[:, 7, :], slab[:, 2, :], ACT.Exp)
                fn(col[:, 3, :], col[:, 4, :], ACT.Exp).then_inc(*c_exd.up())
                take(("c_prep", 3))
                tmf = [slab[:, i, :] for i in (1, 2, 4)]
                for n_tr in range(6):
                    act.wait_ge(*c_tr.at(L, n_tr + 1))
                    fn(tmf[n_tr // 2][:, (n_tr % 2) * T:(n_tr % 2 + 1) * T], ps[4 + n_tr % 4][:, :], ACT.Copy)\
                        .then_inc(*c_tru.up())
                X_, XT_, R_ = c_halves[4:7]
                for c in range(NT):
                    take(("c_mask", c))
                    for k_ in range(11):
                        act.wait_ge(*c_xx.at(L, 11 * c + k_ + 1))
                        n = LEVELS[k_ // 2 + 1]
                        tgt, bk, side = (X_, 5, 0) if k_ % 2 == 0 and k_ < 10 else (XT_, 6, 1)
                        fn(halves(tgt, n, side), packed(ps[bk][:, 0:256], n), ACT.Copy).then_inc(*c_xxu.up())
                        if k_ % 2 or k_ == 10:
                            take(("c_level", c, k_ // 2 + 1, 1))
                    act.wait_ge(*c_b.at(L, c + 1))
                    rhs_ = R_[:, 0:256].rearrange("p (t two v) -> p t two v", two=2, v=HD)
                    fn(rhs_[:, :, 0, :], ps[7][:, 0:P].rearrange("p (t v) -> p t v", v=HD), ACT.Copy)
                    fn(rhs_[:, :, 1, :], ps[4][:, 0:P].rearrange("p (t v) -> p t v", v=HD), ACT.Copy).then_inc(*c_bu.up())
                    take(("c_out", c, 0))
                    act.wait_ge(*c_u.at(L, c + 1))
                    fn(R_[:, 256:512], ps[5][:, 0:256], ACT.Copy).then_inc(*c_uu.up())
                    take(("c_out", c, 1))
                    act.wait_ge(*c_y.at(L, c + 1))
                    fn(S(3)[:, :, c * P:(c + 1) * P], ps[6][:, 0:256].rearrange("p (t n) -> p t n", t=FT), ACT.Copy)\
                        .then_inc(*c_yu.up())
                    take(("c_out", c, 2))
                take(("c_norm", 0))
                act.wait_ge(*c_cen.at(L, 1))
                for t in range(FT):
                    fn(S(5, t), S(3, t), ACT.Square).then_inc(*c_csq.up())
                take(("c_norm", 1))
                act.wait_ge(*c_vv.at(L, 1))
                link(fn(slab[:, 5, :], slab[:, 5, :], ACT.Ln))
                fn(slab[:, 5, :], slab[:, 5, :], ACT.Exp, scale=-0.5).then_inc(*c_rr.up())

                take("D")
                act.wait_ge(*d_abs.at(L, 1))
                s5 = S(13, 0)[SM_F:SM_F + H, :]
                link(fn(s5, s5, ACT.Exp, scale=-1.0))
                fn(s5, s5, ACT.Ln, bias=C("ones", SM_F, SM_F + H, 1)).then_inc(*d_ln.up())
                take(("d_prep", 0))
                for h in range(H):
                    act.wait_ge(*d_bc.at(L, h + 1))
                    fn(S(14 + h // 2, h % 2), ps[4 + h][:, :], ACT.Copy).then_inc(*d_bcu.up())
                take(("d_prep", 1))
                attention(1, 8)

                take("rest")
                norm_rstd(1)
                hi_part(MLP_CHUNK0 + 1)
                for m in range(KT):
                    act.wait_ge(*x_tiles.at(L, X0 + m + 1))
                    if m >= 2:
                        act.wait_ge(*sumsq.at(L, SUMMED[1] + m - 1))
                    fn(tmp[:, m % 2, :], x[:, m, :], ACT.Square).then_inc(*squared.up())
                norm_rstd(2)
                norm_hi(1)
                def square(m):
                    act.wait_ge(*dve_took.at(L, DVE0 + 8 * 3 + m + 1))
                    if m >= 3:
                        act.wait_ge(*added.at(L, KT - 1 + m - 2))
                    fn(tmp[:, m % 2, :] if m else rstd[:, :], acc[:, m, :], ACT.Square).then_inc(*squared.up())

                def split_ahead(q, j, times):
                    c = MLP_CHUNK0 + j + 2
                    act.wait_ge(*dense_done.at(L, q * 16 + (MLP0 + j + 1)))
                    act.wait_ge(w_arrived[j % 2], L * (8 * CHUNKS) + q * 128 + 16 * (c // 2 + 1))
                    fn(wsp[0][:, j % 2, 0:CH], wsl[:, j % 2, 0:CH], ACT.Copy).then_inc(*w_hi_done.up(times))

                def relu_and_split(q, j, times):
                    if j < 8:
                        act.wait_ge(*dense_done.at(L, q * 16 + (MLP0 + j + 1)))
                        act.wait_ge(*u_ready.at(L, q * KT + j + 1))
                        fn(tmp[:, j % 4, :], ps[j % 4][:, :], ACT.Relu).then_inc(*act_took.up(times))
                    split_ahead(q, j, times)

                with act.Fori(0, QUARTERS - 1) as q:
                    for j in range(16):
                        relu_and_split(q, j, QUARTERS - 1)
                for j in range(14):
                    relu_and_split(QUARTERS - 1, j, 1)
                    if j >= 9:
                        square(j - 9)
                for m in range(5, KT):
                    square(m)
                norm_rstd(3)
                for j in (14, 15):
                    split_ahead(QUARTERS - 1, j, 1)

        @block.gpsimd
        def _(pool):
            pool.memset(v1st[:, :, :], 0.0).then_inc(cleared, 1)
            pool.wait_ge(once, ONCE)
            pool.sem_inc(w_split.handle, 2)
            for c in range(2):
                pool.wait_ge(w_arrived[c], 16)
                pool.tensor_copy(wsp[0][:, c, 0:CH], wsl[:, c, 0:CH]).then_inc(w_hi_done.handle, 1)
                pool.wait_ge(w_hi_done.handle, c + 1)
                pool.tensor_tensor(wsp[1][:, c, 0:CH], wsl[:, c, 0:CH], wsp[0][:, c, 0:CH].bitcast(f32), SUB)\
                    .then_inc(w_split.handle, 1)
            with pool.Fori(0, LAYERS) as L:
                def carry_wait():
                    pool.sem_inc(carrier, 1)

                def lo_part(c):
                    pool.wait_ge(*w_hi_done.at(L, c + 1))
                    size = CHM if c in LAST_OF_CHUNK and DENSE[LAST_OF_CHUNK[c]][0].startswith("branch") else CH
                    raw, (hi, lo) = wsl[:, c % 2, 0:size], (w[:, c % 2, 0:size] for w in wsp)
                    pool.tensor_tensor(lo, raw, hi.bitcast(f32), SUB).then_inc(*w_split.up())

                def add_square(j, m):
                    pool.wait_ge(*squared.at(L, j * KT + m + 1))
                    if m > 1:
                        pool.wait_ge(*added.at(L, j // 2 * (KT - 1) + m - 1))
                    pool.tensor_tensor(rstd[:, :], rstd[:, :], tmp[:, m % 2, :], ADD).then_inc(*added.up())

                def norm_lo(n_):
                    m = n_ % KT
                    pool.wait_ge(*h_hi.at(L, n_ + 1))
                    pool.tensor_tensor(hn[1][:, m, :], tmp[:, m % 4, :], hn[0][:, m, :].bitcast(f32), SUB).then_inc(*h_odd.up())

                first_out = CHUNK_OF[INDEX[("out", 0)]]
                for m in range(1, KT, 2):
                    norm_lo(m)
                for c in range(2, MLP_CHUNK0 + 2):
                    if c == MLP_CHUNK0 + 1:
                        add_square(1, KT - 1)
                    lo_part(c)
                    if first_out < c - 2 < MLP_CHUNK0 - 1:
                        add_square(1, c - 2 - first_out)
                    for d in range(MLP0):
                        if DENSE[d][0].startswith("branch") and CHUNK_OF[d] == c - 2:
                            i_ = TAKEN_BY["dve"][d] - 1
                            pool.wait_ge(*product.at(L, i_ + 1))
                            m = DENSE[d][1]
                            if DENSE[d][0] == "branch0":
                                carry_wait()
                                pool.tensor_copy(acc[:, m, :], tmp[:, 2 + i_ % 2, :]).then_inc(*merged.up())
                            else:
                                pool.tensor_tensor(acc[:, m, :], acc[:, m, :], tmp[:, 2 + i_ % 2, :], ADD)\
                                    .then_inc(*merged.up())
                pool.wait_ge(*m_split.at(L, KT))
                carry_wait()
                pool.memset(acc[:, :, :], 0.0).then_inc(*acc0.up())
                pool.wait_ge(*acc0.at(L, 1))
                for _ in range(4):
                    pool.sem_inc(*u_ready.up())
                for m in range(1, KT, 2):
                    norm_lo(KT + m)
                def lo_ahead(q, j, times):
                    pool.wait_ge(*w_hi_done.at(L, q * 16 + (MLP_CHUNK0 + j + 3)))
                    pool.tensor_tensor(wsp[1][:, j % 2, 0:CH], wsl[:, j % 2, 0:CH], wsp[0][:, j % 2, 0:CH].bitcast(f32), SUB)\
                        .then_inc(*w_split.up(times))

                with pool.Fori(0, QUARTERS - 1) as q:
                    for j in range(16):
                        lo_ahead(q, j, QUARTERS - 1)
                for j in range(14):
                    lo_ahead(QUARTERS - 1, j, 1)
                    if j >= 10:
                        add_square(3, j - 9)
                for m in range(5, KT):
                    add_square(3, m)
                for j in (14, 15):
                    lo_ahead(QUARTERS - 1, j, 1)

        @block.vector
        def _(dve):
            tt, ts, stt = dve.tensor_tensor, dve.tensor_scalar, dve.scalar_tensor_tensor

            def link(ins, sig=dve_step):
                ins.then_inc(*sig.up())
                dve.wait_ge(*sig.at(L, sig.count))

            dve.wait_ge(once, ONCE)
            dve.wait_ge(cleared, 1)
            dve.sem_inc(x_tiles.handle, 1)
            for i in range(4):
                dve.wait_ge(x_loaded[i], 16)
                dve.sem_inc(x_tiles.handle, 2)
            dve.wait_ge(masks_loaded, 16)
            NM = 2 * len(LEVELS) * P
            dve.tensor_copy(msk[:, :], slab[:, 0:2, :].rearrange("p a n -> p (a n)")[:, 0:NM]).then_inc(masks_ready, 1)
            dve.wait_ge(masks_ready, 1)
            with dve.Fori(0, LAYERS) as L:
                def carry_wait():
                    dve.sem_inc(carrier, 1)

                def norm_h(j, gain):
                    dve.wait_ge(*rstd_done.at(L, j + 1))
                    for m in range(KT):
                        n_ = j // 2 * KT + m
                        if m >= 4:
                            dve.wait_ge(*(h_odd if m % 2 else h_ready).at(L, (n_ - 4) // 2 + 1))
                        stt(tmp[:, m % 4, :], x[:, m, :], pcol(gain, m), rstd[:, :], MUL, MUL).then_inc(*h_raw.up())
                        if m % 2:
                            norm_lo(n_ - 1)

                def norm_lo(n_):
                    m = n_ % KT
                    dve.wait_ge(*h_hi.at(L, n_ + 1))
                    tt(hn[1][:, m, :], tmp[:, m % 4, :], hn[0][:, m, :].bitcast(f32), SUB).then_inc(*h_ready.up())

                def residual(j, src, gain):
                    dve.wait_ge(*rstd_done.at(L, j + 1))
                    base = dve_step.count

                    def add(m):
                        dve.wait_ge(*dve_step.at(L, base + m + 1))
                        tt(x[:, m, :], x[:, m, :], src[:, m, :], ADD).then_inc(*x_tiles.up())
                    for m in range(KT):
                        stt(src[:, m, :], src[:, m, :], pcol(gain, m), rstd[:, :], MUL, MUL).then_inc(*dve_step.up())
                        if m:
                            add(m - 1)
                    add(KT - 1)

                def split(src, hi, lo, sig):
                    link(dve.tensor_copy(hi, src))
                    tt(lo, src, hi.bitcast(f32), SUB).then_inc(*sig.up())

                place = [0]

                def gated(place_):
                    while place[0] < MLP0 and END[place[0]] <= GATED_TO[place_]:
                        d = place[0]
                        if DENSE[d][3] == "dve":
                            g_ = TAKEN_BY["dve"][d]
                            dve.wait_ge(*dense_done.at(L, d + 1))
                            dve.wait_ge(*act_took.at(L, TAKEN_BY["act"][d]))
                            if g_ > 2:
                                dve.wait_ge(*merged.at(L, g_ - 2))
                            tt(tmp[:, 2 + (g_ - 1) % 2, :], ps[(BANK0 + d) % 4][:, :], tmp[:, g_ % 2, :], MUL)\
                                .then_inc(*product.up())
                            if g_ > 3 * KT + 2:
                                split_merged(g_ - 3 * KT - 3)
                        place[0] += 1

                def split_merged(m):
                    dve.wait_ge(*merged.at(L, 3 * KT + m + 1))
                    split(acc[:, m, :], u[0][:, m, :], u[1][:, m, :], m_split)

                def blocks(ap, n):
                    return ap.rearrange("p (b two n) -> p b two n", two=2, n=n)

                dve.wait_ge(*par_loaded.at(L, 16))
                norm_h(0, "pre")

                lb0, lb1 = par[:, PC["lb0"]:PC["lb0"] + FT], par[:, PC["lb1"]:PC["lb1"] + FT]
                link(tt(col[:, 5, 0:2], lb1, lb0, ALU.max))
                tt(col[:, 6, 0:2], lb0, col[:, 5, 0:2], SUB)
                tt(col[:, 6, 2:4], lb1, col[:, 5, 0:2], SUB).then_inc(*lb_in.up())
                dve.wait_ge(*lb_exp.at(L, 1))
                link(tt(col[:, 5, 2:4], col[:, 7, 0:2], col[:, 7, 2:4], ADD))
                link(dve.reciprocal(col[:, 5, 4:6], col[:, 5, 2:4]))
                link(stt(lb[:, 0, :], col[:, 7, 2:4], pcol("flag"), col[:, 5, 4:6], MUL, MUL))
                link(ts(lb[:, 1, :], lb[:, 0, :], -1.0, 1.0, MUL, ADD))
                dve.wait_ge(*act_took.at(L, TAKEN_BY["act"][INDEX[("ag", 1)]]))
                for t in range(FT):
                    ins = ts(S(1, t), S(1, t), lb[:, 1, t:t + 1], None, MUL)
                ins.then_inc(*a_ops.up())
                for t in range(FT):
                    ins = ts(S(2, t), S(2, t), lb[:, 1, t:t + 1], lb[:, 0, t:t + 1], MUL, ADD)
                link(ins)
                ts(slab[:, 2, :], slab[:, 2, :], 2.0 ** -63, None, ALU.max).then_inc(*a_prep.up())
                tt(slab[:, 3, :], slab[:, 3, :], slab[:, 19, :], MUL)
                link(dve.memset(st[:, :, :], 0.0), a_st)
                dve.wait_ge(*a_ln.at(L, 1))
                for t in range(FT):
                    carry_wait()
                    link(dve.tensor_tensor_scan(S(2, t), con[:, CC["seg"]:CC["seg"] + T], S(2, t), 0.0, MUL, ADD))
                b_, E, q_, k_ = (slab[:, i, :] for i in (2, 5, 0, 1))
                AT = [slab[:, 16 + c // 2, (c % 2) * T:(c % 2 + 1) * T] for c in range(NT)]

                def exponents(n):
                    bb, ee = blocks(b_, n), blocks(E, n)
                    nb = FT * T // (2 * n)
                    beta = bb[:, :, 0, n - 1:n].to_broadcast([P, nb, n])
                    tt(ee[:, :, 0, :], beta, bb[:, :, 0, :], SUB)
                    tt(ee[:, :, 1, :], bb[:, :, 1, :], beta, SUB).then_inc(*a_diff.up())

                for lv in range(8):
                    if lv < 7:
                        n = LEVELS[lv]
                    for c in range(NT):
                        dve.wait_ge(*a_sc.at(L, lv * NT + c + 1))
                        if lv == 0:
                            tt(heads(AT[c]), heads(ps[4 + c][:, :]), over_heads(C("ident")), MUL).then_inc(*a_sc_used.up())
                        else:
                            carry_wait()
                            n_ = LEVELS[lv - 1]
                            dve.copy_predicated(halves(AT[c], n_, 1).rearrange("p (h b) n -> p h b n", h=H),
                                                level_half(0, lv - 1, n_, 1), packed(ps[4 + c][:, 0:256], n_)
                                                .rearrange("p (h b) n -> p h b n", h=H)).then_inc(*a_sc_used.up())
                    if lv < 7:
                        exponents(n)
                        dve.wait_ge(*a_exp.at(L, lv + 1))
                        ee = blocks(E, n)
                        tt(ee[:, :, 0, :], ee[:, :, 0, :], blocks(k_, n)[:, :, 0, :], MUL)
                        tt(ee[:, :, 1, :], ee[:, :, 1, :], blocks(q_, n)[:, :, 1, :], MUL).then_inc(*a_ops.up())
                bc = b_.rearrange("p (b n) -> p b n", n=P)
                tt(slab[:, 5, :].rearrange("p (b n) -> p b n", n=P), bc[:, :, P - 1:P].to_broadcast([P, FT * NT, P]), bc, SUB)\
                    .then_inc(*a_diff.up())
                dve.wait_ge(*a_exp.at(L, 9))
                link(dve.tensor_copy(col[:, 3, :], slab[:, 6, :].rearrange("p (b n) -> p b n", n=P)[:, :, P - 1]))
                tt(slab[:, 6, :], slab[:, 6, :], q_, MUL)
                tt(slab[:, 5, :], slab[:, 5, :], k_, MUL).then_inc(*a_ops.up())
                for c in range(NT):
                    dve.wait_ge(*a_su.at(L, c + 1))
                    for t in range(FT):
                        ins = stt(st[:, t, :], st[:, t, :], col[:, 3, t * NT + c:t * NT + c + 1],
                                  ps[6][:, t * HD:(t + 1) * HD], MUL, ADD)
                    link(ins, a_st)
                dve.wait_ge(*a_ss.at(L, 2))
                for t in range(FT):
                    ins = ts(S(0, t), ps[4 + t][:, :], 1.0 / HD, EPS, MUL, ADD)
                ins.then_inc(*a_var.up())
                dve.wait_ge(*a_r.at(L, 1))
                link(tt(slab[:, 18, :], slab[:, 18, :], slab[:, 0, :], MUL))
                link(stt(slab[:, 18, :], slab[:, 18, :], pcol("hgw"), slab[:, 3, :], MUL, MUL))
                split(S(18), y[0][:, 0, :, :], y[1][:, 0, :, :], y_ready)

                gated("B")
                dve.wait_ge(*act_took.at(L, TAKEN_BY["act"][INDEX[("bv", 1)]]))
                dve.wait_ge(*rope_in_.at(L, 16))
                r_ = 0
                for src, cs in ((S(8), 1), (S(9), 1), (S(11), 2)):
                    for t in range(FT):
                        dve.wait_ge(*b_rot.at(L, r_ + 1))
                        link(tt(S(0, 0), ps[4 + r_ % 2][:, :], S(cs, 1), MUL))
                        link(tt(src[:, t, :], src[:, t, :], S(cs, 0), MUL))
                        link(tt(src[:, t, :], src[:, t, :], S(0, 0), ADD), b_rope)
                        gated(("b_rope", r_))
                        r_ += 1
                dve.wait_ge(*b_rep.at(L, 1))
                dve.wait_ge(*b_rot.at(L, 7))
                tt(S(0, 0), ps[4][:, :], S(2, 1), MUL)
                link(tt(S(0, 1), ps[6][:, :], S(2, 0), MUL))
                link(tt(S(0, 1), S(0, 1), S(0, 0), ADD), b_rope)
                dve.wait_ge(*b_iwc.at(L, 1))

                def scores(b):
                    return S(4 + (b - 1) // 2, (b - 1) % 2)[:, 0:(b + 1) * P]

                n_ix = 0
                for b in range(1, NT):
                    n = (b + 1) * P
                    sc = scores(b)
                    for j in range(IH):
                        dve.wait_ge(*b_relu.at(L, n_ix + 1))
                        r9 = S(3, n_ix % 2)[:, 0:n]
                        if j == 0:
                            ins = ts(sc, r9, iw[:, b, j:j + 1], None, MUL)
                        else:
                            ins = stt(sc, r9, iw[:, b, j:j + 1], sc, MUL, ADD)
                        link(ins, b_acc)
                        n_ix += 1
                        gated(("b_ix", n_ix - 1))
                    link(tt(sc[:, b * P:n], sc[:, b * P:n], C("cneg"), ADD))
                for r in range(TOPK // 8):
                    for b in range(1, NT):
                        n = (b + 1) * P
                        sc = scores(b)
                        carry_wait()
                        ins = dve.max(col[:, b, :], sc)
                    link(ins)
                    carry_wait()
                    for b in range(1, NT):
                        n = (b + 1) * P
                        sc = scores(b)
                        ins = dve.match_replace(sc, col[:, b, :], sc, TAKEN)
                    link(ins)
                    gated(("b_topk", r))
                for b in range(1, NT):
                    n = (b + 1) * P
                    sc = scores(b)
                    ins = ts(sc, sc, -2e38, NEG, ALU.is_gt, MUL)
                link(ins)

                def softmax(which, bias):
                    base = 16 * which

                    def out_lo(b):
                        dve.wait_ge(*y_hi.at(L, which * NT + b + 1))
                        tb = slice(b * P, (b + 1) * P)
                        tt(y[1][:, 1, :, tb], ps[7][:, b % 2 * 256:b % 2 * 256 + 256].rearrange("p (t n) -> p t n", t=FT),
                           y[0][:, 1, :, tb].bitcast(f32), SUB).then_inc(*at_o.up())

                    def probs(i):
                        n = (i // H + 1) * P
                        buf = S(6 + i % 4 // 2, i % 2)[:, 0:n]
                        dve.wait_ge(*at_ex.at(L, base + i + 1))
                        link(dve.reciprocal(col[:, 6, i % 4:i % 4 + 1], col[:, 2, i % 4:i % 4 + 1]))
                        ts(buf, buf, col[:, 6, i % 4:i % 4 + 1], None, MUL).then_inc(*at_p.up())

                    for i in range(16):
                        b, h = divmod(i, H)
                        n = (b + 1) * P
                        buf = S(6 + i % 4 // 2, i % 2)[:, 0:n]
                        dve.wait_ge(*at_lg.at(L, base + i + 1))
                        if i >= 4:
                            dve.wait_ge(*at_tr.at(L, base + i - 3))
                        carry_wait()
                        dve.tensor_tensor_reduce(out=buf, in0=ps[4 + i % 2][:, 0:n], in1=bias(b, h, n), scale=-HD ** -0.5,
                                                 scalar=3e38, op0=ADD, op1=ALU.min, accum_out=col[:, 1, i % 4:i % 4 + 1])\
                            .then_inc(*at_mx.up())
                        if i:
                            probs(i - 1)
                            gated(("bd"[which] + "_att", i - 1, 1))
                        if i % H == 1 and i > 1:
                            out_lo(i // H - 1)
                    probs(15)
                    gated(("bd"[which] + "_att", 15, 1))
                    out_lo(NT - 1)

                softmax(0, lambda b, h, n: C("cneg") if b == 0 else scores(b))

                gated("C")
                dve.wait_ge(*act_took.at(L, TAKEN_BY["act"][INDEX[("cl", 0)]]))
                for i, (s_, n_) in ((3, (15, 1)), (1, (13, 2)), (2, (14, 2)), (0, (12, 2))):
                    src = S(s_)[:, 0:n_, :]
                    dd = S(0)[:, 0:n_, :]
                    tt(dd[:, :, 1:T], src[:, :, 0:T - 1], src[:, :, 1:T], SUB)
                    link(ts(dd[:, :, 0:1], src[:, :, 0:1], -1.0, None, MUL))
                    for t in range(n_):
                        ins = stt(src[:, t, :], dd[:, t, :], pcol("mu", 2 * i + t), src[:, t, :], MUL, ADD)
                    link(ins, c_mix if i in (3, 2) else dve_step)
                for t in range(FT):
                    ins = ts(S(4, t), S(13, t), pcol("kk", t), None, MUL)
                link(ins)
                for t in range(FT):
                    tt(S(5, t), S(4, t), S(4, t), MUL).then_inc(*c_sq.up())
                gated(("c_prep", 0))
                dve.wait_ge(*c_sg.at(L, 4))
                link(ts(slab[:, 2, :], slab[:, 2, :], -float(np.exp(-0.5)), None, MUL))
                for t in range(FT):
                    carry_wait()
                    link(dve.tensor_tensor_scan(S(1, t), con[:, CC["seg"]:CC["seg"] + T], S(2, t), 0.0, MUL, ADD))
                link(ts(slab[:, 0, :], slab[:, 3, :], -1.0, None, ADD))
                for t in range(FT):
                    ins = ts(S(0, t), S(0, t), pcol("ka", t), 1.0, MUL, ADD)
                link(ins)
                link(tt(slab[:, 13, :], slab[:, 13, :], slab[:, 0, :], MUL))
                for t in range(FT):
                    stt(S(0, t), S(12, t), pcol("rk", t), S(13, t), MUL, MUL).then_inc(*c_sq.up())
                gated(("c_prep", 1))
                dve.wait_ge(*c_vgs.at(L, 2))
                link(tt(slab[:, 7, :], v1st[:, :, :].rearrange("p t n -> p (t n)"), slab[:, 14, :], SUB))
                link(stt(slab[:, 7, :], slab[:, 6, :], pcol("flag"), slab[:, 7, :], MUL, MUL))
                link(tt(slab[:, 14, :], slab[:, 14, :], slab[:, 7, :], ADD))
                dve.tensor_copy(v1st[:, :, :].rearrange("p t n -> p (t n)"), slab[:, 14, :])
                dve.wait_ge(*c_ss.at(L, 2))
                for t in range(FT):
                    ins = ts(S(5, t), ps[6 + t][:, :], 1e-24, None, ALU.max)
                ins.then_inc(*c_kkv.up())
                cc = slab[:, 1, :].rearrange("p (b n) -> p b n", n=P)
                mid = col[:, 0, :]
                end = col[:, 1, :]
                mid4 = mid.rearrange("p (t c) -> p t c", t=FT)
                fac4 = col[:, 4, :].rearrange("p (t c) -> p t c", t=FT)
                dve.tensor_copy(mid, cc[:, :, P // 2 - 1])
                link(dve.tensor_copy(end, cc[:, :, P - 1]))
                link(tt(cc, cc, mid[:, :, None].to_broadcast([P, FT * NT, P]), SUB))
                tt(slab[:, 2, :], slab[:, 1, :], slab[:, 2, :], SUB)
                link(tt(col[:, 4, :], end, mid, SUB))
                link(tt(fac4[:, :, 0:NT - 1], fac4[:, :, 0:NT - 1], mid4[:, :, 1:NT], ADD), c_ex)
                gated(("c_prep", 2))
                dve.wait_ge(*c_ss.at(L, 4))
                for t in range(FT):
                    tt(S(0, t), ps[4 + t][:, :], S(14, t), MUL)
                dve.wait_ge(*c_kkr.at(L, 1))
                dve.wait_ge(*c_exd.at(L, 1))
                link(tt(slab[:, 4, :], slab[:, 4, :], slab[:, 5, :], MUL))
                link(tt(slab[:, 3, :], slab[:, 3, :], slab[:, 4, :], MUL))
                tt(slab[:, 6, :], slab[:, 6, :], slab[:, 12, :], MUL)
                stt(slab[:, 7, :], slab[:, 7, :], -1.0, slab[:, 4, :], MUL, MUL)
                link(tt(slab[:, 5, :], slab[:, 8, :], slab[:, 3, :], MUL))
                link(tt(slab[:, 8, :], slab[:, 8, :], slab[:, 13, :], MUL), c_til)
                link(dve.memset(st[:, :, :], 0.0), c_st)
                gated(("c_prep", 3))
                LTm, MTm, RBm, RKm, X_, XT_, R_, *PPs = c_halves
                dve.wait_ge(*c_tru.at(L, 6))
                link(dve.tensor_copy(heads(PPs[1]), over_heads(C("ident"))))
                for c in range(NT):
                    def by_parity(ap, par):
                        return ap.rearrange("p (t two n) -> p t two n", two=2, n=P)[:, :, par, :]

                    gated(("c_mask", c))
                    dve.wait_ge(*c_m.at(L, 6 * c + 1))
                    dve.tensor_copy(heads(X_), over_heads(C("ident")))
                    link(dve.tensor_copy(heads(XT_), over_heads(C("ident"))))
                    for i in range(6):
                        dve.wait_ge(*c_m.at(L, 6 * c + i + 1))
                        if i < 4:
                            pair = c_pairs[i // 2].rearrange("p (m t two n) -> p m t two n", m=2, two=2, n=P)
                            mask = C("slt" if i < 2 else "sle")[:, None, None, :].to_broadcast([P, 2, FT, P])
                            ins = tt(pair[:, :, :, i % 2, :], ps[4 + i][:, :].rearrange("p (m t n) -> p m t n", m=2, n=P),
                                     mask, MUL)
                        else:
                            carry_wait()
                            m0 = len(LEVELS) * P
                            ins = dve.copy_predicated(by_parity(X_, i % 2), msk[:, m0:m0 + P][:, None, :].to_broadcast([P, FT, P]),
                                                      ps[i][:, 0:256].rearrange("p (t n) -> p t n", n=P))
                        ins.then_inc(*c_mu.up())
                    dve.wait_ge(*c_mu.at(L, 6 * c + 2))
                    carry_wait()
                    dve.copy_predicated(heads(XT_), level(0, 0), heads(LTm)).then_inc(*c_x1.up())
                    for lv in range(1, 7):
                        dve.wait_ge(*c_pp.at(L, 6 * c + lv))
                        carry_wait()
                        n = LEVELS[lv]
                        dve.copy_predicated(halves(PPs[lv % 2], n, 0).rearrange("p (h b) n -> p h b n", h=H),
                                            level_half(1, lv, n, 0), packed(ps[4][:, 0:256], n)
                                            .rearrange("p (h b) n -> p h b n", h=H)).then_inc(*c_ppu.up())
                        link(dve.tensor_copy(heads(PPs[(lv + 1) % 2]), over_heads(C("ident"))))
                        gated(("c_level", c, lv, 1))
                    gated(("c_out", c, 1))
                    dve.wait_ge(*c_s.at(L, c + 1))
                    for t in range(FT):
                        ins = tt(st[:, t, :], st[:, t, :], ps[7][:, t * HD:(t + 1) * HD], ADD)
                    link(ins)
                    for t in range(FT):
                        ins = ts(st[:, t, :], st[:, t, :], col[:, 3, t * NT + c:t * NT + c + 1], None, MUL)
                    link(ins, c_st)
                    gated(("c_out", c, 2))
                dve.wait_ge(*c_mean.at(L, 2))
                for t in range(FT):
                    ins = stt(S(3, t), ps[4 + t][:, :], -1.0 / HD, S(3, t), MUL, ADD)
                link(ins, c_cen)
                dve.wait_ge(*c_var.at(L, 2))
                for t in range(FT):
                    ins = ts(S(5, t), ps[6 + t][:, :], 1.0 / HD, GN_EPS, MUL, ADD)
                ins.then_inc(*c_vv.up())
                dve.wait_ge(*c_rr.at(L, 1))
                link(tt(slab[:, 3, :], slab[:, 3, :], slab[:, 5, :], MUL))
                for t in range(FT):
                    ins = ts(S(3, t), S(3, t), pcol("lnw", t), pcol("lnb", t), MUL, ADD)
                link(ins)
                link(tt(slab[:, 3, :], slab[:, 3, :], slab[:, 0, :], ADD))
                dve.wait_ge(*c_g.at(L, 2))
                for t in range(FT):
                    ins = tt(S(3, t), ps[4 + t][:, :], S(3, t), MUL)
                link(ins)
                gated("D")
                dve.wait_ge(*dense_done.at(L, INDEX[("branch0", KT - 1)] + 1))
                split(S(3), y[0][:, 0, :, :], y[1][:, 0, :, :], y_ready)

                f_, t5, c5 = small[SM_F:SM_F + H, :], S(13, 0)[SM_F:SM_F + H, :], S(13, 1)[SM_F:SM_F + H, :]
                link(ts(f_, f_, pcol("foxb", 0, SM_F, SM_F + H), None, ADD))
                stt(t5, f_, -1.0, f_, MUL, ALU.max).then_inc(*d_abs.up())
                link(ts(f_, f_, 0.0, None, ALU.min))
                dve.wait_ge(*d_ln.at(L, 1))
                link(tt(t5, t5, f_, SUB))
                carry_wait()
                dve.tensor_tensor_scan(c5, C("ones", SM_F, SM_F + H, P)[:, 0:1].to_broadcast([H, T]), t5, 0.0, MUL, ADD)\
                    .then_inc(*d_c.up())
                gated(("d_prep", 1))
                dve.wait_ge(*d_bcu.at(L, H))
                softmax(1, lambda b, h, n: S(14 + h // 2, h % 2)[:, 0:n])

                gated("rest")
                split_merged(KT - 2)
                split_merged(KT - 1)
                residual(1, mix, "post")
                norm_h(2, "mpre")
                dve.wait_ge(*acc0.at(L, 1))
                carry_wait()
                with dve.Fori(0, QUARTERS) as q:
                    for m in range(KT):
                        r_ = tmp[:, m % 4, :]
                        dve.wait_ge(*act_took.at(L, q * KT + (ACT0 + m + 1)))
                        def chained(ins, sig=dve_step):
                            per_quarter = 8 * 2 if sig is dve_step else 8
                            base_ = sig.count
                            ins.then_inc(*sig.up())
                            dve.wait_ge(*sig.at(L, q * per_quarter + base_ + 1))
                        chained(tt(r_, r_, r_, MUL))
                        chained(dve.tensor_copy(u[0][:, m, :], r_))
                        tt(u[1][:, m, :], r_, u[0][:, m, :].bitcast(f32), SUB).then_inc(*u_ready.up(QUARTERS))
                    for m in range(KT):
                        dve.wait_ge(*dense_done.at(L, q * 16 + (MLP0 + 8 + m + 1)))
                        tt(acc[:, m, :], acc[:, m, :], ps[m % 4][:, :], ADD).then_inc(*dve_took.up(QUARTERS))
                dve_step.count += 3 * 16
                dve.wait_ge(*dve_took.at(L, DVE0 + 8 * QUARTERS))
                residual(3, acc, "mpost")

    return signals


def pack_weights(inputs):
    w_in, w_branch = np.asarray(inputs["w_in"]), np.asarray(inputs["w_branch"])
    w_out, w_up, w_down = (np.asarray(inputs[n]) for n in ("w_out", "w_up", "w_down"))

    def chunk(w):
        return w.reshape(-1, P, w.shape[1]).transpose(1, 0, 2).reshape(P, -1)
    proj, merge, rest = [], [], []
    for l in range(LAYERS):
        wl = w_in[l]
        small = np.zeros((D, P), np.float32)
        small[:, SM_IK:SM_IK + IDIM] = wl[:, B_IK:B_IK + IDIM]
        small[:, SM_F:SM_F + H] = wl[:, D_F:D_F + H]
        small[:, SM_IW:SM_IW + IH] = wl[:, B_IW:B_IW + IH]
        first = {"aq": A_Q, "af": A_F, "ai": A_I, "ag": A_G, "bq": B_Q, "bk": B_K, "bv": B_V, "biq": B_IQ, "cr": C_R,
                 "ck": C_K, "cv": C_V, "cl": C_L, "dq": D_Q, "dk": D_K, "dv": D_V}
        for name, _, n in PROJ_A + PROJ_B + PROJ_C + PROJ_D:
            proj += [chunk(small if name == "bs" else wl[:, first[name] + P * i:first[name] + P * (i + 1)]) for i in range(n)]
        for n in range(4):
            for i in range(KT):
                cs = slice(P * i, P * (i + 1))
                merge.append(np.concatenate([chunk(wl[:, GATE + n * D:][:, cs]), chunk(w_branch[l, n][:, cs])], axis=1))
        rest += [chunk(w_out[l][:, P * i:P * (i + 1)]) for i in range(KT)]
        for q in range(QUARTERS):
            rest += [chunk(w_up[l][:, D * q + P * i:D * q + P * (i + 1)]) for i in range(KT)]
            rest += [chunk(w_down[l][D * q:D * (q + 1), P * i:P * (i + 1)]) for i in range(KT)]
    return np.stack(proj), np.stack(merge), np.stack(rest)


def pack_params(inputs):
    par = np.zeros((LAYERS, P, PAR), np.float32)
    a = {k: np.asarray(v) for k, v in inputs.items()}
    for l in range(LAYERS):
        g = max(l - 1, 0)

        def put(name, v):
            v = v.reshape(-1, P).T
            par[l, :, PC[name]:PC[name] + v.shape[1]] = v
        for name, key in (("pre", "norm_mix_pre"), ("post", "norm_mix_post"), ("mpre", "norm_mlp_pre"),
                          ("mpost", "norm_mlp_post"), ("mu", "rwkv_mu"), ("w0", "rwkv_w0"), ("a0", "rwkv_a0"),
                          ("kk", "rwkv_k_k"), ("ka", "rwkv_k_a"), ("rk", "rwkv_r_k"), ("lnw", "rwkv_ln_w"),
                          ("lnb", "rwkv_ln_b")):
            put(name, a[key][l])
        put("v0", a["rwkv_v0"][g])
        put("hgw", np.concatenate([a["hgrn_norm_w"][l]] * 2))
        put("lb0", a["hgrn_lb_logits"][0])
        put("lb1", a["hgrn_lb_logits"][1])
        par[l, SM_F:SM_F + H, PC["foxb"]] = a["fox_f_bias"][l]
        par[l, :, PC["flag"]] = min(l, 1)
        par[l, 0:32, NPAR:NPAR + 256] = a["rwkv_w2"][l]
        par[l, 32:64, NPAR:NPAR + 256] = a["rwkv_a2"][l]
        par[l, 64:128, NPAR:NPAR + 256] = a["rwkv_g2"][l]
        par[l, :, NPAR + 256:NPAR + 320] = a["rwkv_v1"][g].reshape(FT, P, 32).transpose(1, 0, 2).reshape(P, 64)
        par[l, 0:32, NPAR + 320:] = a["rwkv_v2"][g]
    return par


def kernel(**inputs):
    import concourse.bacc as bacc
    from concourse.bass_utils import run_bass_kernel_spmd

    nc = bacc.Bacc("TRN2", target_bir_lowering=False, num_devices=1)
    proj, merge, rest = pack_weights(inputs)
    con, msk, rope = constants()
    x = np.asarray(inputs["x"])[0].T.reshape(KT, P, T).transpose(1, 0, 2).reshape(P, KT * T)
    arrays = {"x_in": x, "wproj": proj, "wmerge": merge, "wrest": rest, "params": pack_params(inputs),
              "tables": con, "masks": msk, "rope": rope}
    arrays = {k: np.ascontiguousarray(v) for k, v in arrays.items()}
    args = [nc.dram_tensor(k, v.shape, mybir.dt.from_np(v.dtype), kind="ExternalInput").ap() for k, v in arrays.items()]
    args.append(nc.dram_tensor("out", (P, KT * T), mybir.dt.float32, kind="ExternalOutput").ap())
    trunk_kernel(nc, *args)
    r = run_bass_kernel_spmd(nc, [arrays], core_ids=[0])
    got = r.results[0]["out"]
    return got.reshape(P, KT, T).transpose(1, 0, 2).reshape(D, T).T.reshape(1, T, D)
```
